# Optimizing a Trainium2 kernel written in Bass

```python
import math
import functools
import jax
import jax.numpy as jnp
from jax import lax
import numpy as np

D_MODEL = 1024
BATCH = 1
SEQ = 2048
DEPTH = 1
DEC_BATCH = 8
DEC_SEQ = 4
PAST_LEN = 16384
PAGE_SIZE = 128

ML_HEADS = 4
ML_DK = D_MODEL // 8
ML_DV = D_MODEL // 8
ML_WIDTH = ML_HEADS * ML_DV
ML_CHUNK = 64
GATE_SOFTCAP = 15.0
SWA_HEADS = 8
SWA_KV_HEADS = 2
SWA_HD = D_MODEL // 16
SWA_GROUP = SWA_HEADS // SWA_KV_HEADS
SWA_WIDTH = SWA_HEADS * SWA_HD
WINDOW = 128
REL_BUCKETS = 32
REL_MAX_DIST = 128
MIX_WIDTH = ML_WIDTH + SWA_WIDTH
D_FF = -(-8 * D_MODEL // (3 * 256)) * 256
ALPHA = (2.0 * DEPTH) ** 0.25
BETA = (8.0 * DEPTH) ** -0.25
LN_EPS = 1e-5
NORM_EPS = 1e-6
NEG_INF = -1e30
IN_SIZES = (ML_HEADS * ML_DK, ML_HEADS * ML_DK, ML_WIDTH, ML_WIDTH, ML_HEADS, ML_HEADS,
            SWA_WIDTH, SWA_KV_HEADS * SWA_HD, SWA_KV_HEADS * SWA_HD)
VALUE_COL_GROUPS = (2, 8)
IN_COLS = sum(IN_SIZES)

kernel_name = "hymba_mlstm_swa_sink_step"

def layer_norm(x, g, b):
    xf = x.astype(jnp.float32)
    mu = jnp.mean(xf, -1, keepdims=True)
    var = jnp.mean(jnp.square(xf - mu), -1, keepdims=True)
    return ((xf - mu) * lax.rsqrt(var + LN_EPS) * g + b).astype(x.dtype)

def softcap(a):
    return GATE_SOFTCAP * jnp.tanh(a / GATE_SOFTCAP)

def split_in_proj(proj):
    offs = np.cumsum(IN_SIZES)[:-1].tolist()
    return jnp.split(proj, offs, axis=-1)

def t5_bucket(dist):
    n = jnp.maximum(dist, 0)
    max_exact = REL_BUCKETS // 2
    nf = jnp.maximum(n, 1).astype(jnp.float32)
    large = max_exact + (jnp.log(nf / max_exact) / math.log(REL_MAX_DIST / max_exact)
                         * (REL_BUCKETS - max_exact)).astype(jnp.int32)
    large = jnp.minimum(large, REL_BUCKETS - 1)
    return jnp.where(n < max_exact, n, large)

def rel_pos_bias(dist, rel_bias):
    bias = rel_bias.astype(jnp.float32)[t5_bucket(dist)]
    return jnp.moveaxis(bias, -1, 0).reshape(SWA_KV_HEADS, SWA_GROUP, *dist.shape)

def sink_softmax(s, valid, sinks):
    snk = sinks.astype(jnp.float32).reshape(SWA_KV_HEADS, SWA_GROUP, 1, 1)
    s = jnp.where(valid, s, NEG_INF)
    mx = jnp.maximum(jnp.max(s, -1, keepdims=True), snk)
    p = jnp.exp(s - mx)
    return p / (jnp.sum(p, -1, keepdims=True) + jnp.exp(snk - mx))

def swa_prompt(q, k, v, sinks, rel_bias):
    B, S = q.shape[:2]
    nb = S // WINDOW
    f32 = jnp.float32
    qb = q.reshape(B, nb, WINDOW, SWA_KV_HEADS, SWA_GROUP, SWA_HD).astype(f32)

    def band(a):
        a = a.reshape(B, nb, WINDOW, SWA_KV_HEADS, SWA_HD).astype(f32)
        prev = jnp.concatenate([jnp.zeros_like(a[:, :1]), a[:, :-1]], axis=1)
        return jnp.concatenate([prev, a], axis=2)

    kk, vv = band(k), band(v)
    qi = jnp.arange(WINDOW)[:, None]
    kj = jnp.arange(2 * WINDOW)[None, :]
    dist = WINDOW + qi - kj
    kpos = jnp.arange(nb)[:, None] * WINDOW - WINDOW + jnp.arange(2 * WINDOW)[None, :]
    valid = ((dist >= 0) & (dist < WINDOW))[None] & (kpos >= 0)[:, None, :]
    s = jnp.einsum('bnqhgd,bnkhd->bnhgqk', qb, kk) * (SWA_HD ** -0.5) + rel_pos_bias(dist, rel_bias)
    p = sink_softmax(s, valid[None, :, None, None], sinks)
    o = jnp.einsum('bnhgqk,bnkhd->bnqhgd', p, vv).reshape(B, S, SWA_WIDTH).astype(q.dtype)
    wb = min(WINDOW, S)
    return o, k[:, S - wb:], v[:, S - wb:]

def swa_sample(q, k, v, sinks, rel_bias, kbuf, vbuf):
    B, T = q.shape[:2]
    wb = kbuf.shape[1]
    f32 = jnp.float32
    kk = jnp.concatenate([kbuf.astype(k.dtype), k], axis=1)
    vv = jnp.concatenate([vbuf.astype(v.dtype), v], axis=1)
    qpos = PAST_LEN + jnp.arange(T)
    kpos = PAST_LEN - wb + jnp.arange(wb + T)
    dist = qpos[:, None] - kpos[None, :]
    valid = (dist >= 0) & (dist < WINDOW)
    qh = q.reshape(B, T, SWA_KV_HEADS, SWA_GROUP, SWA_HD).astype(f32)
    s = jnp.einsum('bqhgd,bkhd->bhgqk', qh, kk.astype(f32)) * (SWA_HD ** -0.5) + rel_pos_bias(dist, rel_bias)
    p = sink_softmax(s, valid, sinks)
    o = jnp.einsum('bhgqk,bkhd->bqhgd', p, vv.astype(f32)).reshape(B, T, SWA_WIDTH).astype(q.dtype)
    return o, kk[:, T:], vv[:, T:]

def mlstm_chunkwise(q, k, v, i_pre, f_pre, C0, n0, m0):
    B, NH, L, _ = q.shape
    lc = ML_CHUNK if L % ML_CHUNK == 0 else L
    nc = L // lc

    def to_chunks(a):
        return jnp.moveaxis(a.reshape(B, NH, nc, lc, *a.shape[3:]), 2, 0)

    logf = jax.nn.log_sigmoid(f_pre)
    xs = (to_chunks(q), to_chunks(k), to_chunks(v), to_chunks(i_pre), to_chunks(logf))
    causal = jnp.tril(jnp.ones((lc, lc), bool))

    def step(carry, xc):
        C, n, m = carry
        qc, kc, vc, ic, fc = xc
        b = jnp.cumsum(fc, axis=-1)
        logD = jnp.where(causal, b[..., :, None] - b[..., None, :] + ic[..., None, :], -jnp.inf)
        inter = b + m[..., None]
        m_row = jnp.maximum(inter, jnp.max(logD, -1))
        sc = jnp.exp(inter - m_row)
        qk = jnp.einsum('bhtd,bhsd->bhts', qc, kc) * jnp.exp(logD - m_row[..., None])
        num = sc[..., None] * jnp.einsum('bhtd,bhde->bhte', qc, C) + jnp.einsum('bhts,bhse->bhte', qk, vc)
        den = sc * jnp.einsum('bhtd,bhd->bht', qc, n) + jnp.sum(qk, -1)
        h = num / jnp.maximum(jnp.abs(den), jnp.exp(-m_row))[..., None]
        bL = b[..., -1]
        w = bL[..., None] - b + ic
        m_new = jnp.maximum(bL + m, jnp.max(w, -1))
        a = jnp.exp(bL + m - m_new)
        kw = kc * jnp.exp(w - m_new[..., None])[..., None]
        C_new = a[..., None, None] * C + jnp.einsum('bhsd,bhse->bhde', kw, vc)
        n_new = a[..., None] * n + jnp.sum(kw, axis=2)
        return (C_new, n_new, m_new), h

    (C, n, m), hs = lax.scan(step, (C0, n0, m0), xs)
    h = jnp.moveaxis(hs, 0, 2).reshape(B, NH, L, -1)
    return h, C, n, m

def token_mixers(x, ml_state, swa_fn, w_in, b_ig, b_fg, ml_g, sinks, rel_bias):
    B, L, _ = x.shape
    f32 = jnp.float32
    mq, mk, mv, mo, mi, mf, sq, sk, sv = split_in_proj(x @ w_in)

    def heads(a):
        return a.reshape(B, L, ML_HEADS, -1).transpose(0, 2, 1, 3).astype(f32)

    q, k, v = heads(mq), heads(mk) * (ML_DK ** -0.5), heads(mv)
    i_pre = softcap(mi.astype(f32) + b_ig).transpose(0, 2, 1)
    f_pre = softcap(mf.astype(f32) + b_fg).transpose(0, 2, 1)
    h, C, n, m = mlstm_chunkwise(q, k, v, i_pre, f_pre, *ml_state)
    h = h.transpose(0, 2, 1, 3)
    h = h * lax.rsqrt(jnp.mean(h * h, -1, keepdims=True) + NORM_EPS)
    h_ml = (h.reshape(B, L, ML_WIDTH) * ml_g * jax.nn.sigmoid(mo.astype(f32))).astype(x.dtype)
    h_swa, kb, vb = swa_fn(sq.reshape(B, L, SWA_HEADS, SWA_HD),
                           sk.reshape(B, L, SWA_KV_HEADS, SWA_HD),
                           sv.reshape(B, L, SWA_KV_HEADS, SWA_HD), sinks, rel_bias)
    return jnp.concatenate([h_ml, h_swa], axis=-1), (C, n, m, kb, vb)

def decoder_layer(x, ml_state, swa_fn, w_in, b_ig, b_fg, ml_g, sinks, rel_bias,
                  w_out, ln1_g, ln1_b, w_ffn_in, w_ffn_out, ln2_g, ln2_b):
    mix, state = token_mixers(x, ml_state, swa_fn, w_in, b_ig, b_fg, ml_g, sinks, rel_bias)
    x = layer_norm(ALPHA * x + mix @ w_out, ln1_g, ln1_b)
    gate, up = jnp.split(x @ w_ffn_in, 2, axis=-1)
    x = layer_norm(ALPHA * x + (jax.nn.silu(gate) * up) @ w_ffn_out, ln2_g, ln2_b)
    return x, state

def setup_inputs(seed: int = 0) -> dict:
    key = jax.random.key(seed)
    ks = jax.random.split(key, 20)
    f32 = jnp.float32

    def nrm(k, shape, s):
        return jax.random.normal(k, shape, f32) * s

    wb = min(WINDOW, PAST_LEN)
    col_scale = jnp.concatenate([jnp.full((n,), BETA if i in VALUE_COL_GROUPS else 1.0, f32)
                                 for i, n in enumerate(IN_SIZES)])
    return {
        "x_prompt": nrm(ks[0], (BATCH, SEQ, D_MODEL), 1.0),
        "x_sample": nrm(ks[1], (DEC_BATCH, DEC_SEQ, D_MODEL), 1.0),
        "state_mlstm_C": nrm(ks[2], (DEPTH, DEC_BATCH, ML_HEADS, ML_DK, ML_DV), 0.05),
        "state_mlstm_n": nrm(ks[3], (DEPTH, DEC_BATCH, ML_HEADS, ML_DK), 0.1),
        "state_mlstm_m": nrm(ks[4], (DEPTH, DEC_BATCH, ML_HEADS), 1.0),
        "cache_swa_k": nrm(ks[5], (DEPTH, DEC_BATCH, wb, SWA_KV_HEADS, SWA_HD), 1.0),
        "cache_swa_v": nrm(ks[6], (DEPTH, DEC_BATCH, wb, SWA_KV_HEADS, SWA_HD), BETA),
        "w_in": nrm(ks[7], (DEPTH, D_MODEL, IN_COLS), D_MODEL ** -0.5) * col_scale,
        "b_igate": nrm(ks[8], (DEPTH, ML_HEADS), 0.1),
        "b_fgate": jnp.linspace(3.0, 6.0, ML_HEADS, dtype=f32)[None] + nrm(ks[9], (DEPTH, ML_HEADS), 0.1),
        "ml_norm_g": 1.0 + nrm(ks[10], (DEPTH, ML_WIDTH), 0.02),
        "swa_sinks": nrm(ks[11], (DEPTH, SWA_HEADS), 0.5),
        "rel_bias": nrm(ks[12], (REL_BUCKETS, SWA_HEADS), 0.1),
        "w_out": nrm(ks[13], (DEPTH, MIX_WIDTH, D_MODEL), BETA * MIX_WIDTH ** -0.5),
        "ln1_g": 1.0 + nrm(ks[14], (DEPTH, D_MODEL), 0.02),
        "ln1_b": nrm(ks[15], (DEPTH, D_MODEL), 0.02),
        "w_ffn_in": nrm(ks[16], (DEPTH, D_MODEL, 2 * D_FF), BETA * D_MODEL ** -0.5),
        "w_ffn_out": nrm(ks[17], (DEPTH, D_FF, D_MODEL), BETA * D_FF ** -0.5),
        "ln2_g": 1.0 + nrm(ks[18], (DEPTH, D_MODEL), 0.02),
        "ln2_b": nrm(ks[19], (DEPTH, D_MODEL), 0.02),
    }

def reference(x_prompt, x_sample, state_mlstm_C, state_mlstm_n, state_mlstm_m, cache_swa_k, cache_swa_v,
              w_in, b_igate, b_fgate, ml_norm_g, swa_sinks, rel_bias, w_out, ln1_g, ln1_b,
              w_ffn_in, w_ffn_out, ln2_g, ln2_b):
    f32 = jnp.float32
    bp = x_prompt.shape[0]
    yp, ys = x_prompt, x_sample
    new_p = ([], [], [], [], [])
    new_s = ([], [], [], [], [])
    for l in range(DEPTH):
        lw = (w_in[l], b_igate[l], b_fgate[l], ml_norm_g[l], swa_sinks[l], rel_bias,
              w_out[l], ln1_g[l], ln1_b[l], w_ffn_in[l], w_ffn_out[l], ln2_g[l], ln2_b[l])
        zero_state = (jnp.zeros((bp, ML_HEADS, ML_DK, ML_DV), f32),
                      jnp.zeros((bp, ML_HEADS, ML_DK), f32),
                      jnp.zeros((bp, ML_HEADS), f32))
        yp, st_p = decoder_layer(yp, zero_state, swa_prompt, *lw)
        past_state = (state_mlstm_C[l].astype(f32), state_mlstm_n[l].astype(f32), state_mlstm_m[l].astype(f32))
        swa_fn = functools.partial(swa_sample, kbuf=cache_swa_k[l], vbuf=cache_swa_v[l])
        ys, st_s = decoder_layer(ys, past_state, swa_fn, *lw)
        for lst, a in zip(new_p, st_p):
            lst.append(a)
        for lst, a in zip(new_s, st_s):
            lst.append(a)
    dts = (state_mlstm_C.dtype, state_mlstm_n.dtype, state_mlstm_m.dtype, cache_swa_k.dtype, cache_swa_v.dtype)
    p_C, p_n, p_m, p_k, p_v = [jnp.stack(lst).astype(dt) for lst, dt in zip(new_p, dts)]
    s_C, s_n, s_m, s_k, s_v = [jnp.stack(lst).astype(dt) for lst, dt in zip(new_s, dts)]
    return (yp, ys, p_C, p_n, p_m, p_k, p_v, s_C, s_n, s_m, s_k, s_v)


_drawn_inputs = setup_inputs


def setup_inputs(seed=0):
    import zlib

    import numpy as np

    out = dict(_drawn_inputs(seed))
    spreads = {}
    factors = {'ml_norm_g': 24.666,
     'swa_sinks': 200.0,
     'rel_bias': 110.453,
     'ln1_g': 7.837,
     'ln1_b': 7.769,
     'ln2_g': 24.083,
     'ln2_b': 23.638}
    for name, (base, spread) in spreads.items():
        noise = np.random.default_rng([zlib.crc32(name.encode()), seed]).standard_normal(out[name].shape)
        drawn = base * np.exp(spread * noise) if base else spread * noise
        out[name] = jnp.asarray(drawn.astype(out[name].dtype))
    for name, factor in factors.items():
        out[name] = (out[name] * factor).astype(out[name].dtype)
    return out
```

```python
from contextlib import ExitStack

import numpy as np

import concourse.bass as bass
from concourse import mybir

F32 = mybir.dt.float32
F32R = mybir.dt.float32r
ALU = mybir.AluOpType
ACT = mybir.ActivationFunctionType
AX = mybir.AxisListType

P = 128
D = 1024
KD = D // P
SEQ = 2048
DB, DT = 8, 4
NS = DB * DT
NT = SEQ + NS
NG = 5
TG = NT // NG
TOK = 104
NTT = TG // TOK
H = 4
C = 128
NC = SEQ // C
J = 4
W = 128
PAST = 128
FF = 2816
KF = FF // P
HALF = KF // 2
NPROJ = 22
MQ, MK, MV, MO, SQ, SK, SV = 0, 4, 8, 12, 16, 20, 21
QD, KD_SWA = H * P, 64
ML_SCALE = float(P) ** -0.5
SWA_SCALE = 64.0 ** -0.5
ALPHA = 2.0 ** 0.25
LN_EPS = 1e-5
NORM_EPS = 1e-6
CAP = 15.0
NEG = -1e30
HJ = 384
assert NG * TG == NT and NTT * TOK == TG



class Steps:

    def __init__(self, eng, sem, turn=0, each=0):
        self.eng, self.sem, self.turn, self.each, self.k = eng, sem, turn, each, 0

    def __call__(self, ins):
        self.k += 1
        ins.then_inc(self.sem, 1)
        self.eng.wait_ge(self.sem, self.turn * self.each + self.k)

    def end(self):
        assert self.k == self.each, (self.sem, self.k)


class Store:

    def __init__(self, nc, ctx):
        self.nc, self.ctx = nc, ctx

    def sb(self, name, shape, dt=F32):
        return self.ctx.enter_context(self.nc.sbuf_tensor(name, shape, dt))

    def ps(self, name, shape):
        return self.ctx.enter_context(self.nc.psum_tensor(name, shape, F32))

    def sem(self, name):
        return self.nc.alloc_semaphore(name)


def project(nc, io):
    with ExitStack() as ctx:
        m = Store(nc, ctx)
        xh = m.sb("xh", [P, KD, NT], F32R)
        xl = m.sb("xl", [P, KD, NT], F32R)
        xraw = m.sb("xraw", [P, KD, TG])
        raw = m.sb("raw", [P, 2, KD, P])
        whi = m.sb("whi", [P, 2, KD, P], F32R)
        wlo = m.sb("wlo", [P, 2, KD, P], F32R)
        ghi = m.sb("ghi", [P, KD, P], F32R)
        glo = m.sb("glo", [P, KD, P], F32R)
        out = m.sb("out", [P, 2, NT])
        grow = m.sb("grow", [8, NT])
        acc = [m.ps(f"acc{i}", [P, 512]) for i in range(2)]
        x_in = m.sem("p_x_in")
        x_hi = m.sem("p_x_hi")
        x_split = m.sem("p_x_split")
        g_zero = m.sem("p_g_zero")
        g_in = m.sem("p_g_in")
        g_hi = m.sem("p_g_hi")
        g_split = m.sem("p_g_split")
        raw_in = [m.sem(f"p_raw_in{s}") for s in range(2)]
        hi_done = [m.sem(f"p_hi{s}") for s in range(2)]
        lo_done = [m.sem(f"p_lo{s}") for s in range(2)]
        acc_full = m.sem("p_acc_full")
        acc_free = m.sem("p_acc_free")
        out_free = [m.sem(f"p_out_free{s}") for s in range(2)]
        g_stored = m.sem("p_g_stored")
        ITER = NPROJ // 2
        block = ctx.enter_context(nc.Block())

        @block.sync
        def _(sp):
            def load(i, s):
                sp.dma_start(raw[:, s], io["wA"][bass.ds(i * 2 + s, 1)].rearrange("a p k n -> (a p) k n")).then_inc(raw_in[s], 16)

            def store(i, s):
                sp.wait_ge(acc_free, (i * 2 + s + 2) * NG)
                sp.wait_ge(g_in, 16)
                sp.dma_start(io["projT"][bass.ds(i * 2 + s, 1)].rearrange("a p n -> (a p) n"),
                             out[:, s]).then_inc(out_free[s], 16)

            sp.wait_ge(g_zero, 1)
            sp.dma_start(raw[:, 0, :, 0:8], io["wG"]).then_inc(g_in, 16)
            sp.dma_start(xraw[:], io["xT"][0]).then_inc(x_in, 16)
            sp.wait_ge(g_split, 1)
            for s in range(2):
                load(0, s)
            with sp.Fori(1, NG) as g:
                sp.wait_ge(x_split, g)
                sp.wait_ge(g_in, 16)
                sp.dma_start(xraw[:], io["xT"][bass.ds(g, 1)].rearrange("a p k n -> (a p) k n")).then_inc(x_in, 16)
            with sp.Fori(1, ITER) as i:
                for s in range(2):
                    sp.wait_ge(lo_done[s], i)
                    sp.wait_ge(g_in, 16)
                    load(i, s)
                for s in range(2):
                    store(i - 1, s)
            for s in range(2):
                store(ITER - 1, s)
            sp.wait_ge(acc_free, NG)
            sp.dma_start(io["gateT"], grow[:]).then_inc(g_stored, 16)
            sp.wait_ge(g_stored, 16)
            for s in range(2):
                sp.wait_ge(out_free[s], 16 * (ITER + 1))

        @block.scalar
        def _(act):
            act.wait_ge(g_in, 16)
            nc.scalar.activation(ghi[:], raw[:, 0], ACT.Copy).then_inc(g_hi, 1)
            with act.Fori(0, NG) as g:
                act.wait_ge(x_in, g * 16 + 16)
                act.wait_ge(g_in, 16)
                nc.scalar.activation(xh[:, :, bass.ds(g * TG, TG)], xraw[:], ACT.Copy).then_inc(x_hi, 1)
            for s in range(2):
                act.wait_ge(raw_in[s], 16)
                nc.scalar.activation(whi[:, s], raw[:, s], ACT.Copy).then_inc(hi_done[s], 1)
            with act.Fori(1, ITER) as i:
                for s in range(2):
                    act.wait_ge(raw_in[s], i * 16 + 16)
                    act.wait_ge(acc_full, (i * 2 + s) * NG)
                    act.wait_ge(g_in, 16)
                    nc.scalar.activation(whi[:, s], raw[:, s], ACT.Copy).then_inc(hi_done[s], 1)

        @block.gpsimd
        def _(pool):
            nc.gpsimd.memset(raw[:, 0], 0.0).then_inc(g_zero, 1)
            pool.wait_ge(g_hi, 1)
            nc.gpsimd.tensor_tensor(glo[:], raw[:, 0], ghi[:].bitcast(F32), ALU.subtract).then_inc(g_split, 1)
            with pool.Fori(0, ITER) as i:
                for s in range(2):
                    pool.wait_ge(hi_done[s], i + 1)
                    nc.gpsimd.tensor_tensor(wlo[:, s], raw[:, s], whi[:, s].bitcast(F32),
                                            ALU.subtract).then_inc(lo_done[s], 1)

        @block.tensor
        def _(pe):
            def product(bank, hi, lo, g):
                for k in range(KD):
                    xs = slice(g * TG, (g + 1) * TG)
                    pe.matmul(acc[bank][:, 0:TG], hi[:, k], xh[:, k, xs], start=(k == 0), stop=False)
                    pe.matmul(acc[bank][:, 0:TG], hi[:, k], xl[:, k, xs], start=False, stop=False)
                    last = pe.matmul(acc[bank][:, 0:TG], lo[:, k], xh[:, k, xs], start=False, stop=(k == KD - 1))
                return last

            pe.wait_ge(g_split, 1)
            for g in range(NG):
                pe.wait_ge(x_split, g + 1)
                if g >= 2:
                    pe.wait_ge(acc_free, g - 1)
                product(g % 2, ghi, glo, g).then_inc(acc_full, 1)
            with pe.Fori(0, ITER) as i:
                for s in range(2):
                    pe.wait_ge(lo_done[s], i + 1)
                    for g in range(NG):
                        n = s * NG + g
                        pe.wait_ge(acc_free, i * (2 * NG) + NG + n - 1)
                        product((n + NG) % 2, whi[:, s], wlo[:, s], g).then_inc(acc_full, 1)

        @block.vector
        def _(dve):
            for s in range(2):
                dve.sem_inc(out_free[s], 16)
            with dve.Fori(0, NG) as g:
                dve.wait_ge(x_hi, g + 1)
                xs = bass.ds(g * TG, TG)
                nc.vector.tensor_tensor(xl[:, :, xs], xraw[:], xh[:, :, xs].bitcast(F32),
                                        ALU.subtract).then_inc(x_split, 1)
            for g in range(NG):
                dve.wait_ge(acc_full, g + 1)
                nc.vector.tensor_copy(grow[:, g * TG:(g + 1) * TG], acc[g % 2][0:8, 0:TG]).then_inc(acc_free, 1)
            with dve.Fori(0, ITER) as i:
                for s in range(2):
                    dve.wait_ge(out_free[s], i * 16 + 16)
                    for g in range(NG):
                        n = s * NG + g
                        dve.wait_ge(acc_full, i * (2 * NG) + NG + n + 1)
                        nc.vector.tensor_copy(out[:, s, g * TG:(g + 1) * TG],
                                                     acc[(n + NG) % 2][:, 0:TG]).then_inc(acc_free, 1)


def gates(nc, io, keep):
    cols, bias, bias_prev, ident = keep["cols"], keep["bias"], keep["bias_prev"], keep["ident"]
    with ExitStack() as ctx:
        m = Store(nc, ctx)
        gi = m.sb("gi", [H, NT])
        gf = m.sb("gf", [H, NT])
        b = m.sb("b", [H, NT])
        run = m.sb("run", [H, NT])
        xs = m.sb("xs", [H, 2, NT])
        ue = m.sb("ue", [64, NT])
        start = m.sb("start", [H, SEQ])
        small = m.sb("small", [H, 32])
        m0 = m.sb("m0_sb", [H, DB])
        m_last = m.sb("m_last", [H, DB])
        mprev = m.sb("mprev", [H, NC])
        relb = m.sb("relb", [32, 8])
        onehot = m.sb("onehot", [32, HJ])
        outside = m.sb("outside", [8, HJ])
        ext = m.sb("ext_sb", [8, HJ])
        anti = m.sb("anti", [P, P])
        hank = m.sb("hank", [P, 8, 2 * W])
        srow = m.sb("srow", [32, 132])
        repl = m.sb("repl", [32, P])
        srow_all = m.sb("srow_all", [P, 132])
        smask = m.sb("smask", [P, 2, NS])
        ps = m.ps("ps", [P, 4, 512])
        pt = m.ps("pt", [P, 3, 512])
        loaded = m.sem("g_loaded")
        dve_s, act_s, pe_s, pool_s = m.sem("g_dve"), m.sem("g_act"), m.sem("g_pe"), m.sem("g_pool")
        stored = m.sem("g_stored")
        ext_out = m.sem("g_ext_out")
        ext_in = m.sem("g_ext_in")
        block = ctx.enter_context(nc.Block())
        EXT, CAPPED_BIAS, ONE_MORE, MAXIMA, EXPONENTS, U, TURNED = 2, 4, 5, 21, 26, 27, 30
        SIGMOIDS, LOGS, EXP_M, SCALES = 3, 4, 5, 7

        @block.sync
        def _(sp):
            for dst, src in ((relb[:], io["rel_bias"]), (onehot[:], io["c_onehot"]), (outside[:], io["c_outside"]),
                             (gi[:], io["gateT"][0:H]), (gf[:], io["gateT"][H:2 * H]),
                             (small[:, 0:1], io["b_ig"]), (small[:, 1:2], io["b_fg"]), (m0[:], io["m0"]),
                             (anti[:], io["c_anti"]), (repl[:], io["c_repl"]), (smask[:], io["c_smask"])):
                sp.dma_start(dst, src).then_inc(loaded, 16)
            sp.wait_ge(dve_s, EXT)
            sp.dma_start(io["ext"], ext[:]).then_inc(ext_out, 16)
            sp.wait_ge(ext_out, 16)
            e = io["ext"].tensor
            sp.dma_start(hank[:], bass.AP(tensor=e, offset=0, ap=[[1, P], [HJ, 8], [1, 2 * W]])).then_inc(ext_in, 16)
            for g in range(2):
                for t in range(DT):
                    sp.dma_start(srow[g * 16 + t * J:g * 16 + t * J + J, :],
                                 bass.AP(tensor=e, offset=g * J * HJ + 127 - t, ap=[[HJ, J], [1, 132]])).then_inc(ext_in, 16)
            sp.wait_ge(act_s, SCALES)
            sp.dma_start(io["xsT"], xs[:]).then_inc(stored, 16)
            sp.dma_start(io["p_m"], run[:, SEQ - 1:SEQ]).then_inc(stored, 16)
            sp.dma_start(io["s_m"], m_last[:]).then_inc(stored, 16)
            sp.wait_ge(stored, 48)

        @block.gpsimd
        def _(pool):
            nc.gpsimd.memset(ue[:], 0.0).then_inc(pool_s, 1)
            nc.gpsimd.memset(start[:], 1.0).then_inc(pool_s, 1)
            pool.wait_ge(pool_s, 2)
            nc.gpsimd.memset(start[:, 0:SEQ:C], 0.0).then_inc(pool_s, 1)
            nc.gpsimd.memset(mprev[:], 0.0).then_inc(pool_s, 1)

        @block.scalar
        def _(act):
            a = Steps(act, act_s)
            act.wait_ge(dve_s, CAPPED_BIAS)
            a(nc.scalar.activation(gi[:], gi[:], ACT.Tanh, scale=1 / CAP, bias=small[:, 2:3]))
            a(nc.scalar.activation(gf[:], gf[:], ACT.Tanh, scale=1 / CAP, bias=small[:, 3:4]))
            a(nc.scalar.activation(gf[:], gf[:], ACT.Exp, scale=-CAP))
            act.wait_ge(dve_s, ONE_MORE)
            a(nc.scalar.activation(gf[:], gf[:], ACT.Ln))
            act.wait_ge(dve_s, MAXIMA)
            a(nc.scalar.activation(ue[32:32 + H], run[:], ACT.Exp, scale=-1.0))
            act.wait_ge(dve_s, EXPONENTS)
            a(nc.scalar.activation(xs[:, 1, 0:SEQ], xs[:, 1, 0:SEQ], ACT.Exp))
            a(nc.scalar.activation(xs[:, 1, SEQ:NT], xs[:, 1, SEQ:NT], ACT.Exp))

        @block.vector
        def _(dve):
            v = Steps(dve, dve_s)
            dve.wait_ge(loaded, 16 * 11)
            dve.wait_ge(pe_s, 1)
            v(nc.vector.tensor_copy(ext[:], ps[0:8, 0, 0:HJ]))
            v(nc.vector.tensor_tensor(ext[:], ext[:], outside[:], ALU.add))
            v(nc.vector.tensor_scalar(small[:, 2:3], small[:, 0:1], 1 / CAP, None, ALU.mult))
            v(nc.vector.tensor_scalar(small[:, 3:4], small[:, 1:2], 1 / CAP, None, ALU.mult))
            dve.wait_ge(act_s, SIGMOIDS)
            v(nc.vector.tensor_scalar(gf[:], gf[:], 1.0, None, ALU.add))
            dve.wait_ge(act_s, LOGS)
            v(nc.vector.tensor_scalar(gf[:], gf[:], -1.0, None, ALU.mult))
            v(nc.vector.tensor_scalar(gi[:], gi[:], CAP, None, ALU.mult))
            dve.wait_ge(pool_s, 4)
            v(nc.vector.tensor_tensor_scan(b[:, 0:SEQ], start[:], gf[:, 0:SEQ], 0.0, ALU.mult, ALU.add))
            v(nc.vector.tensor_tensor_scan(run[:, 0:SEQ], gf[:, 0:SEQ], gi[:, 0:SEQ], 0.0, ALU.add, ALU.max))
            at = lambda r, t: r[:, SEQ + t:NT:DT]
            v(nc.vector.tensor_copy(at(b, 0), at(gf, 0)))
            for t in range(1, DT):
                v(nc.vector.tensor_tensor(at(b, t), at(b, t - 1), at(gf, t), ALU.add))
            for t in range(DT):
                v(nc.vector.tensor_tensor(at(run, t), m0[:] if t == 0 else at(run, t - 1), at(gf, t), ALU.add))
                if t < DT - 1:
                    v(nc.vector.tensor_tensor(at(run, t), at(run, t), at(gi, t), ALU.max))
            v(nc.vector.tensor_tensor(at(run, DT - 1), at(run, DT - 1), at(gi, DT - 1), ALU.max))
            assert v.k == MAXIMA
            v(nc.vector.tensor_tensor(xs[:, 0], b[:], run[:], ALU.subtract))
            v(nc.vector.tensor_copy(m_last[:], at(run, DT - 1)))
            v(nc.vector.tensor_copy(mprev[:, 1:NC], run[:, C - 1:SEQ - 1:C]))
            v(nc.vector.tensor_tensor(xs[:, 1, 0:SEQ].rearrange("h (c t) -> h c t", t=C),
                                      xs[:, 0, 0:SEQ].rearrange("h (c t) -> h c t", t=C),
                                      mprev[:].unsqueeze(2).broadcast_to([H, NC, C]), ALU.add))
            v(nc.vector.tensor_tensor(xs[:, 1, SEQ:NT].rearrange("h (c t) -> h c t", t=DT),
                                      xs[:, 0, SEQ:NT].rearrange("h (c t) -> h c t", t=DT),
                                      m0[:].unsqueeze(2).broadcast_to([H, DB, DT]), ALU.add))
            v(nc.vector.tensor_tensor(ue[0:H], gi[:], b[:], ALU.subtract))
            assert v.k == U
            for i in range(3):
                dve.wait_ge(pe_s, 2 + i)
                n = min(8, NC + 1 - 8 * i)
                rows = P if i < 2 else NS
                v(nc.vector.tensor_copy(cols[0:rows, 8 * i:8 * i + n], pt[0:rows, i, 0:n * 64].rearrange("p (c r) -> p c r", r=64)))
            assert v.k == TURNED
            for i in range(4):
                dve.wait_ge(pe_s, 5 + i)
                src = ps[:, i, :].rearrange("p (h k) -> p h k", k=2 * W)
                v(nc.vector.tensor_copy(bias_prev[:, 2 * i:2 * i + 2], src[:, :, 0:W]))
                v(nc.vector.tensor_copy(bias[:, 2 * i:2 * i + 2, W:2 * W], src[:, :, W:2 * W]))
            v(nc.vector.memset(bias[:, :, 0:W], NEG))
            dve.wait_ge(pe_s, 9)
            v(nc.vector.tensor_copy(srow_all[:], pt[:, 0, 0:132]))
            sb = keep["sbias"]
            v(nc.vector.tensor_copy(sb[:, :, 0:P], srow_all[:, 0:P].unsqueeze(1).broadcast_to([P, 2, P])))
            for half in range(2):
                v(nc.vector.tensor_tensor(sb[:, half, P:].rearrange("p (b t) -> p b t", t=DT),
                                          smask[:, half].rearrange("p (b t) -> p b t", t=DT),
                                          srow_all[:, P:132].unsqueeze(1).broadcast_to([P, DB, DT]), ALU.add))

        @block.tensor
        def _(pe):
            q = lambda ins: ins.then_inc(pe_s, 1)
            pe.wait_ge(loaded, 16 * 11)
            q(pe.matmul(ps[0:8, 0, 0:HJ], relb[:], onehot[:], start=True, stop=True))
            pe.wait_ge(act_s, EXP_M)
            pe.wait_ge(dve_s, U)
            pe.wait_ge(keep["ident_in"], 16)
            for i in range(3):
                for c in range(8 * i, min(8 * i + 8, NC + 1)):
                    n = C if c < NC else NS
                    last = pe.transpose(pt[0:n, i, (c - 8 * i) * 64:(c - 8 * i + 1) * 64],
                                        ue[:, c * C:c * C + n], ident[0:64, 0:64])
                q(last)
            pe.wait_ge(ext_in, 16 * 9)
            pe.wait_ge(dve_s, TURNED)
            for i in range(4):
                q(pe.matmul(ps[:, i, :], anti[:], hank[:, 2 * i:2 * i + 2, :], start=True, stop=True))
            q(pe.matmul(pt[:, 0, 0:132], repl[:], srow[:], start=True, stop=True))


def prompt(nc, io, keep):
    cols, bias, bias_prev, ident = keep["cols"], keep["bias"], keep["bias_prev"], keep["ident"]
    with ExitStack() as ctx:
        m = Store(nc, ctx)
        inp = m.sb("inp", [P, 2, 20, C])
        kwin = m.sb("kwin", [P, 2, 2 * W])
        svT = m.sb("svT", [P, 2, W])
        xs = m.sb("xs_b", [P, 2, H, 2, C])
        causal = m.sb("causal", [P, C])
        sinks = m.sb("sinks", [P, 8])
        gml = m.sb("gml", [P, H])
        expo = m.sb("expo", [P, H, C])
        decay = m.sb("decay", [P, H, C])
        qs = m.sb("qs", [P, H, C])
        prob = m.sb("prob", [P, H, C])
        kw = m.sb("kw", [P, H, P])
        vaug = m.sb("vaug", [P, H, P + 1])
        state = m.sb("state", [P, H, P + 1])
        nlast = m.sb("nlast", [P, H])
        den = m.sb("den", [P, H])
        ucol = m.sb("ucol", [P, H])
        rec = m.sb("rec", [P, H])
        ssq = m.sb("ssq", [P, H])
        root = m.sb("root", [P, H])
        sqjunk = m.sb("sqjunk", [P, H, P])
        hn = m.sb("hn", [P, H, P])
        gate = m.sb("gate", [P, H, C])
        sq8 = m.sb("sq8", [P, J, C])
        vs = m.sb("vs", [P, 2, P])
        sw = m.sb("sw", [P, 2, 2, 2 * W])
        pw = m.sb("pw", [P, 2, 2, 2 * W])
        nmx = m.sb("nmx", [P, 8])
        mx = m.sb("mx", [P, 8])
        psums = m.sb("psums", [P, 8])
        snk = m.sb("snk", [P, 8])
        ptw = m.sb("ptw", [P, 2, 4, W])
        ow = m.sb("ow", [P, 4, P])
        mix = m.sb("mixed", [P, 2, 8, C])
        m0, m3 = m.ps("m0b", [P, 512]), m.ps("m3b", [P, 512])
        m12 = m.ps("m12", [P, 2, 512])
        w01 = m.ps("w01", [P, 2, 512])
        w2, w3 = m.ps("w2b", [P, 512]), m.ps("w3b", [P, 512])
        heads_out = m12[:, :, 0:258].rearrange("p b (h e) -> p b h e", e=P + 1)

        const_in, zeroed, fence = m.sem("c_const"), m.sem("c_zeroed"), m.sem("c_fence")
        loaded = [m.sem(f"c_loaded{s}") for s in range(2)]
        names = ("k_turned v_turned scores sv_turned win out_ml state_up p_turned swa_out h_turned o_turned "
                 "e_ready qs_ready sv_ready nmx_ready p_ready kw_ready st_ready den_ready hn_ready ml_mixed "
                 "ow_ready msq_ready snk_arg sq_ready v_copied d_exp eo_ready p_exp pt_copied ssq_ready root_ready snk_exp chunk_done").split()
        S = {n: m.sem("c_" + n) for n in names}
        each = dict.fromkeys(names, 1) | dict.fromkeys(("win", "p_turned", "nmx_ready", "p_exp", "pt_copied"), 4)
        dve_s = m.sem("c_dve")
        DVE_STEPS = 17
        mix_out = [m.sem(f"c_mix_out{s}") for s in range(2)]
        kv_out, st_out = m.sem("c_kv_out"), m.sem("c_st_out")

        def wait(eng, name, c, k=1):
            eng.wait_ge(S[name], c * each[name] + k + 1)

        block = ctx.enter_context(nc.Block())

        @block.sync
        def _(sp):
            def load(c, s):
                tok = bass.ds(c * C, C)
                sp.dma_start(inp[:, s], io["projT"][0:20, :, tok].rearrange("t p n -> p t n")).then_inc(loaded[s], 16)
                sp.dma_start(kwin[:, s], bass.AP(tensor=io["projT"].tensor, offset=SK * P * NT - W + c * C,
                                                 ap=[[NT, P], [1, 2 * W]])).then_inc(loaded[s], 16)
                sp.dma_start(svT[:, s], io["projT"][SV, :, tok]).then_inc(loaded[s], 16)
                sp.dma_start(xs[:, s].rearrange("p h w n -> p (h w) n"),
                             bass.AP(tensor=io["xsT"].tensor, offset=c * C, ap=[[0, P], [NT, 2 * H], [1, C]])).then_inc(loaded[s], 16)

            def store(c, s):
                sp.dma_start(io["mixT"][:, :, bass.ds(c * C, C)].rearrange("t p n -> p t n"), mix[:, s]).then_inc(mix_out[s], 16)

            for dst, src in ((causal[:], io["c_causal"]), (sinks[:], bass.AP(tensor=io["sinks"].tensor, offset=0, ap=[[0, P], [1, 8]])), (gml[:], io["g_ml"])):
                sp.dma_start(dst, src).then_inc(const_in, 16)
            for s in range(2):
                load(s, s)
            sp.dma_start(io["p_k"], io["projT"][SK, :, SEQ - W:SEQ]).then_inc(kv_out, 16)
            sp.dma_start(io["p_v"], io["projT"][SV, :, SEQ - W:SEQ]).then_inc(kv_out, 16)
            with sp.Fori(0, NC // 2 - 1) as i:
                for s in range(2):
                    wait(sp, "chunk_done", 2 * i + s)
                    sp.wait_ge(const_in, 48)
                    load(2 * i + 2 + s, s)
                    store(2 * i + s, s)
            for s in range(2):
                wait(sp, "chunk_done", NC - 2 + s)
                store(NC - 2 + s, s)
            sp.wait_ge(dve_s, NC * DVE_STEPS + 1)
            sp.dma_start(io["p_C"], state[:, :, 0:P]).then_inc(st_out, 16)
            sp.dma_start(io["p_n"], nlast[:]).then_inc(st_out, 16)
            sp.wait_ge(st_out, 32)
            sp.wait_ge(kv_out, 32)
            for s in range(2):
                sp.wait_ge(mix_out[s], 8 * NC + 16)

        @block.gpsimd
        def _(pool):
            nc.gpsimd.memset(state[:], 0.0).then_inc(zeroed, 1)
            nc.gpsimd.memset(vs[:], 0.0).then_inc(zeroed, 1)
            nc.gpsimd.memset(vaug[:], 1.0).then_inc(zeroed, 1)
            for n in names:
                pool.sem_inc(S[n], 1)
            for s in range(2):
                pool.sem_inc(mix_out[s], 16)

        @block.tensor
        def _(pe):
            pe.wait_ge(zeroed, 3)
            with pe.Fori(0, NC // 2) as i:
                for s in range(2):
                    c = 2 * i + s
                    q, k, v = inp[:, s, MQ:MQ + 4], inp[:, s, MK:MK + 4], inp[:, s, MV:MV + 4]

                    def window_scores(r):
                        wait(pe, "nmx_ready", c, r)
                        for g in range(2):
                            gp = slice(64 * g, 64 * g + 64)
                            for a in range(2):
                                last = pe.matmul(w01[:, g, a * 256:a * 256 + 256], sq8[gp, r + a], kwin[gp, s],
                                                 start=True, stop=True)
                            last.then_inc(S["win"], 1)

                    def turn_window(r):
                        wait(pe, "p_exp", c, r + 1)
                        if r:
                            wait(pe, "pt_copied", c, r)
                        for g in range(2):
                            for half in range(2):
                                last = pe.transpose(w2[:, (2 * g + half) * W:(2 * g + half + 1) * W],
                                                    pw[:, r % 2, g, half * W:half * W + W], ident[:])
                        last.then_inc(S["p_turned"], 1)

                    def window_values(r):
                        wait(pe, "pt_copied", c, r + 1)
                        for g in range(2):
                            for half in range(2):
                                last = pe.matmul(w3[:, r * P + g * 64:r * P + g * 64 + 64], ptw[:, r % 2, 2 * g + half],
                                                 vs[:, s if half else 1 - s, g * 64:g * 64 + 64],
                                                 start=(half == 0), stop=(half == 1))
                        return last

                    pe.wait_ge(loaded[s], i * 64 + 64)
                    wait(pe, "st_ready", c, 0)
                    for h in range(H):
                        last = pe.transpose(m0[:, h * C:h * C + C], k[:, h], ident[:])
                    last.then_inc(S["k_turned"], 1)
                    wait(pe, "hn_ready", c, 0)
                    for h in range(H):
                        last = pe.transpose(m12[:, 0, h * C:h * C + C], v[:, h], ident[:])
                    last.then_inc(S["v_turned"], 1)
                    for h in range(H):
                        last = pe.matmul(m12[:, 1, h * C:h * C + C], k[:, h], q[:, h], start=True, stop=True)
                    last.then_inc(S["scores"], 1)
                    wait(pe, "ow_ready", c, 0)
                    pe.transpose(w3[:, 0:P], svT[:, s], ident[:]).then_inc(S["sv_turned"], 1)
                    wait(pe, "sq_ready", c)
                    window_scores(0)
                    wait(pe, "chunk_done", c, 0)
                    turn_window(0)
                    turn_window(1)
                    window_scores(2)
                    wait(pe, "p_ready", c)
                    wait(pe, "v_copied", c)
                    wait(pe, "qs_ready", c)
                    for h in range(H):
                        pe.matmul(heads_out[:, h // 2, h % 2], prob[:, h], vaug[:, h], start=True, stop=False)
                        last = pe.matmul(heads_out[:, h // 2, h % 2], qs[:, h], state[:, h], start=False, stop=True)
                    last.then_inc(S["out_ml"], 1)
                    wait(pe, "kw_ready", c)
                    wait(pe, "ml_mixed", c, 0)
                    for h in range(H):
                        last = pe.matmul((m3, m0)[h // 2][:, (h % 2) * 129:(h % 2) * 129 + 129], kw[:, h], vaug[:, h],
                                         start=True, stop=True)
                    last.then_inc(S["state_up"], 1)
                    wait(pe, "sv_ready", c)
                    window_values(0)
                    turn_window(2)
                    window_values(1)
                    turn_window(3)
                    window_values(2)
                    window_values(3).then_inc(S["swa_out"], 1)
                    wait(pe, "hn_ready", c)
                    wait(pe, "st_ready", c)
                    for h in range(H):
                        last = pe.transpose(m3[:, h * C:h * C + C], hn[:, h], ident[:])
                    last.then_inc(S["h_turned"], 1)
                    wait(pe, "ow_ready", c)
                    wait(pe, "pt_copied", c, 4)
                    for r in range(J):
                        last = pe.transpose(w2[:, r * C:r * C + C], ow[:, r], ident[:])
                    last.then_inc(S["o_turned"], 1)

        @block.scalar
        def _(act):
            with act.Fori(0, NC // 2) as i:
                for s in range(2):
                    c = 2 * i + s

                    def window_exp(r):
                        wait(act, "nmx_ready", c, r + 1)
                        for g in range(2):
                            a = 2 * r + g
                            last = nc.scalar.activation(pw[:, r % 2, g], sw[:, r % 2, g], ACT.Exp, bias=nmx[:, a:a + 1],
                                                        accum_out=psums[:, a:a + 1])
                        last.then_inc(S["p_exp"], 1)

                    def copy_turned(r):
                        wait(act, "p_turned", c, r + 1)
                        nc.scalar.activation(ptw[:, r % 2].rearrange("p a q -> p (a q)"), w2[:], ACT.Copy).then_inc(S["pt_copied"], 1)

                    act.wait_ge(loaded[s], i * 64 + 64)
                    wait(act, "swa_out", c, 0)
                    nc.scalar.activation(sq8[:], inp[:, s, SQ:SQ + 4], ACT.Copy, scale=SWA_SCALE).then_inc(S["sq_ready"], 1)
                    wait(act, "v_turned", c)
                    nc.scalar.activation(vaug[:, :, 0:P], m12[:, 0].rearrange("p (h e) -> p h e", e=P), ACT.Copy).then_inc(S["v_copied"], 1)
                    wait(act, "e_ready", c)
                    nc.scalar.activation(decay[:], expo[:], ACT.Exp).then_inc(S["d_exp"], 1)
                    nc.scalar.activation(gate[:], inp[:, s, MO:MO + 4], ACT.Exp, scale=-1.0).then_inc(S["eo_ready"], 1)
                    window_exp(0)
                    window_exp(1)
                    copy_turned(0)
                    window_exp(2)
                    copy_turned(1)
                    window_exp(3)
                    copy_turned(2)
                    wait(act, "den_ready", c)
                    for h in range(H):
                        last = nc.scalar.activation(sqjunk[:, h], heads_out[:, h // 2, h % 2, 0:P], ACT.Square,
                                                    accum_out=ssq[:, h:h + 1])
                    last.then_inc(S["ssq_ready"], 1)
                    copy_turned(3)
                    wait(act, "snk_arg", c)
                    nc.scalar.activation(snk[:], snk[:], ACT.Exp).then_inc(S["snk_exp"], 1)
                    wait(act, "msq_ready", c)
                    nc.scalar.activation(root[:], root[:], ACT.Sqrt).then_inc(S["root_ready"], 1)

        @block.vector
        def _(dve):
            dve.wait_ge(const_in, 48)
            dve.wait_ge(zeroed, 3)
            with dve.Fori(0, NC // 2) as i:
                for s in range(2):
                    c = 2 * i + s
                    v = Steps(dve, dve_s, c, DVE_STEPS)
                    emcol = cols[:, bass.ds(c, 1), 32:32 + H]
                    x_b, sc_b = xs[:, s, :, 0], xs[:, s, :, 1]

                    def window_max(r):
                        wait(dve, "win", c, 2 * (r // 2) + 2)
                        if r >= 2:
                            wait(dve, "p_exp", c, r - 1)
                        dve.sem_inc(fence, 1)
                        for g in range(2):
                            a, hd = 2 * r + g, g * J + r
                            last = nc.vector.tensor_tensor_reduce(
                                sw[:, r % 2, g], w01[:, g, (r % 2) * 256:(r % 2) * 256 + 256], bias[:, hd], 1.0,
                                sinks[:, a:a + 1], ALU.add, ALU.max, mx[:, a:a + 1])
                        v(last)
                        nc.vector.tensor_scalar(nmx[:, 2 * r:2 * r + 2], mx[:, 2 * r:2 * r + 2], -1.0, None,
                                                ALU.mult).then_inc(S["nmx_ready"], 1)

                    dve.wait_ge(loaded[s], i * 64 + 64)
                    v(nc.vector.tensor_copy(ucol[:].unsqueeze(1), cols[:, bass.ds(c, 1), 0:H]))
                    for h in range(H):
                        last = nc.vector.scalar_tensor_tensor(expo[:, h], x_b[:, h], ucol[:, h:h + 1], causal[:],
                                                              ALU.add, ALU.add)
                    last.then_inc(S["e_ready"], 1)
                    nc.vector.tensor_tensor(qs[:], inp[:, s, MQ:MQ + 4], sc_b, ALU.mult).then_inc(S["qs_ready"], 1)
                    wait(dve, "sv_turned", c)
                    nc.vector.tensor_copy(vs[:, s], w3[:, 0:P]).then_inc(S["sv_ready"], 1)
                    window_max(0)
                    window_max(1)
                    wait(dve, "d_exp", c)
                    wait(dve, "scores", c)
                    nc.vector.scalar_tensor_tensor(prob[:].rearrange("p h t -> p (h t)"), m12[:, 1], ML_SCALE,
                                                   decay[:].rearrange("p h t -> p (h t)"), ALU.mult, ALU.mult).then_inc(S["p_ready"], 1)
                    wait(dve, "k_turned", c)
                    nc.vector.scalar_tensor_tensor(kw[:], m0[:].rearrange("p (h e) -> p h e", e=P), ML_SCALE,
                                                   decay[:, :, C - 1:C].broadcast_to([P, H, P]), ALU.mult, ALU.mult).then_inc(S["kw_ready"], 1)
                    window_max(2)
                    window_max(3)
                    dve.wait_ge(S["nmx_ready"], 4 * c + 5)
                    nc.vector.tensor_copy(bias[:, :, 0:W], bias_prev[:])
                    nc.vector.tensor_tensor(snk[:], sinks[:], nmx[:], ALU.add).then_inc(S["snk_arg"], 1)
                    wait(dve, "out_ml", c)
                    nc.vector.tensor_copy(den[:].rearrange("p (b h) -> p b h", h=2).unsqueeze(3),
                                          heads_out[:, :, :, P:P + 1]).then_inc(S["den_ready"], 1)
                    wait(dve, "state_up", c)
                    for h in range(H):
                        last = nc.vector.scalar_tensor_tensor(state[:, h], state[:, h], sc_b[:, h, C - 1:C],
                                                              (m3, m0)[h // 2][:, (h % 2) * 129:(h % 2) * 129 + 129],
                                                              ALU.mult, ALU.add)
                    last.then_inc(S["st_ready"], 1)
                    wait(dve, "den_ready", c)
                    v(nc.vector.scalar_tensor_tensor(rec[:], den[:], -1.0, den[:], ALU.mult, ALU.max))
                    v(nc.vector.tensor_tensor(rec[:].unsqueeze(1), rec[:].unsqueeze(1), emcol, ALU.max))
                    v(nc.vector.reciprocal(rec[:], rec[:]))
                    wait(dve, "ssq_ready", c)
                    v(nc.vector.tensor_tensor(root[:], ssq[:], rec[:], ALU.mult))
                    v(nc.vector.tensor_tensor(root[:], root[:], rec[:], ALU.mult))
                    nc.vector.tensor_scalar(root[:], root[:], 1.0 / P, NORM_EPS, ALU.mult, ALU.add).then_inc(S["msq_ready"], 1)
                    wait(dve, "eo_ready", c)
                    v(nc.vector.tensor_scalar(gate[:], gate[:], 1.0, None, ALU.add))
                    v(nc.vector.reciprocal(gate[:], gate[:]))
                    v(nc.vector.tensor_tensor(gate[:], gate[:], gml[:].unsqueeze(2).broadcast_to([P, H, C]), ALU.mult))
                    wait(dve, "root_ready", c)
                    v(nc.vector.reciprocal(root[:], root[:]))
                    v(nc.vector.tensor_tensor(rec[:], rec[:], root[:], ALU.mult))
                    nc.vector.tensor_tensor(hn[:].rearrange("p (b h) e -> p b h e", h=2), heads_out[:, :, :, 0:P],
                                            rec[:].rearrange("p (b h) -> p b h", h=2).unsqueeze(3).broadcast_to([P, 2, 2, P]),
                                            ALU.mult).then_inc(S["hn_ready"], 1)
                    wait(dve, "snk_exp", c)
                    v(nc.vector.tensor_tensor(snk[:], snk[:], psums[:], ALU.add))
                    v(nc.vector.reciprocal(snk[:], snk[:]))
                    wait(dve, "swa_out", c)
                    nc.vector.tensor_tensor(ow[:].rearrange("p r (g d) -> p (r g) d", g=2), w3[:].rearrange("p (a d) -> p a d", d=64),
                                            snk[:].unsqueeze(2).broadcast_to([P, 8, 64]), ALU.mult).then_inc(S["ow_ready"], 1)
                    dve.wait_ge(mix_out[s], i * 16 + 16)
                    wait(dve, "h_turned", c)
                    nc.vector.tensor_tensor(mix[:, s, 0:4].rearrange("p h t -> p (h t)"), m3[:],
                                            gate[:].rearrange("p h t -> p (h t)"), ALU.mult).then_inc(S["ml_mixed"], 1)
                    wait(dve, "o_turned", c)
                    nc.vector.tensor_copy(mix[:, s, 4:8].rearrange("p h t -> p (h t)"), w2[:]).then_inc(S["chunk_done"], 1)
                    v.end()
            dve.wait_ge(S["st_ready"], NC + 1)
            nc.vector.tensor_copy(nlast[:].unsqueeze(2), state[:, :, P:P + 1]).then_inc(dve_s, 1)


def sample(nc, io, keep):
    cols, ident, sbias = keep["cols"], keep["ident"], keep["sbias"]
    with ExitStack() as ctx:
        m = Store(nc, ctx)
        inp = m.sb("s_inp", [P, NPROJ, NS])
        xs = m.sb("s_xs", [P, H, 2, NS])
        state = m.sb("s_state", [P, DB * H, P + 1])
        n0 = m.sb("s_n0", [P, DB * H])
        kc = m.sb("s_kc", [P, DB, W])
        vc = m.sb("s_vc", [P, DB, P])
        causal = m.sb("s_causal", [NS, NS])
        sinkcol = m.sb("s_sinkcol", [P, 1])
        gml = m.sb("s_gml", [P, H])
        expo = m.sb("s_expo", [NS, H, NS])
        decay = m.sb("s_decay", [NS, H, NS])
        prob = m.sb("s_prob", [NS, H, NS])
        vaug = m.sb("s_vaug", [NS, H, P + 1])
        ktok = m.sb("s_ktok", [NS, H, P])
        kw = m.sb("s_kw", [NS, DB, H, P])
        qs = m.sb("s_qs", [P, H, DB * (NS + DT)])
        qb = m.sb("s_qb", [P, DB, 2, DT, J])
        swin = m.sb("s_swin", [P, 2, W + NS])
        mx, nmx, psums, snk = (m.sb(n, [P, 2]) for n in ("s_mx", "s_nmx", "s_psums", "s_snk"))
        kvtok = m.sb("s_kvtok", [NS, 2, P])
        pt1 = m.sb("s_pt1", [P, 2, P])
        pt2 = m.sb("s_pt2", [NS, 2, P])
        den, rec, ssq, root = (m.sb(n, [NS, H]) for n in ("s_den", "s_rec", "s_ssq", "s_root"))
        sqjunk = m.sb("s_sqjunk", [NS, H, P])
        hn = m.sb("s_hn", [NS, H, P])
        gate = m.sb("s_gate", [P, H, NS])
        mix = m.sb("s_mixed", [P, 8, NS])
        kv = m.ps("s_kv", [P, 2, 512])
        upd = m.ps("s_upd", [P, 2, 512])
        ho = m.ps("s_ho", [P, 2, 512])
        sc = m.ps("s_sc", [P, 512])
        wi = m.ps("s_wi", [P, 512])
        heads_out = ho[0:NS, :, 0:258].rearrange("p b (h e) -> p b h e", e=P + 1)
        names = "loaded zeroed v_done a_done kv_turned scores win p_turned win_out heads up h_turned stored".split()
        S = {n: m.sem("s_" + n) for n in names}
        LOADS = 12
        block = ctx.enter_context(nc.Block())
        sig = {n: m.sem("s_v_" + n) for n in ("expo", "prob", "kw", "nmx", "snk", "wprob", "pt", "den", "msq", "hn", "state", "mixed", "tok", "qb", "qs")}

        @block.sync
        def _(sp):
            tok = slice(SEQ, NT)
            for dst, src in (
                    (inp[:], io["projT"][:, :, tok].rearrange("t p n -> p t n")),
                    (xs[:].rearrange("p h w n -> p (h w) n"),
                     bass.AP(tensor=io["xsT"].tensor, offset=SEQ, ap=[[0, P], [NT, 2 * H], [1, NS]])),
                    (causal[:], io["c_causal_s"]), (sinkcol[:], io["sink_col"]), (gml[:], io["g_ml"]), (n0[:], io["n0"]),
                    (kc[:], io["cache_kT"]), (vc[:], io["cache_v"].rearrange("b k n -> k b n")),
                    *((state[:, q * 8:q * 8 + 8, 0:P], io["state_C"][:, q * 8:q * 8 + 8]) for q in range(4))):
                sp.dma_start(dst, src).then_inc(S["loaded"], 16)
            for a in "kv":
                sp.dma_start(io[f"s_{a}"][:, 0:W - DT], io[f"cache_{a}"][:, DT:W]).then_inc(S["stored"], 16)
            sp.wait_ge(sig["tok"], 1)
            for i, a in enumerate("kv"):
                sp.dma_start(io[f"s_{a}"][:, W - DT:W], kvtok[:, i]).then_inc(S["stored"], 16)
            sp.wait_ge(sig["mixed"], 3)
            sp.dma_start(io["mixT"][:, :, tok].rearrange("t p n -> p t n"), mix[:]).then_inc(S["stored"], 16)
            sp.wait_ge(sig["state"], DB + 1)
            sp.dma_start(io["s_C"], state[:, :, 0:P]).then_inc(S["stored"], 16)
            sp.dma_start(io["s_n"], n0[:]).then_inc(S["stored"], 16)
            sp.wait_ge(S["stored"], 7 * 16)

        @block.gpsimd
        def _(pool):
            nc.gpsimd.memset(qs[:], 0.0).then_inc(S["zeroed"], 1)
            nc.gpsimd.memset(qb[:], 0.0).then_inc(S["zeroed"], 1)
            nc.gpsimd.memset(vaug[:], 1.0).then_inc(S["zeroed"], 1)

        @block.tensor
        def _(pe):
            pe.wait_ge(S["loaded"], 16 * LOADS)
            for i, a in enumerate((SK, SV)):
                last = pe.transpose(sc[0:NS, P + i * P:2 * P + i * P], inp[:, a], ident[:])
            for h in range(H):
                pe.transpose(kv[0:NS, 0, h * P:h * P + P], inp[:, MK + h], ident[:])
                last = pe.transpose(kv[0:NS, 1, h * P:h * P + P], inp[:, MV + h], ident[:])
            last.then_inc(S["kv_turned"], 1)
            for h in range(H):
                last = pe.matmul(sc[0:NS, h * NS:h * NS + NS], inp[:, MK + h], inp[:, MQ + h], start=True, stop=True)
            last.then_inc(S["scores"], 1)
            pe.wait_ge(sig["qb"], 2)
            for b in range(DB):
                half, rows = b // 4, slice(32 * (b % 4), 32 * (b % 4) + 32)
                q = qb[:, b].rearrange("p g t j -> p (g t j)")
                pe.matmul(wi[rows, half * 160:half * 160 + W], q, kc[:, b], start=True, stop=True)
                last = pe.matmul(wi[rows, half * 160 + W:half * 160 + 160], q, inp[:, SK], start=True, stop=True)
            last.then_inc(S["win"], 1)
            pe.wait_ge(sig["prob"], 2)
            pe.wait_ge(sig["qs"], 1)
            for h in range(H):
                pe.matmul(heads_out[:, h // 2, h % 2], prob[:, h], vaug[:, h], start=True, stop=False)
                for b in range(DB):
                    last = pe.matmul(heads_out[:, h // 2, h % 2], qs[:, h, b * NS:b * NS + NS], state[:, b * H + h],
                                     start=False, stop=(b == DB - 1))
            last.then_inc(S["heads"], 1)
            pe.wait_ge(sig["wprob"], 1)
            for half in range(2):
                pe.transpose(wi[:, half * P:half * P + P], swin[:, half, 0:W], ident[:])
                last = pe.transpose(wi[0:NS, 256 + half * P:256 + half * P + P], swin[:, half, W:W + NS], ident[:])
            last.then_inc(S["p_turned"], 1)
            for b in range(DB):
                pe.wait_ge(sig["kw"], b + 1)
                if b >= 2:
                    pe.wait_ge(sig["state"], b)
                for h in range(H):
                    last = pe.matmul((upd, kv)[b % 2][:, h // 2, (h % 2) * 129:(h % 2) * 129 + 129], kw[:, b, h], vaug[:, h],
                                     start=True, stop=True)
                last.then_inc(S["up"], 1)
            pe.wait_ge(sig["pt"], 1)
            for b in range(DB):
                half, c = b // 4, slice(32 * (b % 4), 32 * (b % 4) + 32)
                pe.matmul(sc[:, b * 32:b * 32 + 32], vc[:, b], pt1[:, half, c], start=True, stop=False)
                last = pe.matmul(sc[:, b * 32:b * 32 + 32], kvtok[:, 1], pt2[:, half, c], start=False, stop=True)
            last.then_inc(S["win_out"], 1)
            pe.wait_ge(sig["hn"], 1)
            for h in range(H):
                last = pe.transpose(wi[:, h * NS:h * NS + NS], hn[:, h], ident[0:NS, 0:NS])
            last.then_inc(S["h_turned"], 1)

        @block.scalar
        def _(act):
            a = Steps(act, S["a_done"])
            act.wait_ge(S["loaded"], 16 * LOADS)
            a(nc.scalar.activation(gate[:], inp[:, MO:MO + 4], ACT.Exp, scale=-1.0))
            act.wait_ge(sig["expo"], 1)
            a(nc.scalar.activation(decay[:], expo[:], ACT.Exp))
            act.wait_ge(sig["nmx"], 1)
            for half in range(2):
                a(nc.scalar.activation(swin[:, half], swin[:, half], ACT.Exp, bias=nmx[:, half:half + 1],
                                       accum_out=psums[:, half:half + 1]))
            act.wait_ge(sig["snk"], 1)
            a(nc.scalar.activation(snk[:], snk[:], ACT.Exp))
            act.wait_ge(sig["den"], 1)
            for h in range(H):
                a(nc.scalar.activation(sqjunk[:, h], heads_out[:, h // 2, h % 2, 0:P], ACT.Square, accum_out=ssq[:, h:h + 1]))
            act.wait_ge(sig["msq"], 1)
            a(nc.scalar.activation(root[:], root[:], ACT.Sqrt))

        @block.vector
        def _(dve):
            v = Steps(dve, S["v_done"])
            dve.wait_ge(S["loaded"], 16 * LOADS)
            dve.wait_ge(S["zeroed"], 3)
            nc.vector.tensor_copy(state[:, :, P:P + 1], n0[:].unsqueeze(2)).then_inc(sig["state"], 1)
            for g in range(2):
                gp = slice(64 * g, 64 * g + 64)
                nc.vector.tensor_scalar(qb[gp, :, g], inp[gp, SQ:SQ + 4].rearrange("p j (b t) -> p b t j", t=DT),
                                        SWA_SCALE, None, ALU.mult).then_inc(sig["qb"], 1)
            for h in range(H):
                last = nc.vector.scalar_tensor_tensor(expo[:, h], xs[0:NS, h, 0], cols[0:NS, NC, h:h + 1], causal[:],
                                                      ALU.add, ALU.add)
            last.then_inc(sig["expo"], 1)
            for h in range(H):
                last = nc.vector.tensor_tensor(
                    qs[:, h].rearrange("p (b r) -> p b r", r=NS + DT)[:, :, 0:DT],
                    inp[:, MQ + h].rearrange("p (b t) -> p b t", t=DT), xs[:, h, 1].rearrange("p (b t) -> p b t", t=DT), ALU.mult)
            last.then_inc(sig["qs"], 1)
            dve.wait_ge(S["scores"], 1)
            nc.vector.tensor_copy(kvtok[:].rearrange("p a n -> p (a n)"), sc[0:NS, P:3 * P]).then_inc(sig["tok"], 1)
            v(nc.vector.tensor_scalar(ktok[:].rearrange("p h e -> p (h e)"), kv[0:NS, 0], ML_SCALE, None, ALU.mult))
            nc.vector.tensor_copy(vaug[:, :, 0:P], kv[0:NS, 1].rearrange("p (h e) -> p h e", e=P)).then_inc(sig["prob"], 1)
            dve.wait_ge(S["a_done"], 2)
            dve.wait_ge(S["scores"], 1)
            nc.vector.scalar_tensor_tensor(prob[:].rearrange("p h t -> p (h t)"), sc[0:NS, 0:P], ML_SCALE,
                                           decay[:].rearrange("p h t -> p (h t)"), ALU.mult, ALU.mult).then_inc(sig["prob"], 1)
            for b in range(DB):
                e = DT * b + DT - 1
                nc.vector.tensor_tensor(kw[:, b], ktok[:], decay[:, :, e:e + 1].broadcast_to([NS, H, P]), ALU.mult).then_inc(sig["kw"], 1)
            dve.wait_ge(S["win"], 1)
            v(nc.vector.tensor_tensor(swin[:].rearrange("p a k -> p (a k)"), wi[:, 0:320], sbias[:].rearrange("p a k -> p (a k)"), ALU.add))
            v(nc.vector.tensor_reduce(mx[:], swin[:], AX.X, ALU.max))
            v(nc.vector.tensor_scalar(mx[:], mx[:], sinkcol[:, 0:1], None, ALU.max))
            nc.vector.tensor_scalar(nmx[:], mx[:], -1.0, None, ALU.mult).then_inc(sig["nmx"], 1)
            dve.wait_ge(sig["nmx"], 1)
            nc.vector.tensor_scalar(snk[:], nmx[:], sinkcol[:, 0:1], None, ALU.add).then_inc(sig["snk"], 1)
            dve.wait_ge(S["heads"], 1)
            nc.vector.tensor_copy(den[:].rearrange("p (b h) -> p b h", h=2).unsqueeze(3), heads_out[:, :, :, P:P + 1]).then_inc(sig["den"], 1)
            dve.wait_ge(S["a_done"], 5)
            v(nc.vector.tensor_tensor(snk[:], snk[:], psums[:], ALU.add))
            v(nc.vector.reciprocal(snk[:], snk[:]))
            for half in range(2):
                last = nc.vector.tensor_scalar(swin[:, half], swin[:, half], snk[:, half:half + 1], None, ALU.mult)
            last.then_inc(sig["wprob"], 1)
            dve.wait_ge(sig["den"], 1)
            v(nc.vector.scalar_tensor_tensor(rec[:], den[:], -1.0, den[:], ALU.mult, ALU.max))
            v(nc.vector.tensor_tensor(rec[:], rec[:], cols[0:NS, NC, 32:32 + H], ALU.max))
            v(nc.vector.reciprocal(rec[:], rec[:]))
            dve.wait_ge(S["a_done"], 9)
            v(nc.vector.tensor_tensor(root[:], ssq[:], rec[:], ALU.mult))
            v(nc.vector.tensor_tensor(root[:], root[:], rec[:], ALU.mult))
            nc.vector.tensor_scalar(root[:], root[:], 1.0 / P, NORM_EPS, ALU.mult, ALU.add).then_inc(sig["msq"], 1)
            dve.wait_ge(S["p_turned"], 1)
            v(nc.vector.tensor_copy(pt1[:].rearrange("p a n -> p (a n)"), wi[:, 0:256]))
            nc.vector.tensor_copy(pt2[:].rearrange("p a n -> p (a n)"), wi[0:NS, 256:512]).then_inc(sig["pt"], 1)
            dve.wait_ge(S["a_done"], 10)
            v(nc.vector.reciprocal(root[:], root[:]))
            v(nc.vector.tensor_tensor(rec[:], rec[:], root[:], ALU.mult))
            nc.vector.tensor_tensor(hn[:].rearrange("p (b h) e -> p b h e", h=2), heads_out[:, :, :, 0:P],
                                    rec[:].rearrange("p (b h) -> p b h", h=2).unsqueeze(3).broadcast_to([NS, 2, 2, P]),
                                    ALU.mult).then_inc(sig["hn"], 1)
            v(nc.vector.tensor_scalar(gate[:], gate[:], 1.0, None, ALU.add))
            v(nc.vector.reciprocal(gate[:], gate[:]))
            v(nc.vector.tensor_tensor(gate[:], gate[:], gml[:].unsqueeze(2).broadcast_to([P, H, NS]), ALU.mult))
            for b in range(DB):
                dve.wait_ge(S["up"], b + 1)
                for h in range(H):
                    last = nc.vector.scalar_tensor_tensor(
                        state[:, b * H + h], state[:, b * H + h], xs[:, h, 1, DT * b + DT - 1:DT * b + DT],
                        (upd, kv)[b % 2][:, h // 2, (h % 2) * 129:(h % 2) * 129 + 129], ALU.mult, ALU.add)
                if b < DB - 1:
                    last.then_inc(sig["state"], 1)
            v(last)
            nc.vector.tensor_copy(n0[:].unsqueeze(2), state[:, :, P:P + 1]).then_inc(sig["state"], 1)
            dve.wait_ge(S["win_out"], 1)
            for g in range(2):
                gp = slice(64 * g, 64 * g + 64)
                nc.vector.tensor_copy(mix[gp, 4:8].rearrange("p j (b t) -> p b t j", t=DT),
                                      sc[gp, 0:DB * 32].rearrange("p (b g t j) -> p b g t j", g=2, t=DT, j=J)[:, :, g]).then_inc(sig["mixed"], 1)
            dve.wait_ge(S["h_turned"], 1)
            nc.vector.tensor_tensor(mix[:, 0:4].rearrange("p h t -> p (h t)"), wi[:, 0:P],
                                    gate[:].rearrange("p h t -> p (h t)"), ALU.mult).then_inc(sig["mixed"], 1)


def layer(nc, io):
    U1 = (8 + 2 * KF) // 2
    UNITS = U1 + 8
    SLABS = 2 * UNITS
    TILES = 8 + 2 * KF + 8
    BANKS = 4
    with ExitStack() as ctx:
        m = Store(nc, ctx)
        raw = m.sb("l_raw", [P, 2, HALF, P])
        whi = m.sb("l_whi", [P, 2, HALF, P], F32R)
        wlo = m.sb("l_wlo", [P, 2, HALF, P], F32R)
        ah = m.sb("ah", [P, KD, TG], F32R)
        al = m.sb("al", [P, KD, TG], F32R)
        mixr = m.sb("mixr", [P, KD, TG])
        xres = m.sb("xres", [P, KD, TG])
        res = m.sb("res", [P, KD, TG])
        hh = m.sb("hh", [P, KF, TG], F32R)
        hl = m.sb("hl", [P, KF, TG], F32R)
        hbuf = m.sb("hbuf", [P, TG])
        silu = m.sb("silu", [P, 2, TG])
        nrm = m.sb("nrm", [TOK, 2, D])
        g2b = m.sb("g2b", [TOK, D])
        b2b = m.sb("b2b", [TOK, D])
        gb1 = m.sb("gb1", [P, 2, KD])
        ident = m.sb("l_ident", [P, P])
        stats = m.sb("stats", [TOK, 2, 6])
        mv = m.sb("mv", [TOK, 2])
        rstd = m.sb("rstd", [TOK, 2])
        acc = m.ps("l_acc", [P, BANKS, 512])
        turned = m.ps("turned", [P, 2, 512])
        back = m.ps("back", [P, 2, 512])
        S = {n: m.sem("l_" + n) for n in
             "const_in mix_in x_in hi_done lo_done slab_done evac mix_split ta_full tb_full normed root_arg root_done "
             "x1_split silu_done h_hi h_split mix_hi y_ready".split()}
        raw_in = [m.sem(f"l_raw_in{s}") for s in range(2)]
        y_out = [m.sem(f"l_y_out{s}") for s in range(2)]
        dve_s = m.sem("l_dve")
        fences = m.sem("l_fences")

        def apart(eng):
            eng.sem_inc(fences, 1)

        DVE_STEPS = 40
        turned_tok = turned[0:TOK].rearrange("p b n -> p (b n)")

        block = ctx.enter_context(nc.Block())

        @block.sync
        def _(sp):
            def slab8(i, s):
                sp.dma_start(raw[:, s, 0:KD], io["wB"][bass.ds(i, 1)].rearrange("a p k n -> (a p) k n")).then_inc(raw_in[s], 16)

            def slab11(i, s):
                sp.dma_start(raw[:, s], io["w2"][bass.ds(i, 1)].rearrange("a p k n -> (a p) k n")).then_inc(raw_in[s], 16)

            def free(g, n):
                sp.wait_ge(S["lo_done"], g * SLABS + n - 1)
                sp.wait_ge(S["const_in"], 16 * 5)

            def tokens(g):
                tok = bass.ds(g * TG, TG)
                sp.dma_start(mixr[:], io["mixT"][:, :, tok].rearrange("t p n -> p t n")).then_inc(S["mix_in"], 16)
                sp.dma_start(xres[:], io["xT"][bass.ds(g, 1)].rearrange("a p k n -> (a p) k n")).then_inc(S["x_in"], 16)

            tokens(0)
            for s in range(2):
                slab8(s, s)
            row = lambda a: bass.AP(tensor=io[a].tensor, offset=0, ap=[[0, TOK], [1, D]])
            for dst, src in ((ident[:], io["c_ident"]), (gb1[:, 0], io["g1"]), (gb1[:, 1], io["b1"]), (g2b[:], row("g2")), (b2b[:], row("b2"))):
                sp.dma_start(dst, src).then_inc(S["const_in"], 16)
            with sp.Fori(0, NG) as g:
                with sp.Fori(1, U1) as u:
                    for s in range(2):
                        free(g, 2 * u + s)
                        slab8(2 * u + s, s)
                sp.wait_ge(S["mix_split"], g + 1)
                sp.wait_ge(S["evac"], g * TILES + 8 + BANKS)
                sp.wait_ge(S["const_in"], 16 * 5)
                tokens((g + 1) % NG)
                with sp.Fori(0, 8) as u:
                    for s in range(2):
                        free(g, 2 * U1 + 2 * u + s)
                        slab11(2 * u + s, s)
                for s in range(2):
                    free(g, SLABS + s)
                    slab8(s, s)

        @block.gpsimd
        def _(pool):
            def rest(g, n, s, k):
                pool.wait_ge(S["hi_done"], g * SLABS + n + 1)
                nc.gpsimd.tensor_tensor(wlo[:, s, 0:k], raw[:, s, 0:k], whi[:, s, 0:k].bitcast(F32), ALU.subtract).then_inc(S["lo_done"], 1)

            for s in range(2):
                rest(0, s, s, KD)
            with pool.Fori(0, NG) as g:
                with pool.Fori(1, U1) as u:
                    for s in range(2):
                        rest(g, 2 * u + s, s, KD)
                with pool.Fori(U1, UNITS) as u:
                    for s in range(2):
                        rest(g, 2 * u + s, s, HALF)
                for s in range(2):
                    rest(g, SLABS + s, s, KD)

        @block.scalar
        def _(act):
            def rounded(g, u, k):
                for s in range(2):
                    act.wait_ge(raw_in[s], (g * UNITS + u) * 16 + 16)
                    act.wait_ge(S["slab_done"], g * SLABS + 2 * u + s + 1)
                    act.wait_ge(S["const_in"], 16 * 5)
                    nc.scalar.activation(whi[:, s, 0:k], raw[:, s, 0:k], ACT.Copy).then_inc(S["hi_done"], 1)

            def roots(g, first):
                for i in range(NTT):
                    act.wait_ge(S["root_arg"], g * 2 * NTT + first + i + 1)
                    act.wait_ge(S["const_in"], 16 * 5)
                    nc.scalar.activation(rstd[:, 0:1], rstd[:, 0:1], ACT.Sqrt).then_inc(S["root_done"], 1)
                    if first:
                        act.wait_ge(S["y_ready"], g * NTT + i + 1)
                        act.dma_start(io["y"][bass.ds(g * TG + i * TOK, TOK), :], nrm[:, i % 2]).then_inc(y_out[i % 2], 16)

            def gated(g, j, s):
                act.wait_ge(S["slab_done"], g * SLABS + 8 + 2 * j + 3)
                act.wait_ge(S["h_split"], g * KF + j + 1)
                act.wait_ge(S["const_in"], 16 * 5)
                nc.scalar.activation(silu[:, s], acc[:, 2 * s, 0:TG], ACT.Silu).then_inc(S["silu_done"], 1)

            for s in range(2):
                act.sem_inc(y_out[s], 16)
            act.wait_ge(S["const_in"], 16 * 5)
            for s in range(2):
                act.wait_ge(raw_in[s], 16)
                nc.scalar.activation(whi[:, s, 0:KD], raw[:, s, 0:KD], ACT.Copy).then_inc(S["hi_done"], 1)
            with act.Fori(0, NG) as g:
                with act.Fori(1, 5) as u:
                    rounded(g, u, KD)
                roots(g, 0)
                with act.Fori(0, HALF - 1) as i:
                    for s in range(2):
                        rounded(g, 2 * i + s + 5, KD)
                        gated(g, 2 * i + s, s)
                rounded(g, U1 - 1, KD)
                gated(g, KF - 2, 0)
                rounded(g, U1, HALF)
                gated(g, KF - 1, 1)
                with act.Fori(U1 + 1, UNITS) as u:
                    rounded(g, u, HALF)
                rounded(g, UNITS, KD)
                roots(g, NTT)
            for s in range(2):
                act.wait_ge(y_out[s], 16 + 16 * NG * NTT // 2)

        @block.tensor
        def _(pe):
            def turn(g, i):
                for k in range(KD):
                    last = pe.transpose(turned[0:TOK, k // 4, (k % 4) * P:(k % 4) * P + P],
                                        res[:, k, i * TOK:i * TOK + TOK], ident[:])
                last.then_inc(S["ta_full"], 1)

            def run_slab(g, base, off, s, bank, hx, lx, k0, k, total):
                pe.wait_ge(S["lo_done"], g * SLABS + base + off + 1)
                for c in range(k):
                    a = k0 + c
                    pe.matmul(acc[:, bank, 0:TG], whi[:, s, c], hx[:, a], start=(a == 0), stop=False)
                    pe.matmul(acc[:, bank, 0:TG], whi[:, s, c], lx[:, a], start=False, stop=False)
                    last = pe.matmul(acc[:, bank, 0:TG], wlo[:, s, c], hx[:, a], start=False, stop=(a == total - 1))
                last.then_inc(S["slab_done"], 1)

            pe.sem_inc(S["slab_done"], 2)
            pe.wait_ge(S["const_in"], 16 * 5)
            with pe.Fori(0, NG) as g:
                pe.wait_ge(S["mix_split"], g + 1)
                apart(pe)
                with pe.Fori(0, 2) as q:
                    for b in range(BANKS):
                        pe.wait_ge(S["evac"], g * TILES + q * BANKS + b + 1)
                        run_slab(g, 4 * q, b, b % 2, b, ah, al, 0, KD, KD)
                pe.wait_ge(S["evac"], g * TILES + 8 + BANKS)
                turn(g, 0)
                for i in range(NTT):
                    pe.wait_ge(S["normed"], g * 2 * NTT + i + 1)
                    if i < NTT - 1:
                        turn(g, i + 1)
                    pe.wait_ge(S["x1_split"], g * NTT + i + 1)
                    for k in range(KD):
                        last = pe.transpose(back[:, k // 4, (k % 4) * TOK:(k % 4) * TOK + TOK],
                                            nrm[:, i % 2, k * P:k * P + P], ident[0:TOK, 0:TOK])
                    last.then_inc(S["tb_full"], 1)
                pe.wait_ge(S["x1_split"], g * NTT + NTT + 1)
                apart(pe)
                with pe.Fori(0, HALF) as q:
                    for b in range(BANKS):
                        pe.wait_ge(S["evac"], g * TILES + 8 + q * BANKS + b + 1)
                        run_slab(g, 8 + 4 * q, b, b % 2, b, ah, al, 0, KD, KD)
                pe.wait_ge(S["h_split"], g * KF + KF + 2)
                apart(pe)
                with pe.Fori(0, 2) as q:
                    for b in range(BANKS):
                        pe.wait_ge(S["evac"], g * TILES + 8 + 2 * KF + q * BANKS + b + 1)
                        for s in range(2):
                            run_slab(g, 2 * U1 + 8 * q, 2 * b + s, s, b, hh, hl, s * HALF, HALF, KF)
                pe.wait_ge(S["evac"], g * TILES + TILES + BANKS)
                for i in range(NTT):
                    pe.wait_ge(S["normed"], g * 2 * NTT + NTT + i)
                    turn(g, i)

        @block.vector
        def _(dve):
            dve.sem_inc(S["evac"], BANKS)
            dve.sem_inc(S["x1_split"], 1)
            dve.sem_inc(S["h_split"], 2)
            dve.wait_ge(S["const_in"], 16 * 5)

            def split_mix(turn):
                nc.vector.tensor_copy(ah[:], mixr[:]).then_inc(S["mix_hi"], 1)
                dve.wait_ge(S["mix_hi"], turn + 1)
                nc.vector.tensor_tensor(al[:], mixr[:], ah[:].bitcast(F32), ALU.subtract).then_inc(S["mix_split"], 1)

            def normed(v, g, i, base):
                dve.wait_ge(S["ta_full"], g * 2 * NTT + base + i + 1)
                for b in range(2):
                    last = nc.vector.bn_stats(stats[:, b], turned[0:TOK, b])
                v(last)
                apart(dve)
                v(nc.vector.bn_aggr(mv[:], stats[:].rearrange("p a b -> p (a b)")))
                nc.vector.tensor_scalar(rstd[:, 0:1], mv[:, 1:2], LN_EPS, None, ALU.add).then_inc(S["root_arg"], 1)
                dve.wait_ge(S["root_done"], g * 2 * NTT + base + i + 1)
                v(nc.vector.reciprocal(rstd[:, 1:2], rstd[:, 0:1]))
                dve.wait_ge(y_out[i % 2], 16 * (g * (NTT // 2) + (i // 2 if base else 0) + 1))
                nc.vector.tensor_scalar(nrm[:, i % 2], turned_tok, mv[:, 0:1], rstd[:, 1:2],
                                        ALU.subtract, ALU.mult).then_inc(S["normed"], 1)

            def split(v, g, i):
                t = slice(i * TOK, i * TOK + TOK)
                dve.wait_ge(S["tb_full"], g * NTT + i + 1)
                for b in range(2):
                    last = nc.vector.tensor_tensor(
                        res[:, 4 * b:4 * b + 4, t], back[:, b, 0:4 * TOK].rearrange("p (k t) -> p k t", t=TOK),
                        gb1[:, 0, 4 * b:4 * b + 4].unsqueeze(2).broadcast_to([P, 4, TOK]), ALU.mult)
                v(last)
                v(nc.vector.tensor_tensor(res[:, :, t], res[:, :, t], gb1[:, 1].unsqueeze(2).broadcast_to([P, KD, TOK]), ALU.add))
                v(nc.vector.tensor_copy(ah[:, :, t], res[:, :, t]))
                nc.vector.tensor_tensor(al[:, :, t], res[:, :, t], ah[:, :, t].bitcast(F32), ALU.subtract).then_inc(S["x1_split"], 1)

            dve.wait_ge(S["mix_in"], 16)
            split_mix(0)
            with dve.Fori(0, NG) as g:
                v = Steps(dve, dve_s, g, DVE_STEPS)
                dve.wait_ge(S["x_in"], g * 16 + 16)
                apart(dve)
                with dve.Fori(0, 2) as q:
                    for b in range(BANKS):
                        dve.wait_ge(S["slab_done"], g * SLABS + q * BANKS + b + 3)
                        k = bass.ds(q * BANKS + b, 1)
                        nc.vector.scalar_tensor_tensor(res[:, k], xres[:, k], ALPHA, acc[:, b:b + 1, 0:TG],
                                                       ALU.mult, ALU.add).then_inc(S["evac"], 1)
                for i in range(NTT):
                    normed(v, g, i, 0)
                    if i:
                        split(v, g, i - 1)
                split(v, g, NTT - 1)
                with dve.Fori(0, HALF) as q:
                    for s in range(2):
                        j = 2 * q + s
                        dve.wait_ge(S["silu_done"], g * KF + j + 1)
                        dve.wait_ge(S["slab_done"], g * SLABS + 8 + 2 * j + 4)
                        dve.wait_ge(S["h_split"], g * KF + j + 2)
                        nc.vector.tensor_tensor(hbuf[:], silu[:, s], acc[:, 2 * s + 1, 0:TG], ALU.mult).then_inc(S["evac"], 2)
                        dve.wait_ge(S["evac"], g * TILES + 8 + 2 * j + 2 + BANKS)
                        nc.vector.tensor_copy(hh[:, bass.ds(j, 1)], hbuf[:].unsqueeze(1)).then_inc(S["h_hi"], 1)
                        dve.wait_ge(S["h_hi"], g * KF + j + 1)
                        nc.vector.tensor_tensor(hl[:, bass.ds(j, 1)], hbuf[:].unsqueeze(1), hh[:, bass.ds(j, 1)].bitcast(F32),
                                                ALU.subtract).then_inc(S["h_split"], 1)
                dve.wait_ge(S["mix_in"], g * 16 + 32)
                dve.wait_ge(S["slab_done"], g * SLABS + 2 * U1 + 2)
                split_mix(g + 1)
                with dve.Fori(0, 2) as q:
                    for b in range(BANKS):
                        dve.wait_ge(S["slab_done"], g * SLABS + 2 * U1 + q * 8 + 2 * b + 4)
                        k = bass.ds(q * BANKS + b, 1)
                        nc.vector.scalar_tensor_tensor(res[:, k], res[:, k], ALPHA, acc[:, b:b + 1, 0:TG],
                                                       ALU.mult, ALU.add).then_inc(S["evac"], 1)
                for i in range(NTT):
                    normed(v, g, i, NTT)
                    dve.wait_ge(S["normed"], g * 2 * NTT + NTT + i + 1)
                    v(nc.vector.tensor_tensor(nrm[:, i % 2], nrm[:, i % 2], g2b[:], ALU.mult))
                    nc.vector.tensor_tensor(nrm[:, i % 2], nrm[:, i % 2], b2b[:], ALU.add).then_inc(S["y_ready"], 1)
                v.end()


def bass_hymba_step(nc, io):
    io["projT"] = nc.dram_tensor("projT", [NPROJ, P, NT], F32, kind="Internal").ap()
    io["gateT"] = nc.dram_tensor("gateT", [8, NT], F32, kind="Internal").ap()
    io["xsT"] = nc.dram_tensor("xsT", [H, 2, NT], F32, kind="Internal").ap()
    io["ext"] = nc.dram_tensor("ext", [8, HJ], F32, kind="Internal").ap()
    io["mixT"] = nc.dram_tensor("mixT", [8, P, NT], F32, kind="Internal").ap()
    project(nc, io)
    with ExitStack() as ctx:
        m = Store(nc, ctx)
        keep = {
            "ident": m.sb("ident", [P, P]),
            "cols": m.sb("cols", [P, NC + 1, 64]),
            "bias": m.sb("bias", [P, 8, 2 * W]),
            "bias_prev": m.sb("bias_prev", [P, 8, W]),
            "sbias": m.sb("sbias", [P, 2, P + NS]),
            "ident_in": m.sem("ident_in"),
        }
        with nc.Block() as block:
            @block.sync
            def _(sp):
                sp.dma_start(keep["ident"][:], io["c_ident"]).then_inc(keep["ident_in"], 16)
                sp.wait_ge(keep["ident_in"], 16)
        gates(nc, io, keep)
        prompt(nc, io, keep)
        sample(nc, io, keep)
    layer(nc, io)


def constants():
    eye = np.eye(P, dtype=np.float32)
    dist = 255 - np.arange(HJ)
    n = np.maximum(dist, 1).astype(np.float32)
    large = 16 + (np.log(n / np.float32(16)) / np.float32(np.log(8.0)) * np.float32(16)).astype(np.int32)
    bucket = np.where(dist < 16, np.maximum(dist, 0), np.minimum(large, 31))
    seen = (dist >= 0) & (dist < W)
    onehot = ((np.arange(32)[:, None] == bucket) & seen).astype(np.float32)
    row = np.arange(P)
    seq = np.arange(NS) // DT
    smask = np.stack([np.where(half * 4 + row[:, None] // 32 == seq, 0.0, NEG) for half in range(2)], 1)
    s, t = np.arange(C)[:, None], np.arange(C)
    ds, dt = np.arange(NS)[:, None], np.arange(NS)
    return {
        "c_ident": eye, "c_anti": eye[::-1], "c_onehot": onehot,
        "c_outside": np.tile(np.where(seen, 0.0, NEG), (8, 1)),
        "c_repl": (np.arange(32)[:, None] == row % 32).astype(np.float32),
        "c_smask": smask,
        "c_causal": np.where(s <= t, 0.0, NEG),
        "c_causal_s": np.where((ds <= dt) & (ds // DT == dt // DT), 0.0, NEG),
    }


def w_in_order():
    base = 2056
    sq = [base + (g * J + j) * 64 + d for j in range(J) for g in range(2) for d in range(64)]
    return np.array([*range(2048), *sq, *range(base + 512, base + 768)]), np.arange(2048, 2056)


def layout(a):
    f = lambda k: np.asarray(a[k], np.float32)
    cols, gates = w_in_order()
    slabs = lambda w, k: np.ascontiguousarray(w.reshape(k, P, w.shape[1] // P, P).transpose(2, 1, 0, 3))
    x = np.concatenate([f("x_prompt").reshape(SEQ, D), f("x_sample").reshape(NS, D)])
    w = f("w_in")[0]
    out = {
        "xT": np.ascontiguousarray(x.reshape(NG, TG, KD, P).transpose(0, 3, 2, 1)),
        "wA": slabs(w[:, cols], KD),
        "wG": np.ascontiguousarray(w[:, gates].reshape(KD, P, 8).transpose(1, 0, 2)),
    }
    swa = [512 + (g * J + j) * 64 + d for j in range(J) for g in range(2) for d in range(64)]
    w1 = slabs(f("w_ffn_in")[0], KD)
    out.update({
        "wB": np.concatenate([slabs(f("w_out")[0][[*range(512), *swa]], KD), w1.reshape(2, KF, P, KD, P).swapaxes(0, 1).reshape(2 * KF, P, KD, P)]),
        "w2": f("w_ffn_out")[0].reshape(2, HALF, P, KD, P).transpose(3, 0, 2, 1, 4).reshape(2 * KD, P, HALF, P),
        "g1": f("ln1_g").reshape(KD, P).T, "b1": f("ln1_b").reshape(KD, P).T, "g2": f("ln2_g"), "b2": f("ln2_b"),
    })
    out.update({
        "b_ig": f("b_igate").reshape(H, 1), "b_fg": f("b_fgate").reshape(H, 1),
        "m0": f("state_mlstm_m")[0].T, "rel_bias": f("rel_bias"),
    })
    heads = [g * J + j for j in range(J) for g in range(2)]
    sinks = f("swa_sinks")[0]
    out.update({
        "sinks": sinks[heads].reshape(1, 8),
        "sink_col": np.broadcast_to(sinks.reshape(1, 2, 1, J), (4, 2, DT, J)).reshape(P, 1),
        "g_ml": f("ml_norm_g").reshape(H, P).T,
        "state_C": f("state_mlstm_C")[0].reshape(DB * H, P, P).transpose(1, 0, 2),
        "n0": f("state_mlstm_n")[0].reshape(DB * H, P).T,
        "cache_kT": f("cache_swa_k")[0].reshape(DB, W, P).transpose(2, 0, 1),
        "cache_k": f("cache_swa_k")[0].reshape(DB, W, P),
        "cache_v": f("cache_swa_v")[0].reshape(DB, W, P),
    })
    out.update(constants())
    return {k: np.ascontiguousarray(v, dtype=np.float32) for k, v in out.items()}


OUTS = {
    "y": [NT, D],
    "p_C": [P, H, P], "p_n": [P, H], "p_m": [H, 1], "p_k": [P, W], "p_v": [P, W],
    "s_C": [P, DB * H, P], "s_n": [P, DB * H], "s_m": [H, DB], "s_k": [DB, W, P], "s_v": [DB, W, P],
}


def kernel(**inputs):
    import concourse.bacc as bacc
    from concourse.bass_utils import run_bass_kernel_spmd

    nc = bacc.Bacc("TRN2", target_bir_lowering=False, num_devices=1)
    arrays = layout(inputs)
    io = {n: nc.dram_tensor("in_" + n, a.shape, F32, kind="ExternalInput").ap() for n, a in arrays.items()}
    io.update({n: nc.dram_tensor("out_" + n, s, F32, kind="ExternalOutput").ap() for n, s in OUTS.items()})
    bass_hymba_step(nc, io)
    r = run_bass_kernel_spmd(nc, [{"in_" + n: a for n, a in arrays.items()}], core_ids=[0]).results[0]
    o = {n: r["out_" + n] for n in OUTS}
    one = lambda x: np.ascontiguousarray(x)[None]
    feature = lambda x: x.T.reshape(1, W, 2, 64)
    return (
        one(o["y"][0:SEQ]), np.ascontiguousarray(o["y"][SEQ:NT]).reshape(DB, DT, D),
        one(o["p_C"].transpose(1, 0, 2)[None]), one(o["p_n"].T[None]), one(o["p_m"].T), one(feature(o["p_k"])), one(feature(o["p_v"])),
        one(o["s_C"].transpose(1, 0, 2).reshape(DB, H, P, P)), one(o["s_n"].T.reshape(DB, H, P)), one(o["s_m"].T),
        one(o["s_k"].reshape(DB, W, 2, 64)), one(o["s_v"].reshape(DB, W, 2, 64)),
    )
```

```python
from contextlib import ExitStack

import numpy as np

import concourse.bass as bass
from concourse import mybir

F32 = mybir.dt.float32
F32R = mybir.dt.float32r
ALU = mybir.AluOpType
ACT = mybir.ActivationFunctionType
AX = mybir.AxisListType

P = 128
D = 1024
KD = D // P
SEQ = 2048
DB, DT = 8, 4
NS = DB * DT
NT = SEQ + NS
NG = 5
TG = NT // NG
TOK = 104
NTT = TG // TOK
H = 4
C = 128
NC = SEQ // C
J = 4
W = 128
PAST = 128
FF = 2816
KF = FF // P
HALF = KF // 2
NPROJ = 22
MQ, MK, MV, MO, SQ, SK, SV = 0, 4, 8, 12, 16, 20, 21
QD, KD_SWA = H * P, 64
ML_SCALE = float(P) ** -0.5
SWA_SCALE = 64.0 ** -0.5
ALPHA = 2.0 ** 0.25
LN_EPS = 1e-5
NORM_EPS = 1e-6
CAP = 15.0
NEG = -1e30
HJ = 384
assert NG * TG == NT and NTT * TOK == TG



class Steps:

    def __init__(self, eng, sem, turn=0, each=0):
        self.eng, self.sem, self.turn, self.each, self.k = eng, sem, turn, each, 0

    def __call__(self, ins):
        self.k += 1
        ins.then_inc(self.sem, 1)
        self.eng.wait_ge(self.sem, self.turn * self.each + self.k)

    def end(self):
        assert self.k == self.each, (self.sem, self.k)


class Store:

    def __init__(self, nc, ctx):
        self.nc, self.ctx = nc, ctx

    def sb(self, name, shape, dt=F32):
        return self.ctx.enter_context(self.nc.sbuf_tensor(name, shape, dt))

    def ps(self, name, shape):
        return self.ctx.enter_context(self.nc.psum_tensor(name, shape, F32))

    def sem(self, name):
        return self.nc.alloc_semaphore(name)


def project(nc, io):
    with ExitStack() as ctx:
        m = Store(nc, ctx)
        xh = m.sb("xh", [P, KD, NT], F32R)
        xl = m.sb("xl", [P, KD, NT], F32R)
        xraw = m.sb("xraw", [P, KD, TG])
        raw = m.sb("raw", [P, 2, KD, P])
        whi = m.sb("whi", [P, 2, KD, P], F32R)
        wlo = m.sb("wlo", [P, 2, KD, P], F32R)
        ghi = m.sb("ghi", [P, KD, P], F32R)
        glo = m.sb("glo", [P, KD, P], F32R)
        out = m.sb("out", [P, 2, NT])
        grow = m.sb("grow", [8, NT])
        acc = [m.ps(f"acc{i}", [P, 512]) for i in range(2)]
        x_in = m.sem("p_x_in")
        x_hi = m.sem("p_x_hi")
        x_split = m.sem("p_x_split")
        g_zero = m.sem("p_g_zero")
        g_in = m.sem("p_g_in")
        g_hi = m.sem("p_g_hi")
        g_split = m.sem("p_g_split")
        raw_in = [m.sem(f"p_raw_in{s}") for s in range(2)]
        hi_done = [m.sem(f"p_hi{s}") for s in range(2)]
        lo_done = [m.sem(f"p_lo{s}") for s in range(2)]
        acc_full = m.sem("p_acc_full")
        acc_free = m.sem("p_acc_free")
        out_free = [m.sem(f"p_out_free{s}") for s in range(2)]
        g_stored = m.sem("p_g_stored")
        ITER = NPROJ // 2
        block = ctx.enter_context(nc.Block())

        @block.sync
        def _(sp):
            def load(i, s):
                sp.dma_start(raw[:, s], io["wA"][bass.ds(i * 2 + s, 1)].rearrange("a p k n -> (a p) k n")).then_inc(raw_in[s], 16)

            def store(i, s):
                sp.wait_ge(acc_free, (i * 2 + s + 2) * NG)
                sp.wait_ge(g_in, 16)
                sp.dma_start(io["projT"][bass.ds(i * 2 + s, 1)].rearrange("a p n -> (a p) n"),
                             out[:, s]).then_inc(out_free[s], 16)

            sp.wait_ge(g_zero, 1)
            sp.dma_start(raw[:, 0, :, 0:8], io["wG"]).then_inc(g_in, 16)
            sp.dma_start(xraw[:], io["xT"][0]).then_inc(x_in, 16)
            sp.wait_ge(g_split, 1)
            for s in range(2):
                load(0, s)
            with sp.Fori(1, NG) as g:
                sp.wait_ge(x_split, g)
                sp.wait_ge(g_in, 16)
                sp.dma_start(xraw[:], io["xT"][bass.ds(g, 1)].rearrange("a p k n -> (a p) k n")).then_inc(x_in, 16)
            with sp.Fori(1, ITER) as i:
                for s in range(2):
                    sp.wait_ge(lo_done[s], i)
                    sp.wait_ge(g_in, 16)
                    load(i, s)
                for s in range(2):
                    store(i - 1, s)
            for s in range(2):
                store(ITER - 1, s)
            sp.wait_ge(acc_free, NG)
            sp.dma_start(io["gateT"], grow[:]).then_inc(g_stored, 16)
            sp.wait_ge(g_stored, 16)
            for s in range(2):
                sp.wait_ge(out_free[s], 16 * (ITER + 1))

        @block.scalar
        def _(act):
            act.wait_ge(g_in, 16)
            nc.scalar.activation(ghi[:], raw[:, 0], ACT.Copy).then_inc(g_hi, 1)
            with act.Fori(0, NG) as g:
                act.wait_ge(x_in, g * 16 + 16)
                act.wait_ge(g_in, 16)
                nc.scalar.activation(xh[:, :, bass.ds(g * TG, TG)], xraw[:], ACT.Copy).then_inc(x_hi, 1)
            for s in range(2):
                act.wait_ge(raw_in[s], 16)
                nc.scalar.activation(whi[:, s], raw[:, s], ACT.Copy).then_inc(hi_done[s], 1)
            with act.Fori(1, ITER) as i:
                for s in range(2):
                    act.wait_ge(raw_in[s], i * 16 + 16)
                    act.wait_ge(acc_full, (i * 2 + s) * NG)
                    act.wait_ge(g_in, 16)
                    nc.scalar.activation(whi[:, s], raw[:, s], ACT.Copy).then_inc(hi_done[s], 1)

        @block.gpsimd
        def _(pool):
            nc.gpsimd.memset(raw[:, 0], 0.0).then_inc(g_zero, 1)
            pool.wait_ge(g_hi, 1)
            nc.gpsimd.tensor_tensor(glo[:], raw[:, 0], ghi[:].bitcast(F32), ALU.subtract).then_inc(g_split, 1)
            with pool.Fori(0, ITER) as i:
                for s in range(2):
                    pool.wait_ge(hi_done[s], i + 1)
                    nc.gpsimd.tensor_tensor(wlo[:, s], raw[:, s], whi[:, s].bitcast(F32),
                                            ALU.subtract).then_inc(lo_done[s], 1)

        @block.tensor
        def _(pe):
            def product(bank, hi, lo, g):
                for k in range(KD):
                    xs = slice(g * TG, (g + 1) * TG)
                    pe.matmul(acc[bank][:, 0:TG], hi[:, k], xh[:, k, xs], start=(k == 0), stop=False)
                    pe.matmul(acc[bank][:, 0:TG], hi[:, k], xl[:, k, xs], start=False, stop=False)
                    last = pe.matmul(acc[bank][:, 0:TG], lo[:, k], xh[:, k, xs], start=False, stop=(k == KD - 1))
                return last

            pe.wait_ge(g_split, 1)
            for g in range(NG):
                pe.wait_ge(x_split, g + 1)
                if g >= 2:
                    pe.wait_ge(acc_free, g - 1)
                product(g % 2, ghi, glo, g).then_inc(acc_full, 1)
            with pe.Fori(0, ITER) as i:
                for s in range(2):
                    pe.wait_ge(lo_done[s], i + 1)
                    for g in range(NG):
                        n = s * NG + g
                        pe.wait_ge(acc_free, i * (2 * NG) + NG + n - 1)
                        product((n + NG) % 2, whi[:, s], wlo[:, s], g).then_inc(acc_full, 1)

        @block.vector
        def _(dve):
            for s in range(2):
                dve.sem_inc(out_free[s], 16)
            with dve.Fori(0, NG) as g:
                dve.wait_ge(x_hi, g + 1)
                xs = bass.ds(g * TG, TG)
                nc.vector.tensor_tensor(xl[:, :, xs], xraw[:], xh[:, :, xs].bitcast(F32),
                                        ALU.subtract).then_inc(x_split, 1)
            for g in range(NG):
                dve.wait_ge(acc_full, g + 1)
                nc.vector.tensor_copy(grow[:, g * TG:(g + 1) * TG], acc[g % 2][0:8, 0:TG]).then_inc(acc_free, 1)
            with dve.Fori(0, ITER) as i:
                for s in range(2):
                    dve.wait_ge(out_free[s], i * 16 + 16)
                    for g in range(NG):
                        n = s * NG + g
                        dve.wait_ge(acc_full, i * (2 * NG) + NG + n + 1)
                        nc.vector.tensor_copy(out[:, s, g * TG:(g + 1) * TG],
                                                     acc[(n + NG) % 2][:, 0:TG]).then_inc(acc_free, 1)


def gates(nc, io, keep):
    cols, bias, bias_prev, ident = keep["cols"], keep["bias"], keep["bias_prev"], keep["ident"]
    with ExitStack() as ctx:
        m = Store(nc, ctx)
        gi = m.sb("gi", [H, NT])
        gf = m.sb("gf", [H, NT])
        b = m.sb("b", [H, NT])
        run = m.sb("run", [H, NT])
        xs = m.sb("xs", [H, 2, NT])
        ue = m.sb("ue", [64, NT])
        start = m.sb("start", [H, SEQ])
        small = m.sb("small", [H, 32])
        m0 = m.sb("m0_sb", [H, DB])
        m_last = m.sb("m_last", [H, DB])
        mprev = m.sb("mprev", [H, NC])
        relb = m.sb("relb", [32, 8])
        onehot = m.sb("onehot", [32, HJ])
        outside = m.sb("outside", [8, HJ])
        ext = m.sb("ext_sb", [8, HJ])
        anti = m.sb("anti", [P, P])
        hank = m.sb("hank", [P, 8, 2 * W])
        srow = m.sb("srow", [32, 132])
        repl = m.sb("repl", [32, P])
        srow_all = m.sb("srow_all", [P, 132])
        smask = m.sb("smask", [P, 2, NS])
        ps = m.ps("ps", [P, 4, 512])
        pt = m.ps("pt", [P, 3, 512])
        loaded = m.sem("g_loaded")
        dve_s, act_s, pe_s, pool_s = m.sem("g_dve"), m.sem("g_act"), m.sem("g_pe"), m.sem("g_pool")
        stored = m.sem("g_stored")
        ext_out = m.sem("g_ext_out")
        ext_in = m.sem("g_ext_in")
        block = ctx.enter_context(nc.Block())
        EXT, CAPPED_BIAS, ONE_MORE, MAXIMA, EXPONENTS, U, TURNED = 2, 4, 5, 21, 26, 27, 30
        SIGMOIDS, LOGS, EXP_M, SCALES = 3, 4, 5, 7

        @block.sync
        def _(sp):
            for dst, src in ((relb[:], io["rel_bias"]), (onehot[:], io["c_onehot"]), (outside[:], io["c_outside"]),
                             (gi[:], io["gateT"][0:H]), (gf[:], io["gateT"][H:2 * H]),
                             (small[:, 0:1], io["b_ig"]), (small[:, 1:2], io["b_fg"]), (m0[:], io["m0"]),
                             (anti[:], io["c_anti"]), (repl[:], io["c_repl"]), (smask[:], io["c_smask"])):
                sp.dma_start(dst, src).then_inc(loaded, 16)
            sp.wait_ge(dve_s, EXT)
            sp.dma_start(io["ext"], ext[:]).then_inc(ext_out, 16)
            sp.wait_ge(ext_out, 16)
            e = io["ext"].tensor
            sp.dma_start(hank[:], bass.AP(tensor=e, offset=0, ap=[[1, P], [HJ, 8], [1, 2 * W]])).then_inc(ext_in, 16)
            for g in range(2):
                for t in range(DT):
                    sp.dma_start(srow[g * 16 + t * J:g * 16 + t * J + J, :],
                                 bass.AP(tensor=e, offset=g * J * HJ + 127 - t, ap=[[HJ, J], [1, 132]])).then_inc(ext_in, 16)
            sp.wait_ge(act_s, SCALES)
            sp.dma_start(io["xsT"], xs[:]).then_inc(stored, 16)
            sp.dma_start(io["p_m"], run[:, SEQ - 1:SEQ]).then_inc(stored, 16)
            sp.dma_start(io["s_m"], m_last[:]).then_inc(stored, 16)
            sp.wait_ge(stored, 48)

        @block.gpsimd
        def _(pool):
            nc.gpsimd.memset(ue[:], 0.0).then_inc(pool_s, 1)
            nc.gpsimd.memset(start[:], 1.0).then_inc(pool_s, 1)
            pool.wait_ge(pool_s, 2)
            nc.gpsimd.memset(start[:, 0:SEQ:C], 0.0).then_inc(pool_s, 1)
            nc.gpsimd.memset(mprev[:], 0.0).then_inc(pool_s, 1)

        @block.scalar
        def _(act):
            a = Steps(act, act_s)
            act.wait_ge(dve_s, CAPPED_BIAS)
            a(nc.scalar.activation(gi[:], gi[:], ACT.Tanh, scale=1 / CAP, bias=small[:, 2:3]))
            a(nc.scalar.activation(gf[:], gf[:], ACT.Tanh, scale=1 / CAP, bias=small[:, 3:4]))
            a(nc.scalar.activation(gf[:], gf[:], ACT.Exp, scale=-CAP))
            act.wait_ge(dve_s, ONE_MORE)
            a(nc.scalar.activation(gf[:], gf[:], ACT.Ln))
            act.wait_ge(dve_s, MAXIMA)
            a(nc.scalar.activation(ue[32:32 + H], run[:], ACT.Exp, scale=-1.0))
            act.wait_ge(dve_s, EXPONENTS)
            a(nc.scalar.activation(xs[:, 1, 0:SEQ], xs[:, 1, 0:SEQ], ACT.Exp))
            a(nc.scalar.activation(xs[:, 1, SEQ:NT], xs[:, 1, SEQ:NT], ACT.Exp))

        @block.vector
        def _(dve):
            v = Steps(dve, dve_s)
            dve.wait_ge(loaded, 16 * 11)
            dve.wait_ge(pe_s, 1)
            v(nc.vector.tensor_copy(ext[:], ps[0:8, 0, 0:HJ]))
            v(nc.vector.tensor_tensor(ext[:], ext[:], outside[:], ALU.add))
            v(nc.vector.tensor_scalar(small[:, 2:3], small[:, 0:1], 1 / CAP, None, ALU.mult))
            v(nc.vector.tensor_scalar(small[:, 3:4], small[:, 1:2], 1 / CAP, None, ALU.mult))
            dve.wait_ge(act_s, SIGMOIDS)
            v(nc.vector.tensor_scalar(gf[:], gf[:], 1.0, None, ALU.add))
            dve.wait_ge(act_s, LOGS)
            v(nc.vector.tensor_scalar(gf[:], gf[:], -1.0, None, ALU.mult))
            v(nc.vector.tensor_scalar(gi[:], gi[:], CAP, None, ALU.mult))
            dve.wait_ge(pool_s, 4)
            v(nc.vector.tensor_tensor_scan(b[:, 0:SEQ], start[:], gf[:, 0:SEQ], 0.0, ALU.mult, ALU.add))
            v(nc.vector.tensor_tensor_scan(run[:, 0:SEQ], gf[:, 0:SEQ], gi[:, 0:SEQ], 0.0, ALU.add, ALU.max))
            at = lambda r, t: r[:, SEQ + t:NT:DT]
            v(nc.vector.tensor_copy(at(b, 0), at(gf, 0)))
            for t in range(1, DT):
                v(nc.vector.tensor_tensor(at(b, t), at(b, t - 1), at(gf, t), ALU.add))
            for t in range(DT):
                v(nc.vector.tensor_tensor(at(run, t), m0[:] if t == 0 else at(run, t - 1), at(gf, t), ALU.add))
                if t < DT - 1:
                    v(nc.vector.tensor_tensor(at(run, t), at(run, t), at(gi, t), ALU.max))
            v(nc.vector.tensor_tensor(at(run, DT - 1), at(run, DT - 1), at(gi, DT - 1), ALU.max))
            assert v.k == MAXIMA
            v(nc.vector.tensor_tensor(xs[:, 0], b[:], run[:], ALU.subtract))
            v(nc.vector.tensor_copy(m_last[:], at(run, DT - 1)))
            v(nc.vector.tensor_copy(mprev[:, 1:NC], run[:, C - 1:SEQ - 1:C]))
            v(nc.vector.tensor_tensor(xs[:, 1, 0:SEQ].rearrange("h (c t) -> h c t", t=C),
                                      xs[:, 0, 0:SEQ].rearrange("h (c t) -> h c t", t=C),
                                      mprev[:].unsqueeze(2).broadcast_to([H, NC, C]), ALU.add))
            v(nc.vector.tensor_tensor(xs[:, 1, SEQ:NT].rearrange("h (c t) -> h c t", t=DT),
                                      xs[:, 0, SEQ:NT].rearrange("h (c t) -> h c t", t=DT),
                                      m0[:].unsqueeze(2).broadcast_to([H, DB, DT]), ALU.add))
            v(nc.vector.tensor_tensor(ue[0:H], gi[:], b[:], ALU.subtract))
            assert v.k == U
            for i in range(3):
                dve.wait_ge(pe_s, 2 + i)
                n = min(8, NC + 1 - 8 * i)
                rows = P if i < 2 else NS
                v(nc.vector.tensor_copy(cols[0:rows, 8 * i:8 * i + n], pt[0:rows, i, 0:n * 64].rearrange("p (c r) -> p c r", r=64)))
            assert v.k == TURNED
            for i in range(4):
                dve.wait_ge(pe_s, 5 + i)
                src = ps[:, i, :].rearrange("p (h k) -> p h k", k=2 * W)
                v(nc.vector.tensor_copy(bias_prev[:, 2 * i:2 * i + 2], src[:, :, 0:W]))
                v(nc.vector.tensor_copy(bias[:, 2 * i:2 * i + 2, W:2 * W], src[:, :, W:2 * W]))
            v(nc.vector.memset(bias[:, :, 0:W], NEG))
            dve.wait_ge(pe_s, 9)
            v(nc.vector.tensor_copy(srow_all[:], pt[:, 0, 0:132]))
            sb = keep["sbias"]
            v(nc.vector.tensor_copy(sb[:, :, 0:P], srow_all[:, 0:P].unsqueeze(1).broadcast_to([P, 2, P])))
            for half in range(2):
                v(nc.vector.tensor_tensor(sb[:, half, P:].rearrange("p (b t) -> p b t", t=DT),
                                          smask[:, half].rearrange("p (b t) -> p b t", t=DT),
                                          srow_all[:, P:132].unsqueeze(1).broadcast_to([P, DB, DT]), ALU.add))

        @block.tensor
        def _(pe):
            q = lambda ins: ins.then_inc(pe_s, 1)
            pe.wait_ge(loaded, 16 * 11)
            q(pe.matmul(ps[0:8, 0, 0:HJ], relb[:], onehot[:], start=True, stop=True))
            pe.wait_ge(act_s, EXP_M)
            pe.wait_ge(dve_s, U)
            pe.wait_ge(keep["ident_in"], 16)
            for i in range(3):
                for c in range(8 * i, min(8 * i + 8, NC + 1)):
                    n = C if c < NC else NS
                    last = pe.transpose(pt[0:n, i, (c - 8 * i) * 64:(c - 8 * i + 1) * 64],
                                        ue[:, c * C:c * C + n], ident[0:64, 0:64])
                q(last)
            pe.wait_ge(ext_in, 16 * 9)
            pe.wait_ge(dve_s, TURNED)
            for i in range(4):
                q(pe.matmul(ps[:, i, :], anti[:], hank[:, 2 * i:2 * i + 2, :], start=True, stop=True))
            q(pe.matmul(pt[:, 0, 0:132], repl[:], srow[:], start=True, stop=True))


def prompt(nc, io, keep):
    cols, bias, bias_prev, ident = keep["cols"], keep["bias"], keep["bias_prev"], keep["ident"]
    with ExitStack() as ctx:
        m = Store(nc, ctx)
        inp = m.sb("inp", [P, 2, 20, C])
        kwin = m.sb("kwin", [P, 2, 2 * W])
        svT = m.sb("svT", [P, 2, W])
        xs = m.sb("xs_b", [P, 2, H, 2, C])
        causal = m.sb("causal", [P, C])
        ones = m.sb("ones", [P, C])
        sinks = m.sb("sinks", [P, 8])
        gml = m.sb("gml", [P, H])
        expo = m.sb("expo", [P, H, C])
        decay = m.sb("decay", [P, H, C])
        qs = m.sb("qs", [P, H, C])
        prob = m.sb("prob", [P, H, C])
        kw = m.sb("kw", [P, H, P])
        vaug = m.sb("vaug", [P, H, P + 1])
        state = m.sb("state", [P, H, P + 1])
        nlast = m.sb("nlast", [P, H])
        den = m.sb("den", [P, H])
        ucol = m.sb("ucol", [P, 2, H])
        rec = m.sb("rec", [P, H])
        ssq = m.sb("ssq", [P, H])
        root = m.sb("root", [P, H])
        sqjunk = m.sb("sqjunk", [P, H, P])
        hn = m.sb("hn", [P, H, P])
        gate = m.sb("gate", [P, H, C])
        sq8 = m.sb("sq8", [P, J, C])
        vs = m.sb("vs", [P, 2, P])
        sw = m.sb("sw", [P, 2, 2, 2 * W])
        pw = m.sb("pw", [P, 2, 2, 2 * W])
        nmx = m.sb("nmx", [P, 8])
        mx = m.sb("mx", [P, 8])
        psums = m.sb("psums", [P, 2, 8])
        snk = m.sb("snk", [P, 8])
        ptw = m.sb("ptw", [P, 2, 4, W])
        ow = m.sb("ow", [P, 4, P])
        mix = m.sb("mixed", [P, 2, 8, C])
        m0, m3 = m.ps("m0b", [P, 512]), m.ps("m3b", [P, 512])
        m12 = m.ps("m12", [P, 2, 512])
        w01 = m.ps("w01", [P, 2, 512])
        w2, w3 = m.ps("w2b", [P, 512]), m.ps("w3b", [P, 512])
        heads_out = m12[:, :, 0:258].rearrange("p b (h e) -> p b h e", e=P + 1)

        const_in, zeroed, fence = m.sem("c_const"), m.sem("c_zeroed"), m.sem("c_fence")
        loaded = [m.sem(f"c_loaded{s}") for s in range(2)]
        names = ("k_turned v_turned scores sv_turned win out_ml state_up p_turned swa_out h_turned o_turned "
                 "e_ready qs_ready sv_ready nmx_ready p_ready kw_ready st_ready den_ready hn_ready ml_mixed "
                 "ow_ready msq_ready snk_arg sq_ready v_copied d_exp eo_ready p_exp pt_copied ssq_ready root_ready snk_exp "
                 "u_ready gate_sum gate_inv gate_ready bias_whole chunk_done").split()
        S = {n: m.sem("c_" + n) for n in names}
        each = dict.fromkeys(names, 1) | dict.fromkeys(("win", "p_turned", "nmx_ready", "p_exp", "pt_copied"), 4)
        dve_s = m.sem("c_dve")
        DVE_STEPS = 13
        AHEAD = 2
        mix_out = [m.sem(f"c_mix_out{s}") for s in range(2)]
        kv_out, st_out = m.sem("c_kv_out"), m.sem("c_st_out")

        def wait(eng, name, c, k=1):
            eng.wait_ge(S[name], c * each[name] + k + 1)

        block = ctx.enter_context(nc.Block())

        @block.sync
        def _(sp):
            def load(c, s):
                tok = bass.ds(c * C, C)
                sp.dma_start(inp[:, s], io["projT"][0:20, :, tok].rearrange("t p n -> p t n")).then_inc(loaded[s], 16)
                sp.dma_start(kwin[:, s], bass.AP(tensor=io["projT"].tensor, offset=SK * P * NT - W + c * C,
                                                 ap=[[NT, P], [1, 2 * W]])).then_inc(loaded[s], 16)
                sp.dma_start(svT[:, s], io["projT"][SV, :, tok]).then_inc(loaded[s], 16)
                sp.dma_start(xs[:, s].rearrange("p h w n -> p (h w) n"),
                             bass.AP(tensor=io["xsT"].tensor, offset=c * C, ap=[[0, P], [NT, 2 * H], [1, C]])).then_inc(loaded[s], 16)

            def store(c, s):
                sp.dma_start(io["mixT"][:, :, bass.ds(c * C, C)].rearrange("t p n -> p t n"), mix[:, s]).then_inc(mix_out[s], 16)

            for dst, src in ((causal[:], io["c_causal"]), (sinks[:], bass.AP(tensor=io["sinks"].tensor, offset=0, ap=[[0, P], [1, 8]])), (gml[:], io["g_ml"])):
                sp.dma_start(dst, src).then_inc(const_in, 16)
            for s in range(2):
                load(s, s)
            sp.dma_start(io["p_k"], io["projT"][SK, :, SEQ - W:SEQ]).then_inc(kv_out, 16)
            sp.dma_start(io["p_v"], io["projT"][SV, :, SEQ - W:SEQ]).then_inc(kv_out, 16)
            with sp.Fori(0, NC // 2 - 1) as i:
                for s in range(2):
                    wait(sp, "st_ready", 2 * i + s)
                    wait(sp, "eo_ready", 2 * i + s)
                    sp.wait_ge(const_in, 48)
                    load(2 * i + 2 + s, s)
                    wait(sp, "chunk_done", 2 * i + s)
                    sp.wait_ge(const_in, 48)
                    store(2 * i + s, s)
            for s in range(2):
                wait(sp, "chunk_done", NC - 2 + s)
                store(NC - 2 + s, s)
            sp.wait_ge(dve_s, NC * DVE_STEPS + AHEAD + 1)
            sp.dma_start(io["p_C"], state[:, :, 0:P]).then_inc(st_out, 16)
            sp.dma_start(io["p_n"], nlast[:]).then_inc(st_out, 16)
            sp.wait_ge(st_out, 32)
            sp.wait_ge(kv_out, 32)
            for s in range(2):
                sp.wait_ge(mix_out[s], 8 * NC + 16)

        @block.gpsimd
        def _(pool):
            nc.gpsimd.memset(state[:], 0.0).then_inc(zeroed, 1)
            nc.gpsimd.memset(vs[:], 0.0).then_inc(zeroed, 1)
            nc.gpsimd.memset(vaug[:], 1.0).then_inc(zeroed, 1)
            nc.gpsimd.memset(ones[:], 1.0).then_inc(zeroed, 1)
            for n in names:
                pool.sem_inc(S[n], 1)
            for s in range(2):
                pool.sem_inc(mix_out[s], 16)
            pool.wait_ge(const_in, 48)
            pool.wait_ge(zeroed, 4)

            def chunk(i, s):
                c = 2 * i + s
                pool.wait_ge(loaded[s], i * 64 + 64)
                wait(pool, "d_exp", c, 0)
                nc.gpsimd.tensor_tensor(expo[:], xs[:, s, :, 0], causal[:].unsqueeze(1).broadcast_to([P, H, C]),
                                        ALU.add).then_inc(S["e_ready"], 1)
                wait(pool, "out_ml", c, 0)
                nc.gpsimd.tensor_tensor(qs[:], inp[:, s, MQ:MQ + 4], xs[:, s, :, 1], ALU.mult).then_inc(S["qs_ready"], 1)
                wait(pool, "eo_ready", c)
                nc.gpsimd.tensor_tensor(gate[:], gate[:], ones[:].unsqueeze(1).broadcast_to([P, H, C]), ALU.add).then_inc(S["gate_sum"], 1)
                wait(pool, "gate_inv", c)
                nc.gpsimd.tensor_tensor(gate[:], gate[:], gml[:].unsqueeze(2).broadcast_to([P, H, C]),
                                        ALU.mult).then_inc(S["gate_ready"], 1)

            for s in range(2):
                chunk(0, s)
                if s == 0:
                    wait(pool, "nmx_ready", 0, 4)
                    nc.gpsimd.tensor_copy(bias[:, :, 0:W], bias_prev[:]).then_inc(S["bias_whole"], 1)
            with pool.Fori(1, NC // 2) as i:
                for s in range(2):
                    chunk(i, s)

        @block.tensor
        def _(pe):
            def window_scores(c, s, r):
                wait(pe, "nmx_ready", c, r)
                for g in range(2):
                    gp = slice(64 * g, 64 * g + 64)
                    for a in range(2):
                        last = pe.matmul(w01[:, g, a * 256:a * 256 + 256], sq8[gp, r + a], kwin[gp, s],
                                         start=True, stop=True)
                    last.then_inc(S["win"], 1)

            def turn_window(c, r, bank):
                wait(pe, "p_exp", c, r + 1)
                for g in range(2):
                    for half in range(2):
                        last = pe.transpose(bank[:, (2 * g + half) * W:(2 * g + half + 1) * W],
                                            pw[:, r % 2, g, half * W:half * W + W], ident[:])
                last.then_inc(S["p_turned"], 1)

            def window_values(c, s, r):
                wait(pe, "pt_copied", c, r + 1)
                for g in range(2):
                    for half in range(2):
                        last = pe.matmul(w3[:, r * P + g * 64:r * P + g * 64 + 64], ptw[:, r % 2, 2 * g + half],
                                         vs[:, s if half else 1 - s, g * 64:g * 64 + 64],
                                         start=(half == 0), stop=(half == 1))
                return last

            def turn_keys(c, s):
                for h in range(H):
                    last = pe.transpose(m0[:, h * C:h * C + C], inp[:, s, MK + h], ident[:])
                last.then_inc(S["k_turned"], 1)

            def chunk(i, s, more):
                c = 2 * i + s
                q, k, v = inp[:, s, MQ:MQ + 4], inp[:, s, MK:MK + 4], inp[:, s, MV:MV + 4]
                wait(pe, "hn_ready", c, 0)
                for h in range(H):
                    last = pe.transpose(m12[:, 0, h * C:h * C + C], v[:, h], ident[:])
                last.then_inc(S["v_turned"], 1)
                for h in range(H):
                    last = pe.matmul(m12[:, 1, h * C:h * C + C], k[:, h], q[:, h], start=True, stop=True)
                last.then_inc(S["scores"], 1)
                wait(pe, "ow_ready", c, 0)
                pe.transpose(w3[:, 0:P], svT[:, s], ident[:]).then_inc(S["sv_turned"], 1)
                wait(pe, "chunk_done", c, 0)
                turn_window(c, 0, w2)
                wait(pe, "ml_mixed", c, 0)
                turn_window(c, 1, m3)
                window_scores(c, s, 2)
                wait(pe, "p_ready", c)
                wait(pe, "v_copied", c)
                wait(pe, "qs_ready", c)
                for h in range(H):
                    pe.matmul(heads_out[:, h // 2, h % 2], prob[:, h], vaug[:, h], start=True, stop=False)
                    last = pe.matmul(heads_out[:, h // 2, h % 2], qs[:, h], state[:, h], start=False, stop=True)
                last.then_inc(S["out_ml"], 1)
                wait(pe, "kw_ready", c)
                wait(pe, "pt_copied", c, 2)
                for h in range(H):
                    last = pe.matmul((m3, m0)[h // 2][:, (h % 2) * 129:(h % 2) * 129 + 129], kw[:, h], vaug[:, h],
                                     start=True, stop=True)
                last.then_inc(S["state_up"], 1)
                wait(pe, "sv_ready", c)
                window_values(c, s, 0)
                turn_window(c, 2, w2)
                window_values(c, s, 1)
                wait(pe, "pt_copied", c, 3)
                turn_window(c, 3, w2)
                if more:
                    pe.wait_ge(loaded[1 - s], (i + s) * 64 + 64)
                    wait(pe, "sq_ready", c + 1)
                    window_scores(c + 1, 1 - s, 0)
                window_values(c, s, 2)
                window_values(c, s, 3).then_inc(S["swa_out"], 1)
                wait(pe, "st_ready", c)
                if more:
                    turn_keys(c + 1, 1 - s)
                wait(pe, "hn_ready", c)
                for h in range(H):
                    last = pe.transpose(m3[:, h * C:h * C + C], hn[:, h], ident[:])
                last.then_inc(S["h_turned"], 1)
                wait(pe, "ow_ready", c)
                for r in range(J):
                    last = pe.transpose(w2[:, r * C:r * C + C], ow[:, r], ident[:])
                last.then_inc(S["o_turned"], 1)

            pe.wait_ge(zeroed, 4)
            pe.wait_ge(loaded[0], 64)
            turn_keys(0, 0)
            wait(pe, "sq_ready", 0)
            window_scores(0, 0, 0)
            with pe.Fori(0, NC // 2 - 1) as i:
                for s in range(2):
                    chunk(i, s, True)
            for s in range(2):
                chunk(NC // 2 - 1, s, s == 0)

        @block.scalar
        def _(act):
            def window_exp(c, s, r):
                wait(act, "nmx_ready", c, r + 1)
                for g in range(2):
                    a = 2 * r + g
                    last = nc.scalar.activation(pw[:, r % 2, g], sw[:, r % 2, g], ACT.Exp, bias=nmx[:, a:a + 1],
                                                accum_out=psums[:, s, a:a + 1])
                last.then_inc(S["p_exp"], 1)

            def copy_turned(c, r):
                wait(act, "p_turned", c, r + 1)
                nc.scalar.activation(ptw[:, r % 2].rearrange("p a q -> p (a q)"), (m3 if r == 1 else w2)[:], ACT.Copy).then_inc(S["pt_copied"], 1)

            def scale_queries(s):
                nc.scalar.activation(sq8[:], inp[:, s, SQ:SQ + 4], ACT.Copy, scale=SWA_SCALE).then_inc(S["sq_ready"], 1)

            def chunk(i, s, more):
                c = 2 * i + s
                wait(act, "e_ready", c)
                wait(act, "u_ready", c)
                wait(act, "kw_ready", c, 0)
                for h in range(H):
                    last = nc.scalar.activation(decay[:, h], expo[:, h], ACT.Exp, bias=ucol[:, s, h:h + 1])
                last.then_inc(S["d_exp"], 1)
                wait(act, "v_turned", c)
                nc.scalar.activation(vaug[:, :, 0:P], m12[:, 0].rearrange("p (h e) -> p h e", e=P), ACT.Copy).then_inc(S["v_copied"], 1)
                copy_turned(c, 0)
                copy_turned(c, 1)
                wait(act, "ml_mixed", c, 0)
                nc.scalar.activation(gate[:], inp[:, s, MO:MO + 4], ACT.Exp, scale=-1.0).then_inc(S["eo_ready"], 1)
                window_exp(c, s, 2)
                window_exp(c, s, 3)
                if more:
                    act.wait_ge(loaded[1 - s], (i + s) * 64 + 64)
                    wait(act, "win", c, 4)
                    scale_queries(1 - s)
                copy_turned(c, 2)
                wait(act, "den_ready", c)
                for h in range(H):
                    last = nc.scalar.activation(sqjunk[:, h], heads_out[:, h // 2, h % 2, 0:P], ACT.Square,
                                                accum_out=ssq[:, h:h + 1])
                last.then_inc(S["ssq_ready"], 1)
                copy_turned(c, 3)
                wait(act, "snk_arg", c)
                nc.scalar.activation(snk[:], snk[:], ACT.Exp).then_inc(S["snk_exp"], 1)
                wait(act, "msq_ready", c)
                nc.scalar.activation(root[:], root[:], ACT.Sqrt).then_inc(S["root_ready"], 1)
                if more:
                    window_exp(c + 1, 1 - s, 0)
                    window_exp(c + 1, 1 - s, 1)

            act.wait_ge(loaded[0], 64)
            scale_queries(0)
            window_exp(0, 0, 0)
            window_exp(0, 0, 1)
            with act.Fori(0, NC // 2 - 1) as i:
                for s in range(2):
                    chunk(i, s, True)
            for s in range(2):
                chunk(NC // 2 - 1, s, s == 0)

        @block.vector
        def _(dve):
            def window_max(v, c, r, first=False):
                wait(dve, "win", c, 2 * (r // 2) + 2)
                if not first:
                    wait(dve, "p_exp", c, r - 1)
                dve.sem_inc(fence, 1)
                for g in range(2):
                    a, hd = 2 * r + g, g * J + r
                    last = nc.vector.tensor_tensor_reduce(
                        sw[:, r % 2, g], w01[:, g, (r % 2) * 256:(r % 2) * 256 + 256], bias[:, hd], 1.0,
                        sinks[:, a:a + 1], ALU.add, ALU.max, mx[:, a:a + 1])
                v(last)
                nc.vector.tensor_scalar(nmx[:, 2 * r:2 * r + 2], mx[:, 2 * r:2 * r + 2], -1.0, None,
                                        ALU.mult).then_inc(S["nmx_ready"], 1)

            def chunk(i, s, more):
                c = 2 * i + s
                v = Steps(dve, dve_s, c, DVE_STEPS)
                v.k = AHEAD
                emcol = cols[:, bass.ds(c, 1), 32:32 + H]
                sc_b = xs[:, s, :, 1]
                dve.wait_ge(loaded[s], i * 64 + 64)
                wait(dve, "d_exp", c, 0)
                nc.vector.tensor_copy(ucol[:, s].unsqueeze(1), cols[:, bass.ds(c, 1), 0:H]).then_inc(S["u_ready"], 1)
                wait(dve, "sv_turned", c)
                nc.vector.tensor_copy(vs[:, s], w3[:, 0:P]).then_inc(S["sv_ready"], 1)
                wait(dve, "d_exp", c)
                wait(dve, "scores", c)
                nc.vector.scalar_tensor_tensor(prob[:].rearrange("p h t -> p (h t)"), m12[:, 1], ML_SCALE,
                                               decay[:].rearrange("p h t -> p (h t)"), ALU.mult, ALU.mult).then_inc(S["p_ready"], 1)
                wait(dve, "k_turned", c)
                nc.vector.scalar_tensor_tensor(kw[:], m0[:].rearrange("p (h e) -> p h e", e=P), ML_SCALE,
                                               decay[:, :, C - 1:C].broadcast_to([P, H, P]), ALU.mult, ALU.mult).then_inc(S["kw_ready"], 1)
                window_max(v, c, 2)
                window_max(v, c, 3)
                wait(dve, "nmx_ready", c, 4)
                nc.vector.tensor_tensor(snk[:], sinks[:], nmx[:], ALU.add).then_inc(S["snk_arg"], 1)
                wait(dve, "gate_sum", c)
                nc.vector.reciprocal(gate[:], gate[:]).then_inc(S["gate_inv"], 1)
                wait(dve, "out_ml", c)
                nc.vector.tensor_copy(den[:].rearrange("p (b h) -> p b h", h=2).unsqueeze(3),
                                      heads_out[:, :, :, P:P + 1]).then_inc(S["den_ready"], 1)
                wait(dve, "state_up", c)
                for h in range(H):
                    last = nc.vector.scalar_tensor_tensor(state[:, h], state[:, h], sc_b[:, h, C - 1:C],
                                                          (m3, m0)[h // 2][:, (h % 2) * 129:(h % 2) * 129 + 129],
                                                          ALU.mult, ALU.add)
                last.then_inc(S["st_ready"], 1)
                wait(dve, "den_ready", c)
                v(nc.vector.scalar_tensor_tensor(rec[:], den[:], -1.0, den[:], ALU.mult, ALU.max))
                v(nc.vector.tensor_tensor(rec[:].unsqueeze(1), rec[:].unsqueeze(1), emcol, ALU.max))
                v(nc.vector.reciprocal(rec[:], rec[:]))
                wait(dve, "ssq_ready", c)
                v(nc.vector.tensor_tensor(root[:], ssq[:], rec[:], ALU.mult))
                v(nc.vector.tensor_tensor(root[:], root[:], rec[:], ALU.mult))
                nc.vector.tensor_scalar(root[:], root[:], 1.0 / P, NORM_EPS, ALU.mult, ALU.add).then_inc(S["msq_ready"], 1)
                wait(dve, "root_ready", c)
                v(nc.vector.reciprocal(root[:], root[:]))
                v(nc.vector.tensor_tensor(rec[:], rec[:], root[:], ALU.mult))
                nc.vector.tensor_tensor(hn[:].rearrange("p (b h) e -> p b h e", h=2), heads_out[:, :, :, 0:P],
                                        rec[:].rearrange("p (b h) -> p b h", h=2).unsqueeze(3).broadcast_to([P, 2, 2, P]),
                                        ALU.mult).then_inc(S["hn_ready"], 1)
                wait(dve, "snk_exp", c)
                wait(dve, "p_exp", c, 4)
                if more:
                    wait(dve, "bias_whole", 0)
                    window_max(v, c + 1, 0)
                    window_max(v, c + 1, 1)
                v(nc.vector.tensor_tensor(snk[:], snk[:], psums[:, s], ALU.add))
                v(nc.vector.reciprocal(snk[:], snk[:]))
                wait(dve, "swa_out", c)
                nc.vector.tensor_tensor(ow[:].rearrange("p r (g d) -> p (r g) d", g=2), w3[:].rearrange("p (a d) -> p a d", d=64),
                                        snk[:].unsqueeze(2).broadcast_to([P, 8, 64]), ALU.mult).then_inc(S["ow_ready"], 1)
                dve.wait_ge(mix_out[s], i * 16 + 16)
                wait(dve, "h_turned", c)
                wait(dve, "gate_ready", c)
                nc.vector.tensor_tensor(mix[:, s, 0:4].rearrange("p h t -> p (h t)"), m3[:],
                                        gate[:].rearrange("p h t -> p (h t)"), ALU.mult).then_inc(S["ml_mixed"], 1)
                wait(dve, "o_turned", c)
                nc.vector.tensor_copy(mix[:, s, 4:8].rearrange("p h t -> p (h t)"), w2[:]).then_inc(S["chunk_done"], 1)
                if more:
                    assert v.k == DVE_STEPS + AHEAD, v.k
                else:
                    dve.sem_inc(dve_s, AHEAD)

            dve.wait_ge(const_in, 48)
            dve.wait_ge(zeroed, 4)
            ahead = Steps(dve, dve_s)
            window_max(ahead, 0, 0, True)
            window_max(ahead, 0, 1, True)
            with dve.Fori(0, NC // 2 - 1) as i:
                for s in range(2):
                    chunk(i, s, True)
            for s in range(2):
                chunk(NC // 2 - 1, s, s == 0)
            dve.wait_ge(S["st_ready"], NC + 1)
            nc.vector.tensor_copy(nlast[:].unsqueeze(2), state[:, :, P:P + 1]).then_inc(dve_s, 1)


def sample(nc, io, keep):
    cols, ident, sbias = keep["cols"], keep["ident"], keep["sbias"]
    with ExitStack() as ctx:
        m = Store(nc, ctx)
        inp = m.sb("s_inp", [P, NPROJ, NS])
        xs = m.sb("s_xs", [P, H, 2, NS])
        state = m.sb("s_state", [P, DB * H, P + 1])
        n0 = m.sb("s_n0", [P, DB * H])
        kc = m.sb("s_kc", [P, DB, W])
        vc = m.sb("s_vc", [P, DB, P])
        causal = m.sb("s_causal", [NS, NS])
        sinkcol = m.sb("s_sinkcol", [P, 1])
        gml = m.sb("s_gml", [P, H])
        expo = m.sb("s_expo", [NS, H, NS])
        decay = m.sb("s_decay", [NS, H, NS])
        prob = m.sb("s_prob", [NS, H, NS])
        vaug = m.sb("s_vaug", [NS, H, P + 1])
        ktok = m.sb("s_ktok", [NS, H, P])
        kw = m.sb("s_kw", [NS, DB, H, P])
        qs = m.sb("s_qs", [P, H, DB * (NS + DT)])
        qb = m.sb("s_qb", [P, DB, 2, DT, J])
        swin = m.sb("s_swin", [P, 2, W + NS])
        mx, nmx, psums, snk = (m.sb(n, [P, 2]) for n in ("s_mx", "s_nmx", "s_psums", "s_snk"))
        kvtok = m.sb("s_kvtok", [NS, 2, P])
        pt1 = m.sb("s_pt1", [P, 2, P])
        pt2 = m.sb("s_pt2", [NS, 2, P])
        den, rec, ssq, root = (m.sb(n, [NS, H]) for n in ("s_den", "s_rec", "s_ssq", "s_root"))
        sqjunk = m.sb("s_sqjunk", [NS, H, P])
        hn = m.sb("s_hn", [NS, H, P])
        gate = m.sb("s_gate", [P, H, NS])
        mix = m.sb("s_mixed", [P, 8, NS])
        kv = m.ps("s_kv", [P, 2, 512])
        upd = m.ps("s_upd", [P, 2, 512])
        ho = m.ps("s_ho", [P, 2, 512])
        sc = m.ps("s_sc", [P, 512])
        wi = m.ps("s_wi", [P, 512])
        heads_out = ho[0:NS, :, 0:258].rearrange("p b (h e) -> p b h e", e=P + 1)
        names = "loaded zeroed v_done a_done kv_turned scores win p_turned win_out heads up h_turned stored".split()
        S = {n: m.sem("s_" + n) for n in names}
        LOADS = 12
        block = ctx.enter_context(nc.Block())
        sig = {n: m.sem("s_v_" + n) for n in ("expo", "prob", "kw", "nmx", "snk", "wprob", "pt", "den", "msq", "hn", "state", "mixed", "tok", "qb", "qs")}

        @block.sync
        def _(sp):
            tok = slice(SEQ, NT)
            for dst, src in (
                    (inp[:], io["projT"][:, :, tok].rearrange("t p n -> p t n")),
                    (xs[:].rearrange("p h w n -> p (h w) n"),
                     bass.AP(tensor=io["xsT"].tensor, offset=SEQ, ap=[[0, P], [NT, 2 * H], [1, NS]])),
                    (causal[:], io["c_causal_s"]), (sinkcol[:], io["sink_col"]), (gml[:], io["g_ml"]), (n0[:], io["n0"]),
                    (kc[:], io["cache_kT"]), (vc[:], io["cache_v"].rearrange("b k n -> k b n")),
                    *((state[:, q * 8:q * 8 + 8, 0:P], io["state_C"][:, q * 8:q * 8 + 8]) for q in range(4))):
                sp.dma_start(dst, src).then_inc(S["loaded"], 16)
            for a in "kv":
                sp.dma_start(io[f"s_{a}"][:, 0:W - DT], io[f"cache_{a}"][:, DT:W]).then_inc(S["stored"], 16)
            sp.wait_ge(sig["tok"], 1)
            for i, a in enumerate("kv"):
                sp.dma_start(io[f"s_{a}"][:, W - DT:W], kvtok[:, i]).then_inc(S["stored"], 16)
            sp.wait_ge(sig["mixed"], 3)
            sp.dma_start(io["mixT"][:, :, tok].rearrange("t p n -> p t n"), mix[:]).then_inc(S["stored"], 16)
            sp.wait_ge(sig["state"], DB + 1)
            sp.dma_start(io["s_C"], state[:, :, 0:P]).then_inc(S["stored"], 16)
            sp.dma_start(io["s_n"], n0[:]).then_inc(S["stored"], 16)
            sp.wait_ge(S["stored"], 7 * 16)

        @block.gpsimd
        def _(pool):
            nc.gpsimd.memset(qs[:], 0.0).then_inc(S["zeroed"], 1)
            nc.gpsimd.memset(qb[:], 0.0).then_inc(S["zeroed"], 1)
            nc.gpsimd.memset(vaug[:], 1.0).then_inc(S["zeroed"], 1)

        @block.tensor
        def _(pe):
            pe.wait_ge(S["loaded"], 16 * LOADS)
            for i, a in enumerate((SK, SV)):
                last = pe.transpose(sc[0:NS, P + i * P:2 * P + i * P], inp[:, a], ident[:])
            for h in range(H):
                pe.transpose(kv[0:NS, 0, h * P:h * P + P], inp[:, MK + h], ident[:])
                last = pe.transpose(kv[0:NS, 1, h * P:h * P + P], inp[:, MV + h], ident[:])
            last.then_inc(S["kv_turned"], 1)
            for h in range(H):
                last = pe.matmul(sc[0:NS, h * NS:h * NS + NS], inp[:, MK + h], inp[:, MQ + h], start=True, stop=True)
            last.then_inc(S["scores"], 1)
            pe.wait_ge(sig["qb"], 2)
            for b in range(DB):
                half, rows = b // 4, slice(32 * (b % 4), 32 * (b % 4) + 32)
                q = qb[:, b].rearrange("p g t j -> p (g t j)")
                pe.matmul(wi[rows, half * 160:half * 160 + W], q, kc[:, b], start=True, stop=True)
                last = pe.matmul(wi[rows, half * 160 + W:half * 160 + 160], q, inp[:, SK], start=True, stop=True)
            last.then_inc(S["win"], 1)
            pe.wait_ge(sig["prob"], 2)
            pe.wait_ge(sig["qs"], 1)
            for h in range(H):
                pe.matmul(heads_out[:, h // 2, h % 2], prob[:, h], vaug[:, h], start=True, stop=False)
                for b in range(DB):
                    last = pe.matmul(heads_out[:, h // 2, h % 2], qs[:, h, b * NS:b * NS + NS], state[:, b * H + h],
                                     start=False, stop=(b == DB - 1))
            last.then_inc(S["heads"], 1)
            pe.wait_ge(sig["wprob"], 1)
            for half in range(2):
                pe.transpose(wi[:, half * P:half * P + P], swin[:, half, 0:W], ident[:])
                last = pe.transpose(wi[0:NS, 256 + half * P:256 + half * P + P], swin[:, half, W:W + NS], ident[:])
            last.then_inc(S["p_turned"], 1)
            for b in range(DB):
                pe.wait_ge(sig["kw"], b + 1)
                if b >= 2:
                    pe.wait_ge(sig["state"], b)
                for h in range(H):
                    last = pe.matmul((upd, kv)[b % 2][:, h // 2, (h % 2) * 129:(h % 2) * 129 + 129], kw[:, b, h], vaug[:, h],
                                     start=True, stop=True)
                last.then_inc(S["up"], 1)
            pe.wait_ge(sig["pt"], 1)
            for b in range(DB):
                half, c = b // 4, slice(32 * (b % 4), 32 * (b % 4) + 32)
                pe.matmul(sc[:, b * 32:b * 32 + 32], vc[:, b], pt1[:, half, c], start=True, stop=False)
                last = pe.matmul(sc[:, b * 32:b * 32 + 32], kvtok[:, 1], pt2[:, half, c], start=False, stop=True)
            last.then_inc(S["win_out"], 1)
            pe.wait_ge(sig["hn"], 1)
            for h in range(H):
                last = pe.transpose(wi[:, h * NS:h * NS + NS], hn[:, h], ident[0:NS, 0:NS])
            last.then_inc(S["h_turned"], 1)

        @block.scalar
        def _(act):
            a = Steps(act, S["a_done"])
            act.wait_ge(S["loaded"], 16 * LOADS)
            a(nc.scalar.activation(gate[:], inp[:, MO:MO + 4], ACT.Exp, scale=-1.0))
            act.wait_ge(sig["expo"], 1)
            a(nc.scalar.activation(decay[:], expo[:], ACT.Exp))
            act.wait_ge(sig["nmx"], 1)
            for half in range(2):
                a(nc.scalar.activation(swin[:, half], swin[:, half], ACT.Exp, bias=nmx[:, half:half + 1],
                                       accum_out=psums[:, half:half + 1]))
            act.wait_ge(sig["snk"], 1)
            a(nc.scalar.activation(snk[:], snk[:], ACT.Exp))
            act.wait_ge(sig["den"], 1)
            for h in range(H):
                a(nc.scalar.activation(sqjunk[:, h], heads_out[:, h // 2, h % 2, 0:P], ACT.Square, accum_out=ssq[:, h:h + 1]))
            act.wait_ge(sig["msq"], 1)
            a(nc.scalar.activation(root[:], root[:], ACT.Sqrt))

        @block.vector
        def _(dve):
            v = Steps(dve, S["v_done"])
            dve.wait_ge(S["loaded"], 16 * LOADS)
            dve.wait_ge(S["zeroed"], 3)
            nc.vector.tensor_copy(state[:, :, P:P + 1], n0[:].unsqueeze(2)).then_inc(sig["state"], 1)
            for g in range(2):
                gp = slice(64 * g, 64 * g + 64)
                nc.vector.tensor_scalar(qb[gp, :, g], inp[gp, SQ:SQ + 4].rearrange("p j (b t) -> p b t j", t=DT),
                                        SWA_SCALE, None, ALU.mult).then_inc(sig["qb"], 1)
            for h in range(H):
                last = nc.vector.scalar_tensor_tensor(expo[:, h], xs[0:NS, h, 0], cols[0:NS, NC, h:h + 1], causal[:],
                                                      ALU.add, ALU.add)
            last.then_inc(sig["expo"], 1)
            for h in range(H):
                last = nc.vector.tensor_tensor(
                    qs[:, h].rearrange("p (b r) -> p b r", r=NS + DT)[:, :, 0:DT],
                    inp[:, MQ + h].rearrange("p (b t) -> p b t", t=DT), xs[:, h, 1].rearrange("p (b t) -> p b t", t=DT), ALU.mult)
            last.then_inc(sig["qs"], 1)
            dve.wait_ge(S["scores"], 1)
            nc.vector.tensor_copy(kvtok[:].rearrange("p a n -> p (a n)"), sc[0:NS, P:3 * P]).then_inc(sig["tok"], 1)
            v(nc.vector.tensor_scalar(ktok[:].rearrange("p h e -> p (h e)"), kv[0:NS, 0], ML_SCALE, None, ALU.mult))
            nc.vector.tensor_copy(vaug[:, :, 0:P], kv[0:NS, 1].rearrange("p (h e) -> p h e", e=P)).then_inc(sig["prob"], 1)
            dve.wait_ge(S["a_done"], 2)
            dve.wait_ge(S["scores"], 1)
            nc.vector.scalar_tensor_tensor(prob[:].rearrange("p h t -> p (h t)"), sc[0:NS, 0:P], ML_SCALE,
                                           decay[:].rearrange("p h t -> p (h t)"), ALU.mult, ALU.mult).then_inc(sig["prob"], 1)
            for b in range(DB):
                e = DT * b + DT - 1
                nc.vector.tensor_tensor(kw[:, b], ktok[:], decay[:, :, e:e + 1].broadcast_to([NS, H, P]), ALU.mult).then_inc(sig["kw"], 1)
            dve.wait_ge(S["win"], 1)
            v(nc.vector.tensor_tensor(swin[:].rearrange("p a k -> p (a k)"), wi[:, 0:320], sbias[:].rearrange("p a k -> p (a k)"), ALU.add))
            v(nc.vector.tensor_reduce(mx[:], swin[:], AX.X, ALU.max))
            v(nc.vector.tensor_scalar(mx[:], mx[:], sinkcol[:, 0:1], None, ALU.max))
            nc.vector.tensor_scalar(nmx[:], mx[:], -1.0, None, ALU.mult).then_inc(sig["nmx"], 1)
            dve.wait_ge(sig["nmx"], 1)
            nc.vector.tensor_scalar(snk[:], nmx[:], sinkcol[:, 0:1], None, ALU.add).then_inc(sig["snk"], 1)
            dve.wait_ge(S["heads"], 1)
            nc.vector.tensor_copy(den[:].rearrange("p (b h) -> p b h", h=2).unsqueeze(3), heads_out[:, :, :, P:P + 1]).then_inc(sig["den"], 1)
            dve.wait_ge(S["a_done"], 5)
            v(nc.vector.tensor_tensor(snk[:], snk[:], psums[:], ALU.add))
            v(nc.vector.reciprocal(snk[:], snk[:]))
            for half in range(2):
                last = nc.vector.tensor_scalar(swin[:, half], swin[:, half], snk[:, half:half + 1], None, ALU.mult)
            last.then_inc(sig["wprob"], 1)
            dve.wait_ge(sig["den"], 1)
            v(nc.vector.scalar_tensor_tensor(rec[:], den[:], -1.0, den[:], ALU.mult, ALU.max))
            v(nc.vector.tensor_tensor(rec[:], rec[:], cols[0:NS, NC, 32:32 + H], ALU.max))
            v(nc.vector.reciprocal(rec[:], rec[:]))
            dve.wait_ge(S["a_done"], 9)
            v(nc.vector.tensor_tensor(root[:], ssq[:], rec[:], ALU.mult))
            v(nc.vector.tensor_tensor(root[:], root[:], rec[:], ALU.mult))
            nc.vector.tensor_scalar(root[:], root[:], 1.0 / P, NORM_EPS, ALU.mult, ALU.add).then_inc(sig["msq"], 1)
            dve.wait_ge(S["p_turned"], 1)
            v(nc.vector.tensor_copy(pt1[:].rearrange("p a n -> p (a n)"), wi[:, 0:256]))
            nc.vector.tensor_copy(pt2[:].rearrange("p a n -> p (a n)"), wi[0:NS, 256:512]).then_inc(sig["pt"], 1)
            dve.wait_ge(S["a_done"], 10)
            v(nc.vector.reciprocal(root[:], root[:]))
            v(nc.vector.tensor_tensor(rec[:], rec[:], root[:], ALU.mult))
            nc.vector.tensor_tensor(hn[:].rearrange("p (b h) e -> p b h e", h=2), heads_out[:, :, :, 0:P],
                                    rec[:].rearrange("p (b h) -> p b h", h=2).unsqueeze(3).broadcast_to([NS, 2, 2, P]),
                                    ALU.mult).then_inc(sig["hn"], 1)
            v(nc.vector.tensor_scalar(gate[:], gate[:], 1.0, None, ALU.add))
            v(nc.vector.reciprocal(gate[:], gate[:]))
            v(nc.vector.tensor_tensor(gate[:], gate[:], gml[:].unsqueeze(2).broadcast_to([P, H, NS]), ALU.mult))
            for b in range(DB):
                dve.wait_ge(S["up"], b + 1)
                for h in range(H):
                    last = nc.vector.scalar_tensor_tensor(
                        state[:, b * H + h], state[:, b * H + h], xs[:, h, 1, DT * b + DT - 1:DT * b + DT],
                        (upd, kv)[b % 2][:, h // 2, (h % 2) * 129:(h % 2) * 129 + 129], ALU.mult, ALU.add)
                if b < DB - 1:
                    last.then_inc(sig["state"], 1)
            v(last)
            nc.vector.tensor_copy(n0[:].unsqueeze(2), state[:, :, P:P + 1]).then_inc(sig["state"], 1)
            dve.wait_ge(S["win_out"], 1)
            for g in range(2):
                gp = slice(64 * g, 64 * g + 64)
                nc.vector.tensor_copy(mix[gp, 4:8].rearrange("p j (b t) -> p b t j", t=DT),
                                      sc[gp, 0:DB * 32].rearrange("p (b g t j) -> p b g t j", g=2, t=DT, j=J)[:, :, g]).then_inc(sig["mixed"], 1)
            dve.wait_ge(S["h_turned"], 1)
            nc.vector.tensor_tensor(mix[:, 0:4].rearrange("p h t -> p (h t)"), wi[:, 0:P],
                                    gate[:].rearrange("p h t -> p (h t)"), ALU.mult).then_inc(sig["mixed"], 1)


def layer(nc, io):
    OUT1, IN, OUT2 = 8, 2 * KF, 16
    FIRST = OUT1 + IN
    SLABS = OUT1 + IN + OUT2
    TILES = OUT1 + IN + 8
    HEAD = 2
    BANKS = 4
    NORMS = 2 * NTT
    with ExitStack() as ctx:
        m = Store(nc, ctx)
        raw = m.sb("l_raw", [P, 2, HALF, P])
        whi = m.sb("l_whi", [P, 2, HALF, P], F32R)
        wlo = m.sb("l_wlo", [P, 2, HALF, P], F32R)
        ah = m.sb("ah", [P, KD, TG], F32R)
        al = m.sb("al", [P, KD, TG], F32R)
        mixr = m.sb("mixr", [P, KD, TG])
        nxt = m.sb("nxt", [P, KD, TG])
        res = m.sb("res", [P, KD, TG])
        hh = m.sb("hh", [P, KF, TG], F32R)
        hl = m.sb("hl", [P, KF, TG], F32R)
        hbuf = m.sb("hbuf", [P, TG])
        silu = m.sb("silu", [P, 2, TG])
        nrm = m.sb("nrm", [TOK, 2, D])
        g2b = m.sb("g2b", [TOK, D])
        b2b = m.sb("b2b", [TOK, D])
        gb1 = m.sb("gb1", [P, 2, KD])
        ident = m.sb("l_ident", [P, P])
        stats = m.sb("stats", [TOK, 2, 6])
        mv = m.sb("mv", [TOK, 2])
        rstd = m.sb("rstd", [TOK, 2])
        acc = m.ps("l_acc", [P, BANKS, 512])
        turned = m.ps("turned", [P, 2, 512])
        back = m.ps("back", [P, 2, 512])
        S = {n: m.sem("l_" + n) for n in
             "const_in mix_in x_in hi_done lo_done slab_done evac mix_split ta_full tb_full normed root_arg root_done "
             "x1_split silu_done h_hi h_split mix_hi y_ready moved".split()}
        raw_in = [m.sem(f"l_raw_in{s}") for s in range(2)]
        y_out = [m.sem(f"l_y_out{s}") for s in range(2)]
        dve_s = m.sem("l_dve")
        fences = m.sem("l_fences")
        turned_tok = turned[0:TOK].rearrange("p b n -> p (b n)")
        CONSTS = 16 * 5

        def apart(eng):
            eng.sem_inc(fences, 1)

        block = ctx.enter_context(nc.Block())

        @block.sync
        def _(sp):
            def slab8(i, s):
                sp.dma_start(raw[:, s, 0:KD], io["wB"][bass.ds(i, 1)].rearrange("a p k n -> (a p) k n")).then_inc(raw_in[s], 16)

            def slab11(i, s):
                sp.dma_start(raw[:, s], io["w2"][bass.ds(i, 1)].rearrange("a p k n -> (a p) k n")).then_inc(raw_in[s], 16)

            def stream(base, lo, hi, load, off):
                with sp.Fori(lo, hi) as u:
                    for s in range(2):
                        sp.wait_ge(S["lo_done"], base + 2 * u + s - 1)
                        apart(sp)
                        load(2 * u + s + off, s)

            def mixed(g):
                sp.dma_start(mixr[:], io["mixT"][:, :, bass.ds(g * TG, TG)].rearrange("t p n -> p t n")).then_inc(S["mix_in"], 16)

            def tokens(g):
                sp.dma_start(nxt[:], io["xT"][bass.ds(g, 1)].rearrange("a p k n -> (a p) k n")).then_inc(S["x_in"], 16)

            for s in range(2):
                slab8(s, s)
            mixed(0)
            tokens(0)
            row = lambda a: bass.AP(tensor=io[a].tensor, offset=0, ap=[[0, TOK], [1, D]])
            for dst, src in ((ident[:], io["c_ident"]), (gb1[:, 0], io["g1"]), (gb1[:, 1], io["b1"]), (g2b[:], row("g2")), (b2b[:], row("b2"))):
                sp.dma_start(dst, src).then_inc(S["const_in"], 16)
            stream(0, 1, (OUT1 + IN) // 2, slab8, 0)
            with sp.Fori(0, NG - 1) as g:
                at = g * SLABS + FIRST
                sp.wait_ge(S["mix_split"], g + 1)
                apart(sp)
                mixed(g + 1)
                sp.wait_ge(S["moved"], g + 1)
                apart(sp)
                tokens(g + 1)
                stream(at, 0, HEAD, slab11, 0)
                stream(at + 2 * HEAD, 0, OUT1 // 2, slab8, 0)
                stream(at + OUT1, HEAD, 8, slab11, 0)
                stream(at + OUT1 + OUT2, 0, KF, slab8, OUT1)
            stream((NG - 1) * SLABS + FIRST, 0, 8, slab11, 0)

        @block.gpsimd
        def _(pool):
            def rest(base, lo, hi, k):
                with pool.Fori(lo, hi) as u:
                    for s in range(2):
                        pool.wait_ge(S["hi_done"], base + 2 * u + s + 1)
                        nc.gpsimd.tensor_tensor(wlo[:, s, 0:k], raw[:, s, 0:k], whi[:, s, 0:k].bitcast(F32), ALU.subtract).then_inc(S["lo_done"], 1)

            rest(0, 0, FIRST // 2, KD)
            with pool.Fori(0, NG - 1) as g:
                at = g * SLABS + FIRST
                rest(at, 0, HEAD, HALF)
                rest(at + 2 * HEAD, 0, OUT1 // 2, KD)
                rest(at + OUT1, HEAD, 8, HALF)
                rest(at + OUT1 + OUT2, 0, KF, KD)
            rest((NG - 1) * SLABS + FIRST, 0, 8, HALF)

        @block.scalar
        def _(act):
            def rounded(n, k):
                for s in range(2):
                    act.wait_ge(raw_in[s], n // 2 * 16 + 16 if isinstance(n, int) else n * 8 + 16)
                    act.wait_ge(S["slab_done"], n + s + 1)
                    act.wait_ge(S["const_in"], CONSTS)
                    nc.scalar.activation(whi[:, s, 0:k], raw[:, s, 0:k], ACT.Copy).then_inc(S["hi_done"], 1)

            def root(n):
                act.wait_ge(S["root_arg"], n + 1)
                act.wait_ge(S["const_in"], CONSTS)
                nc.scalar.activation(rstd[:, 0:1], rstd[:, 0:1], ACT.Sqrt).then_inc(S["root_done"], 1)

            def store(g, i):
                act.wait_ge(S["y_ready"], g * NTT + i + 1)
                act.dma_start(io["y"][bass.ds(g * TG + i * TOK, TOK), :], nrm[:, i % 2]).then_inc(y_out[i % 2], 16)

            def gated(g, base, j, s):
                act.wait_ge(S["slab_done"], base + 2 * j + 3)
                act.wait_ge(S["h_split"], g * KF + j + 1)
                act.wait_ge(S["const_in"], CONSTS)
                nc.scalar.activation(silu[:, s], acc[:, 2 * s, 0:TG], ACT.Silu).then_inc(S["silu_done"], 1)

            def pairs(g, base, lo, hi, last):
                with act.Fori(lo // 2, hi // 2 - last) as q:
                    for s in range(2):
                        rounded(base + 4 * q + 2 * s + 2, KD)
                        gated(g, base, 2 * q + s, s)
                if last:
                    rounded(base + 2 * hi - 2, KD)
                    gated(g, base, hi - 2, 0)
                    rounded(base + 2 * hi, HALF)
                    gated(g, base, hi - 1, 1)

            for s in range(2):
                act.sem_inc(y_out[s], 16)
            for s in range(2):
                act.wait_ge(raw_in[s], 16)
                nc.scalar.activation(whi[:, s, 0:KD], raw[:, s, 0:KD], ACT.Copy).then_inc(S["hi_done"], 1)
            with act.Fori(1, 5) as u:
                rounded(u * 2, KD)
            for i in range(NTT):
                root(i)
            pairs(0, OUT1, 0, KF, 1)
            with act.Fori(0, NG - 1) as g:
                at = g * SLABS + FIRST
                norm = g * NORMS + NTT
                rounded(at + 2, HALF)
                rounded(at + 4, KD)
                with act.Fori(1, OUT1 // 2) as u:
                    rounded(at + 4 + 2 * u, KD)
                rounded(at + OUT1 + 2 * HEAD, HALF)
                for t in range(HEAD, 8):
                    rounded(at + OUT1 + 2 * t + 2, HALF if t < 7 else KD)
                    if t < HEAD + NTT:
                        root(norm + t - HEAD)
                for i in range(NTT):
                    rounded(at + OUT1 + OUT2 + 2 * i + 2, KD)
                    gated(g + 1, at + OUT1 + OUT2, i, i % 2)
                    root(norm + NTT + i)
                    store(g, i)
                pairs(g + 1, at + OUT1 + OUT2, NTT, KF, 1)
            at = (NG - 1) * SLABS + FIRST
            with act.Fori(1, 8) as u:
                rounded(at + 2 * u, HALF)
            for i in range(NTT):
                root((NG - 1) * NORMS + NTT + i)
                store(NG - 1, i)
            for s in range(2):
                act.wait_ge(y_out[s], 16 + 16 * NG * NTT // 2)

        @block.tensor
        def _(pe):
            def slab(n, s, bank, hx, lx, k0, k, total):
                pe.wait_ge(S["lo_done"], n + 1)
                for c in range(k):
                    a = k0 + c
                    pe.matmul(acc[:, bank, 0:TG], whi[:, s, c], hx[:, a], start=(a == 0), stop=False)
                    pe.matmul(acc[:, bank, 0:TG], whi[:, s, c], lx[:, a], start=False, stop=False)
                    last = pe.matmul(acc[:, bank, 0:TG], wlo[:, s, c], hx[:, a], start=False, stop=(a == total - 1))
                last.then_inc(S["slab_done"], 1)

            def tile(n, m, b):
                pe.wait_ge(S["evac"], m + 1)
                slab(n, b % 2, b, ah, al, 0, KD, KD)

            def tile2(n, m, b):
                pe.wait_ge(S["evac"], m + 1)
                for s in range(2):
                    slab(n + s, s, b, hh, hl, s * HALF, HALF, KF)

            def turn(src, i):
                for k in range(KD):
                    last = pe.transpose(turned[0:TOK, k // 4, (k % 4) * P:(k % 4) * P + P],
                                        src[:, k, i * TOK:i * TOK + TOK], ident[:])
                last.then_inc(S["ta_full"], 1)

            def turn_back(g, i):
                pe.wait_ge(S["x1_split"], g * NTT + i + 1)
                for k in range(KD):
                    last = pe.transpose(back[:, k // 4, (k % 4) * TOK:(k % 4) * TOK + TOK],
                                        nrm[:, i % 2, k * P:k * P + P], ident[0:TOK, 0:TOK])
                last.then_inc(S["tb_full"], 1)

            pe.sem_inc(S["slab_done"], 2)
            pe.wait_ge(S["const_in"], CONSTS)
            pe.wait_ge(S["mix_split"], 1)
            with pe.Fori(0, OUT1 // BANKS) as q:
                for b in range(BANKS):
                    tile(q * BANKS + b, q * BANKS + b, b)
            pe.wait_ge(S["evac"], OUT1 + BANKS)
            turn(nxt, 0)
            for i in range(NTT):
                pe.wait_ge(S["normed"], i + 1)
                if i < NTT - 1:
                    turn(nxt, i + 1)
                turn_back(0, i)
            pe.wait_ge(S["x1_split"], NTT + 1)
            with pe.Fori(0, IN // BANKS) as q:
                for b in range(BANKS):
                    tile(q * BANKS + b + OUT1, q * BANKS + b + OUT1, b)
            with pe.Fori(0, NG - 1) as g:
                at = g * SLABS + FIRST
                ta = g * TILES + FIRST
                norm = g * NORMS + NTT
                pe.wait_ge(S["h_split"], g * KF + KF + 2)
                for t in range(HEAD):
                    tile2(at + 2 * t, ta + t, t)
                pe.wait_ge(S["mix_split"], g + 2)
                for t in range(OUT1):
                    tile(at + 2 * HEAD + t, ta + HEAD + t, (HEAD + t) % BANKS) if HEAD % 2 == 0 else None
                for t in range(HEAD, 8):
                    tile2(at + OUT1 + 2 * t, ta + OUT1 + t, t % BANKS)
                    i = t - HEAD
                    if i == 0:
                        pe.wait_ge(S["evac"], ta + HEAD + OUT1 + BANKS)
                    if 1 <= i <= NTT:
                        pe.wait_ge(S["normed"], norm + i)
                    if i < NTT:
                        turn(nxt, i)
                    if 1 <= i <= NTT:
                        turn_back(g + 1, i - 1)
                pe.wait_ge(S["x1_split"], (g + 2) * NTT + 1)
                ai, ti = at + OUT1 + OUT2, ta + OUT1 + 8
                for j in range(NTT):
                    for b in range(2):
                        tile(ai + 2 * j + b, ti + 2 * j + b, (2 * j + b) % BANKS)
                    if j == 0:
                        pe.wait_ge(S["evac"], ti + BANKS)
                    pe.wait_ge(S["normed"], norm + NTT + j)
                    turn(res, j)
                apart(pe)
                with pe.Fori(NTT // 2, KF // 2) as q:
                    for b in range(BANKS):
                        tile(ai + q * BANKS + b, ti + q * BANKS + b, b)
            at, ta = (NG - 1) * SLABS + FIRST, (NG - 1) * TILES + FIRST
            pe.wait_ge(S["h_split"], NG * KF + 2)
            with pe.Fori(0, 2) as q:
                for b in range(BANKS):
                    tile2(at + 8 * q + 2 * b, ta + BANKS * q + b, b)
            pe.wait_ge(S["evac"], ta + 8 + BANKS)
            for i in range(NTT):
                pe.wait_ge(S["normed"], (NG - 1) * NORMS + NTT + i)
                turn(res, i)

        @block.vector
        def _(dve):
            dve.sem_inc(S["evac"], BANKS)
            dve.sem_inc(S["x1_split"], 1)
            dve.sem_inc(S["h_split"], 2)

            def split_mix(turn):
                nc.vector.tensor_copy(ah[:], mixr[:]).then_inc(S["mix_hi"], 1)
                dve.wait_ge(S["mix_hi"], turn + 1)
                nc.vector.tensor_tensor(al[:], mixr[:], ah[:].bitcast(F32), ALU.subtract).then_inc(S["mix_split"], 1)

            def add(dst, t, bank, slab):
                dve.wait_ge(S["slab_done"], slab + 3)
                nc.vector.scalar_tensor_tensor(dst[:, t], dst[:, t], ALPHA, acc[:, bank, 0:TG], ALU.mult, ALU.add).then_inc(S["evac"], 1)

            def normed(v, n, g, i, second):
                dve.wait_ge(S["ta_full"], n + 1)
                for b in range(2):
                    last = nc.vector.bn_stats(stats[:, b], turned[0:TOK, b])
                v(last)
                apart(dve)
                v(nc.vector.bn_aggr(mv[:], stats[:].rearrange("p a b -> p (a b)")))
                nc.vector.tensor_scalar(rstd[:, 0:1], mv[:, 1:2], LN_EPS, None, ALU.add).then_inc(S["root_arg"], 1)
                dve.wait_ge(S["root_done"], n + 1)
                v(nc.vector.reciprocal(rstd[:, 1:2], rstd[:, 0:1]))
                dve.wait_ge(y_out[i % 2], 16 * (2 * g + (i // 2 if second else 0) + 1))
                nc.vector.tensor_scalar(nrm[:, i % 2], turned_tok, mv[:, 0:1], rstd[:, 1:2],
                                        ALU.subtract, ALU.mult).then_inc(S["normed"], 1)

            def split(v, g, i):
                t = slice(i * TOK, i * TOK + TOK)
                dve.wait_ge(S["tb_full"], g * NTT + i + 1)
                for b in range(2):
                    last = nc.vector.tensor_tensor(
                        nxt[:, 4 * b:4 * b + 4, t], back[:, b, 0:4 * TOK].rearrange("p (k t) -> p k t", t=TOK),
                        gb1[:, 0, 4 * b:4 * b + 4].unsqueeze(2).broadcast_to([P, 4, TOK]), ALU.mult)
                v(last)
                v(nc.vector.tensor_tensor(nxt[:, :, t], nxt[:, :, t], gb1[:, 1].unsqueeze(2).broadcast_to([P, KD, TOK]), ALU.add))
                v(nc.vector.tensor_copy(ah[:, :, t], nxt[:, :, t]))
                nc.vector.tensor_tensor(al[:, :, t], nxt[:, :, t], ah[:, :, t].bitcast(F32), ALU.subtract).then_inc(S["x1_split"], 1)

            def output(v, n, i):
                dve.wait_ge(S["normed"], n + 1)
                v(nc.vector.tensor_tensor(nrm[:, i % 2], nrm[:, i % 2], g2b[:], ALU.mult))
                nc.vector.tensor_tensor(nrm[:, i % 2], nrm[:, i % 2], b2b[:], ALU.add).then_inc(S["y_ready"], 1)

            def gated(g, base, tiles, j, s):
                dve.wait_ge(S["silu_done"], g * KF + j + 1)
                dve.wait_ge(S["slab_done"], base + 2 * j + 4)
                dve.wait_ge(S["h_split"], g * KF + j + 2)
                nc.vector.tensor_tensor(hbuf[:], silu[:, s], acc[:, 2 * s + 1, 0:TG], ALU.mult).then_inc(S["evac"], 2)
                dve.wait_ge(S["evac"], tiles + 2 * j + 2 + BANKS)
                at = bass.ds(j, 1)
                nc.vector.tensor_copy(hh[:, at], hbuf[:].unsqueeze(1)).then_inc(S["h_hi"], 1)
                dve.wait_ge(S["h_hi"], g * KF + j + 1)
                nc.vector.tensor_tensor(hl[:, at], hbuf[:].unsqueeze(1), hh[:, at].bitcast(F32), ALU.subtract).then_inc(S["h_split"], 1)

            dve.wait_ge(S["mix_in"], 16)
            split_mix(0)
            dve.wait_ge(S["const_in"], CONSTS)
            dve.wait_ge(S["x_in"], 16)
            for t in range(OUT1):
                add(nxt, t, t % BANKS, t)
            v = Steps(dve, dve_s)
            for i in range(NTT):
                normed(v, i, 0, i, False)
                if i:
                    split(v, 0, i - 1)
            split(v, 0, NTT - 1)
            dve.wait_ge(S["x1_split"], NTT + 1)
            nc.vector.tensor_copy(res[:], nxt[:]).then_inc(S["moved"], 1)
            with dve.Fori(0, KF // 2) as q:
                for s in range(2):
                    gated(0, OUT1, OUT1, 2 * q + s, s)
            before = v.k
            with dve.Fori(0, NG - 1) as g:
                at = g * SLABS + FIRST
                ta = g * TILES + FIRST
                norm = g * NORMS + NTT
                v = Steps(dve, dve_s, g, 3 * NORMS + 4 * NTT)
                v.k = before
                dve.wait_ge(S["mix_in"], g * 16 + 32)
                dve.wait_ge(S["slab_done"], at + 2)
                split_mix(g + 1)
                for t in range(HEAD):
                    add(res, t, t, at + 2 * t + 1)
                dve.wait_ge(S["x_in"], g * 16 + 32)
                for t in range(OUT1):
                    add(nxt, t, (HEAD + t) % BANKS, at + 2 * HEAD + t)
                for t in range(HEAD, 8):
                    add(res, t, t % BANKS, at + OUT1 + 2 * t + 1)
                    i = t - HEAD
                    if 1 <= i <= NTT:
                        split(v, g + 1, i - 1)
                    if i < NTT:
                        normed(v, norm + i, g, i, False)
                ai, ti = at + OUT1 + OUT2, ta + OUT1 + 8
                for j in range(NTT):
                    gated(g + 1, ai, ti, j, j % 2)
                    normed(v, norm + NTT + j, g, j, True)
                    output(v, norm + NTT + j, j)
                dve.wait_ge(S["x1_split"], (g + 2) * NTT + 1)
                nc.vector.tensor_copy(res[:], nxt[:]).then_inc(S["moved"], 1)
                with dve.Fori(NTT // 2, KF // 2) as q:
                    for s in range(2):
                        gated(g + 1, ai, ti, 2 * q + s, s)
                assert v.k == before + v.each
            at = (NG - 1) * SLABS + FIRST
            for t in range(8):
                add(res, t, t % BANKS, at + 2 * t + 1)
            v = Steps(dve, dve_s, NG - 1, v.each)
            v.k = before
            for i in range(NTT):
                normed(v, (NG - 1) * NORMS + NTT + i, NG - 1, i, True)
                output(v, (NG - 1) * NORMS + NTT + i, i)


def bass_hymba_step(nc, io):
    io["projT"] = nc.dram_tensor("projT", [NPROJ, P, NT], F32, kind="Internal").ap()
    io["gateT"] = nc.dram_tensor("gateT", [8, NT], F32, kind="Internal").ap()
    io["xsT"] = nc.dram_tensor("xsT", [H, 2, NT], F32, kind="Internal").ap()
    io["ext"] = nc.dram_tensor("ext", [8, HJ], F32, kind="Internal").ap()
    io["mixT"] = nc.dram_tensor("mixT", [8, P, NT], F32, kind="Internal").ap()
    project(nc, io)
    with ExitStack() as ctx:
        m = Store(nc, ctx)
        keep = {
            "ident": m.sb("ident", [P, P]),
            "cols": m.sb("cols", [P, NC + 1, 64]),
            "bias": m.sb("bias", [P, 8, 2 * W]),
            "bias_prev": m.sb("bias_prev", [P, 8, W]),
            "sbias": m.sb("sbias", [P, 2, P + NS]),
            "ident_in": m.sem("ident_in"),
        }
        with nc.Block() as block:
            @block.sync
            def _(sp):
                sp.dma_start(keep["ident"][:], io["c_ident"]).then_inc(keep["ident_in"], 16)
                sp.wait_ge(keep["ident_in"], 16)
        gates(nc, io, keep)
        prompt(nc, io, keep)
        sample(nc, io, keep)
    layer(nc, io)


def constants():
    eye = np.eye(P, dtype=np.float32)
    dist = 255 - np.arange(HJ)
    n = np.maximum(dist, 1).astype(np.float32)
    large = 16 + (np.log(n / np.float32(16)) / np.float32(np.log(8.0)) * np.float32(16)).astype(np.int32)
    bucket = np.where(dist < 16, np.maximum(dist, 0), np.minimum(large, 31))
    seen = (dist >= 0) & (dist < W)
    onehot = ((np.arange(32)[:, None] == bucket) & seen).astype(np.float32)
    row = np.arange(P)
    seq = np.arange(NS) // DT
    smask = np.stack([np.where(half * 4 + row[:, None] // 32 == seq, 0.0, NEG) for half in range(2)], 1)
    s, t = np.arange(C)[:, None], np.arange(C)
    ds, dt = np.arange(NS)[:, None], np.arange(NS)
    return {
        "c_ident": eye, "c_anti": eye[::-1], "c_onehot": onehot,
        "c_outside": np.tile(np.where(seen, 0.0, NEG), (8, 1)),
        "c_repl": (np.arange(32)[:, None] == row % 32).astype(np.float32),
        "c_smask": smask,
        "c_causal": np.where(s <= t, 0.0, NEG),
        "c_causal_s": np.where((ds <= dt) & (ds // DT == dt // DT), 0.0, NEG),
    }


def w_in_order():
    base = 2056
    sq = [base + (g * J + j) * 64 + d for j in range(J) for g in range(2) for d in range(64)]
    return np.array([*range(2048), *sq, *range(base + 512, base + 768)]), np.arange(2048, 2056)


def layout(a):
    f = lambda k: np.asarray(a[k], np.float32)
    cols, gates = w_in_order()
    slabs = lambda w, k: np.ascontiguousarray(w.reshape(k, P, w.shape[1] // P, P).transpose(2, 1, 0, 3))
    x = np.concatenate([f("x_prompt").reshape(SEQ, D), f("x_sample").reshape(NS, D)])
    w = f("w_in")[0]
    out = {
        "xT": np.ascontiguousarray(x.reshape(NG, TG, KD, P).transpose(0, 3, 2, 1)),
        "wA": slabs(w[:, cols], KD),
        "wG": np.ascontiguousarray(w[:, gates].reshape(KD, P, 8).transpose(1, 0, 2)),
    }
    swa = [512 + (g * J + j) * 64 + d for j in range(J) for g in range(2) for d in range(64)]
    w1 = slabs(f("w_ffn_in")[0], KD)
    out.update({
        "wB": np.concatenate([slabs(f("w_out")[0][[*range(512), *swa]], KD), w1.reshape(2, KF, P, KD, P).swapaxes(0, 1).reshape(2 * KF, P, KD, P)]),
        "w2": f("w_ffn_out")[0].reshape(2, HALF, P, KD, P).transpose(3, 0, 2, 1, 4).reshape(2 * KD, P, HALF, P),
        "g1": f("ln1_g").reshape(KD, P).T, "b1": f("ln1_b").reshape(KD, P).T, "g2": f("ln2_g"), "b2": f("ln2_b"),
    })
    out.update({
        "b_ig": f("b_igate").reshape(H, 1), "b_fg": f("b_fgate").reshape(H, 1),
        "m0": f("state_mlstm_m")[0].T, "rel_bias": f("rel_bias"),
    })
    heads = [g * J + j for j in range(J) for g in range(2)]
    sinks = f("swa_sinks")[0]
    out.update({
        "sinks": sinks[heads].reshape(1, 8),
        "sink_col": np.broadcast_to(sinks.reshape(1, 2, 1, J), (4, 2, DT, J)).reshape(P, 1),
        "g_ml": f("ml_norm_g").reshape(H, P).T,
        "state_C": f("state_mlstm_C")[0].reshape(DB * H, P, P).transpose(1, 0, 2),
        "n0": f("state_mlstm_n")[0].reshape(DB * H, P).T,
        "cache_kT": f("cache_swa_k")[0].reshape(DB, W, P).transpose(2, 0, 1),
        "cache_k": f("cache_swa_k")[0].reshape(DB, W, P),
        "cache_v": f("cache_swa_v")[0].reshape(DB, W, P),
    })
    out.update(constants())
    return {k: np.ascontiguousarray(v, dtype=np.float32) for k, v in out.items()}


OUTS = {
    "y": [NT, D],
    "p_C": [P, H, P], "p_n": [P, H], "p_m": [H, 1], "p_k": [P, W], "p_v": [P, W],
    "s_C": [P, DB * H, P], "s_n": [P, DB * H], "s_m": [H, DB], "s_k": [DB, W, P], "s_v": [DB, W, P],
}


def kernel(**inputs):
    import concourse.bacc as bacc
    from concourse.bass_utils import run_bass_kernel_spmd

    nc = bacc.Bacc("TRN2", target_bir_lowering=False, num_devices=1)
    arrays = layout(inputs)
    io = {n: nc.dram_tensor("in_" + n, a.shape, F32, kind="ExternalInput").ap() for n, a in arrays.items()}
    io.update({n: nc.dram_tensor("out_" + n, s, F32, kind="ExternalOutput").ap() for n, s in OUTS.items()})
    bass_hymba_step(nc, io)
    r = run_bass_kernel_spmd(nc, [{"in_" + n: a for n, a in arrays.items()}], core_ids=[0]).results[0]
    o = {n: r["out_" + n] for n in OUTS}
    one = lambda x: np.ascontiguousarray(x)[None]
    feature = lambda x: x.T.reshape(1, W, 2, 64)
    return (
        one(o["y"][0:SEQ]), np.ascontiguousarray(o["y"][SEQ:NT]).reshape(DB, DT, D),
        one(o["p_C"].transpose(1, 0, 2)[None]), one(o["p_n"].T[None]), one(o["p_m"].T), one(feature(o["p_k"])), one(feature(o["p_v"])),
        one(o["s_C"].transpose(1, 0, 2).reshape(DB, H, P, P)), one(o["s_n"].T.reshape(DB, H, P)), one(o["s_m"].T),
        one(o["s_k"].reshape(DB, W, 2, 64)), one(o["s_v"].reshape(DB, W, 2, 64)),
    )
```

```python
from contextlib import ExitStack

import numpy as np

import concourse.bass as bass
from concourse import mybir

F32 = mybir.dt.float32
F32R = mybir.dt.float32r
ALU = mybir.AluOpType
ACT = mybir.ActivationFunctionType
AX = mybir.AxisListType

P = 128
D = 1024
KD = D // P
SEQ = 2048
DB, DT = 8, 4
NS = DB * DT
NT = SEQ + NS
NG = 5
TG = NT // NG
TOK = 104
NTT = TG // TOK
H = 4
C = 128
NC = SEQ // C
J = 4
W = 128
PAST = 128
FF = 2816
KF = FF // P
HALF = KF // 2
NPROJ = 22
MQ, MK, MV, MO, SQ, SK, SV = 0, 4, 8, 12, 16, 20, 21
QD, KD_SWA = H * P, 64
ML_SCALE = float(P) ** -0.5
SWA_SCALE = 64.0 ** -0.5
ALPHA = 2.0 ** 0.25
LN_EPS = 1e-5
NORM_EPS = 1e-6
CAP = 15.0
NEG = -1e30
HJ = 384
assert NG * TG == NT and NTT * TOK == TG



class Steps:

    def __init__(self, eng, sem, turn=0, each=0):
        self.eng, self.sem, self.turn, self.each, self.k = eng, sem, turn, each, 0

    def __call__(self, ins):
        self.k += 1
        ins.then_inc(self.sem, 1)
        self.eng.wait_ge(self.sem, self.turn * self.each + self.k)

    def end(self):
        assert self.k == self.each, (self.sem, self.k)


class Store:

    def __init__(self, nc, ctx):
        self.nc, self.ctx = nc, ctx

    def sb(self, name, shape, dt=F32):
        return self.ctx.enter_context(self.nc.sbuf_tensor(name, shape, dt))

    def ps(self, name, shape):
        return self.ctx.enter_context(self.nc.psum_tensor(name, shape, F32))

    def sem(self, name):
        return self.nc.alloc_semaphore(name)


def gate_inputs(m):
    t = {n: m.sb(n, s) for n, s in (
        ("gi", [H * NC, C]), ("gf", [H * NC, C]), ("gi_s", [H, NS]), ("gf_s", [H, NS]),
        ("small", [H * NC, 4]), ("small_s", [H, 4]), ("m0_sb", [H, DB]))}
    t["loaded"] = m.sem("g_loaded")
    return t


def load_gates(sp, io, t):
    def get(dst, src):
        sp.dma_start(dst, src).then_inc(t["loaded"], 16)

    for i, (n, bias) in enumerate((("gi", "b_ig"), ("gf", "b_fg"))):
        get(t[n][:], bass.AP(tensor=io["gateT"].tensor, offset=i * H * NT, ap=[[NT, H], [C, NC], [1, C]]))
        get(t[n + "_s"][:], io["gateT"][i * H:i * H + H, SEQ:NT])
        get(t["small"][:, i:i + 1], bass.AP(tensor=io[bias].tensor, offset=0, ap=[[1, H], [0, NC], [1, 1]]))
        get(t["small_s"][:, i:i + 1], io[bias])
    get(t["m0_sb"][:], io["m0"])


def project(nc, io, gate_in):
    with ExitStack() as ctx:
        m = Store(nc, ctx)
        XK, XR = KD // 2, 3
        xh = m.sb("xh", [P, KD, NT], F32R)
        xl = m.sb("xl", [P, KD, NT], F32R)
        xraw = m.sb("xraw", [P, XR, XK, TG])
        graw = m.sb("graw", [P, KD, P])
        raw = m.sb("raw", [P, 2, KD, P])
        whi = m.sb("whi", [P, 2, KD, P], F32R)
        wlo = m.sb("wlo", [P, 2, KD, P], F32R)
        ghi = m.sb("ghi", [P, KD, P], F32R)
        glo = m.sb("glo", [P, KD, P], F32R)
        out = m.sb("out", [P, 2, NT])
        grow = m.sb("grow", [8, 2, TG])
        acc = [m.ps(f"acc{i}", [P, 512]) for i in range(8)]
        x_in = [m.sem(f"p_x_in{r}") for r in range(XR)]
        x_hi = m.sem("p_x_hi")
        x_split = m.sem("p_x_split")
        g_zero = m.sem("p_g_zero")
        g_in = m.sem("p_g_in")
        g_hi = m.sem("p_g_hi")
        g_split = m.sem("p_g_split")
        raw_in = [m.sem(f"p_raw_in{s}") for s in range(2)]
        hi_done = [m.sem(f"p_hi{s}") for s in range(2)]
        lo_done = [m.sem(f"p_lo{s}") for s in range(2)]
        acc_full = m.sem("p_acc_full")
        acc_free = m.sem("p_acc_free")
        out_free = [m.sem(f"p_out_free{s}") for s in range(2)]
        g_stored = [m.sem(f"p_g_stored{s}") for s in range(2)]
        table_in, ext_full, ext_ready, ext_out = (m.sem("p_" + n) for n in ("table_in", "ext_full", "ext_ready", "ext_out"))
        onehot, relb = out[0:32, 0, 0:HJ], out[0:32, 0, HJ:HJ + 8]
        outside, ext = out[0:8, 0, 2 * HJ:3 * HJ], out[0:8, 0, 3 * HJ:4 * HJ]
        ITER = NPROJ // 2
        FIRST = 3 * NG
        block = ctx.enter_context(nc.Block())

        def half(t, h):
            return t[:, h % 2 * XK:h % 2 * XK + XK, h // 2 * TG:h // 2 * TG + TG]

        @block.sync
        def _(sp):
            def load(i, s):
                sp.dma_start(raw[:, s], io["wA"][bass.ds(i * 2 + s, 1)].rearrange("a p k n -> (a p) k n")).then_inc(raw_in[s], 16)

            def load_x(h):
                sp.dma_start(xraw[:, h % XR], io["xT"][h // 2, :, h % 2 * XK:h % 2 * XK + XK]).then_inc(x_in[h % XR], 16)

            def store(i, s, tiles=None):
                sp.wait_ge(acc_free, tiles or (i * 2 + s + 2) * NG)
                sp.wait_ge(g_in, 16)
                sp.dma_start(io["projT"][bass.ds(i * 2 + s, 1)].rearrange("a p n -> (a p) n"),
                             out[:, s]).then_inc(out_free[s], 16)

            def store_gates(g):
                sp.wait_ge(acc_free, 3 * g + 1)
                sp.dma_start(io["gateT"][:, g * TG:g * TG + TG], grow[:, g % 2]).then_inc(g_stored[g % 2], 16)

            for dst, src in ((relb, io["rel_bias"]), (onehot, io["c_onehot"]), (outside, io["c_outside"])):
                sp.dma_start(dst, src).then_inc(table_in, 16)
            load_x(0)
            sp.wait_ge(g_zero, 1)
            sp.dma_start(graw[:, :, 0:8], io["wG"]).then_inc(g_in, 16)
            load_x(1)
            for s in range(2):
                load(0, s)
            load_x(2)
            sp.wait_ge(ext_ready, 2)
            sp.dma_start(io["ext"], ext).then_inc(ext_out, 16)
            for h in range(XR, 2 * NG):
                sp.wait_ge(x_split, h - XR + 1)
                load_x(h)
                if h >= 5 and h % 2:
                    store_gates((h - 5) // 2)
            for s in range(2):
                sp.wait_ge(lo_done[s], 1)
                load(1, s)
            for g in range(NG - 2, NG):
                store_gates(g)
            for s in range(2):
                store(0, s, FIRST)
            for s in range(2):
                sp.wait_ge(g_stored[s], (NG + 1 - s) // 2 * 16)
            load_gates(sp, io, gate_in)
            with sp.Fori(2, ITER) as i:
                for s in range(2):
                    sp.wait_ge(lo_done[s], i)
                    sp.wait_ge(g_in, 16)
                    load(i, s)
                for s in range(2):
                    store(i - 1, s)
            for s in range(2):
                store(ITER - 1, s)

        @block.scalar
        def _(act):
            def round_x(h):
                act.wait_ge(x_in[h % XR], h // XR * 16 + 16)
                nc.scalar.activation(half(xh, h), xraw[:, h % XR], ACT.Copy).then_inc(x_hi, 1)

            round_x(0)
            act.wait_ge(g_in, 16)
            nc.scalar.activation(ghi[:], graw[:], ACT.Copy).then_inc(g_hi, 1)
            round_x(1)
            for s in range(2):
                act.wait_ge(raw_in[s], 16)
                nc.scalar.activation(whi[:, s], raw[:, s], ACT.Copy).then_inc(hi_done[s], 1)
            for h in range(2, 2 * NG):
                round_x(h)
            for s in range(2):
                act.wait_ge(raw_in[s], 32)
                act.wait_ge(acc_full, FIRST - 1 + s)
                nc.scalar.activation(whi[:, s], raw[:, s], ACT.Copy).then_inc(hi_done[s], 1)
            with act.Fori(2, ITER) as i:
                for s in range(2):
                    act.wait_ge(raw_in[s], i * 16 + 16)
                    act.wait_ge(acc_full, (i * 2 + s) * NG)
                    act.wait_ge(g_in, 16)
                    nc.scalar.activation(whi[:, s], raw[:, s], ACT.Copy).then_inc(hi_done[s], 1)

        @block.gpsimd
        def _(pool):
            nc.gpsimd.memset(graw[:], 0.0).then_inc(g_zero, 1)
            pool.wait_ge(g_hi, 1)
            nc.gpsimd.tensor_tensor(glo[:], graw[:], ghi[:].bitcast(F32), ALU.subtract).then_inc(g_split, 1)
            with pool.Fori(0, ITER) as i:
                for s in range(2):
                    pool.wait_ge(hi_done[s], i + 1)
                    nc.gpsimd.tensor_tensor(wlo[:, s], raw[:, s], whi[:, s].bitcast(F32),
                                            ALU.subtract).then_inc(lo_done[s], 1)

        @block.tensor
        def _(pe):
            def product(bank, hi, lo, g, halves=False):
                for k in range(KD):
                    if halves and k % XK == 0:
                        pe.wait_ge(x_split, 2 * g + k // XK + 1)
                    xs = slice(g * TG, (g + 1) * TG)
                    pe.matmul(acc[bank][:, 0:TG], hi[:, k], xh[:, k, xs], start=(k == 0), stop=False)
                    pe.matmul(acc[bank][:, 0:TG], hi[:, k], xl[:, k, xs], start=False, stop=False)
                    last = pe.matmul(acc[bank][:, 0:TG], lo[:, k], xh[:, k, xs], start=False, stop=(k == KD - 1))
                last.then_inc(acc_full, 1)

            pe.wait_ge(table_in, 48)
            pe.matmul(acc[0][0:8, 0:HJ], relb, onehot, start=True, stop=True).then_inc(ext_full, 1)
            pe.wait_ge(g_split, 1)
            for g in range(NG):
                for j, (hi, lo) in enumerate(((ghi, glo), *((whi[:, s], wlo[:, s]) for s in range(2)))):
                    t = 3 * g + j
                    if g == 0 and j:
                        pe.wait_ge(lo_done[j - 1], 1)
                    if t >= 6:
                        pe.wait_ge(acc_free, t - 5)
                    product(2 + t % 6, hi, lo, g, halves=(j == 0))
            with pe.Fori(1, ITER) as i:
                for s in range(2):
                    pe.wait_ge(lo_done[s], i + 1)
                    for g in range(NG):
                        n = s * NG + g
                        pe.wait_ge(acc_free, i * (2 * NG) + NG + n - 1)
                        product((n + NG) % 2, whi[:, s], wlo[:, s], g)

        @block.vector
        def _(dve):
            def split_x(h):
                dve.wait_ge(x_hi, h + 1)
                nc.vector.tensor_tensor(half(xl, h), xraw[:, h % XR], half(xh, h).bitcast(F32),
                                        ALU.subtract).then_inc(x_split, 1)

            for s in range(2):
                dve.sem_inc(out_free[s], 16)
            dve.wait_ge(ext_full, 1)
            dve.wait_ge(table_in, 48)
            nc.vector.tensor_copy(ext, acc[0][0:8, 0:HJ]).then_inc(ext_ready, 1)
            dve.wait_ge(ext_ready, 1)
            nc.vector.tensor_tensor(ext, ext, outside, ALU.add).then_inc(ext_ready, 1)
            split_x(0)
            split_x(1)
            for g in range(NG):
                if g < NG - 1:
                    split_x(2 * g + 2)
                    split_x(2 * g + 3)
                for j in range(3):
                    t = 3 * g + j
                    if j == 0 and g >= 2:
                        dve.wait_ge(g_stored[g % 2], g // 2 * 16)
                    dve.wait_ge(acc_full, t + 1)
                    if j == 0:
                        nc.vector.tensor_copy(grow[:, g % 2], acc[2 + t % 6][0:8, 0:TG]).then_inc(acc_free, 1)
                    else:
                        if t == 1:
                            dve.wait_ge(ext_out, 16)
                        nc.vector.tensor_copy(out[:, j - 1, g * TG:(g + 1) * TG], acc[2 + t % 6][:, 0:TG]).then_inc(acc_free, 1)
            with dve.Fori(1, ITER) as i:
                for s in range(2):
                    dve.wait_ge(out_free[s], i * 16 + 16)
                    for g in range(NG):
                        n = s * NG + g
                        dve.wait_ge(acc_full, i * (2 * NG) + NG + n + 1)
                        nc.vector.tensor_copy(out[:, s, g * TG:(g + 1) * TG],
                                                     acc[(n + NG) % 2][:, 0:TG]).then_inc(acc_free, 1)
    return out_free


def prompt_inputs(m):
    return {
        "inp": m.sb("inp", [P, 2, 20, C]),
        "kwin": m.sb("kwin", [P, 2, 2 * W]),
        "svT": m.sb("svT", [P, 2, W]),
        "xs": m.sb("xs_b", [P, 2, H, 2, C]),
        "loaded": [m.sem(f"c_loaded{s}") for s in range(2)],
    }


def load_tokens(sp, io, t, c, s):
    tok = bass.ds(c * C, C)
    sp.dma_start(t["inp"][:, s], io["projT"][0:20, :, tok].rearrange("t p n -> p t n")).then_inc(t["loaded"][s], 16)
    sp.dma_start(t["kwin"][:, s], bass.AP(tensor=io["projT"].tensor, offset=SK * P * NT - W + c * C,
                                          ap=[[NT, P], [1, 2 * W]])).then_inc(t["loaded"][s], 16)
    sp.dma_start(t["svT"][:, s], io["projT"][SV, :, tok]).then_inc(t["loaded"][s], 16)


def load_rows(sp, io, t, c, s):
    sp.dma_start(t["xs"][:, s].rearrange("p h w n -> p (h w) n"),
                 bass.AP(tensor=io["xsT"].tensor, offset=c * C, ap=[[0, P], [NT, 2 * H], [1, C]])).then_inc(t["loaded"][s], 16)


def gates(nc, io, keep, gate_in, first, proj_out):
    cols, bias, bias_prev, ident = keep["cols"], keep["bias"], keep["bias_prev"], keep["ident"]
    R = H * NC
    with ExitStack() as ctx:
        m = Store(nc, ctx)
        tile = lambda n: (m.sb(n, [R, C]), m.sb(n + "_s", [H, NS]))
        gi, gf, gis, gfs, small, small_s, m0, loaded = (
            gate_in[n] for n in ("gi", "gf", "gi_s", "gf_s", "small", "small_s", "m0_sb", "loaded"))
        b, b_s = tile("b")
        run, runs = tile("run")
        u, us = tile("u")
        em, ems = tile("em")
        own = m.sb("own", [R, C])
        xs, xss = m.sb("xs", [R, 2, C]), m.sb("xss", [H, 2, NS])
        ones = m.sb("ones_r", [R, C])
        m_last = m.sb("m_last", [H, DB])
        m_end = m.sb("m_end", [1, H])
        ends = m.sb("ends", [1, 2, H, NC])
        after = m.sb("after", [1, H, NC])
        before = m.sb("before", [1, H, NC])
        inherited = m.sb("inherited", [R, 1])
        anti = m.sb("anti", [P, P])
        hank = m.sb("hank", [P, 8, 2 * W])
        srow = m.sb("srow", [32, 132])
        repl = m.sb("repl", [32, P])
        srow_all = m.sb("srow_all", [P, 132])
        smask = m.sb("smask", [P, 2, NS])
        ps = m.ps("ps", [P, 4, 512])
        pw = m.ps("srow_ps", [P, 512])
        pt = m.ps("pt", [P, 512])
        pe_row = m.ps("rows_ps", [P, 512])
        table_in = m.sem("g_table_in")
        dve_s, act_s, pe_s, pool_s = m.sem("g_dve"), m.sem("g_act"), m.sem("g_pe"), m.sem("g_pool")
        stored = m.sem("g_stored")
        ext_in = m.sem("g_ext_in")
        block = ctx.enter_context(nc.Block())
        CAPPED_BIAS, ONE_MORE, OWN, BEFORE, MAXIMA, EXPONENTS, U, SAMPLE_X = 2, 4, 10, 15, 17, 19, 20, 37
        SIGMOIDS, LOGS, SCALES, SROWS = 6, 8, 12, 13
        ENDS, INHERITED, SROW, HANK, COLUMNS = 1, 2, 3, 4, 8

        @block.sync
        def _(sp):
            sp.dma_start(ident[:], io["c_ident"]).then_inc(keep["ident_in"], 16)
            for s in range(2):
                sp.wait_ge(proj_out[s], 16 * (NPROJ // 2 + 1))
            for dst, src in ((anti[:], io["c_anti"]), (repl[:], io["c_repl"]), (smask[:], io["c_smask"])):
                sp.dma_start(dst, src).then_inc(table_in, 16)
            e = io["ext"].tensor
            sp.dma_start(hank[:], bass.AP(tensor=e, offset=0, ap=[[1, P], [HJ, 8], [1, 2 * W]])).then_inc(ext_in, 16)
            for g in range(2):
                for t in range(DT):
                    sp.dma_start(srow[g * 16 + t * J:g * 16 + t * J + J, :],
                                 bass.AP(tensor=e, offset=g * J * HJ + 127 - t, ap=[[HJ, J], [1, 132]])).then_inc(ext_in, 16)
            load_tokens(sp, io, first, 0, 0)
            sp.wait_ge(act_s, SCALES)
            for w in range(2):
                sp.dma_start(bass.AP(tensor=io["xsT"].tensor, offset=w * NT, ap=[[2 * NT, H], [C, NC], [1, C]]), xs[:, w]).then_inc(stored, 16)
            sp.dma_start(io["xsT"][:, :, SEQ:NT], xss[:]).then_inc(stored, 16)
            sp.wait_ge(dve_s, U + 1)
            sp.dma_start(io["p_m"].rearrange("h a -> a h"), m_end[:]).then_inc(stored, 16)
            sp.dma_start(io["s_m"], m_last[:]).then_inc(stored, 16)
            sp.wait_ge(stored, 80)
            load_rows(sp, io, first, 0, 0)
            load_tokens(sp, io, first, 1, 1)
            load_rows(sp, io, first, 1, 1)

        @block.gpsimd
        def _(pool):
            nc.gpsimd.memset(ones[:], 1.0).then_inc(pool_s, 1)
            nc.gpsimd.memset(before[:], 0.0).then_inc(pool_s, 1)
            nc.gpsimd.memset(bias[:, :, 0:W], NEG).then_inc(pool_s, 1)
            pool.wait_ge(table_in, 16 * 3)
            pool.wait_ge(act_s, SROWS)
            sb = keep["sbias"]
            nc.gpsimd.tensor_copy(sb[:, :, 0:P], srow_all[:, 0:P].unsqueeze(1).broadcast_to([P, 2, P])).then_inc(pool_s, 1)
            for half in range(2):
                nc.gpsimd.tensor_tensor(sb[:, half, P:].rearrange("p (b t) -> p b t", t=DT),
                                        smask[:, half].rearrange("p (b t) -> p b t", t=DT),
                                        srow_all[:, P:132].unsqueeze(1).broadcast_to([P, DB, DT]), ALU.add).then_inc(pool_s, 1)

        @block.scalar
        def _(act):
            a = Steps(act, act_s)
            act.wait_ge(dve_s, CAPPED_BIAS)
            for t, small_t, i in ((gi, small, 2), (gf, small, 3), (gis, small_s, 2), (gfs, small_s, 3)):
                a(nc.scalar.activation(t[:], t[:], ACT.Tanh, scale=1 / CAP, bias=small_t[:, i:i + 1]))
            a(nc.scalar.activation(gf[:], gf[:], ACT.Exp, scale=-CAP))
            a(nc.scalar.activation(gfs[:], gfs[:], ACT.Exp, scale=-CAP))
            assert a.k == SIGMOIDS
            act.wait_ge(dve_s, ONE_MORE)
            a(nc.scalar.activation(gf[:], gf[:], ACT.Ln))
            a(nc.scalar.activation(gfs[:], gfs[:], ACT.Ln))
            assert a.k == LOGS
            act.wait_ge(dve_s, MAXIMA)
            a(nc.scalar.activation(em[:], run[:], ACT.Exp, scale=-1.0))
            act.wait_ge(dve_s, EXPONENTS)
            a(nc.scalar.activation(xs[:, 1], xs[:, 1], ACT.Exp))
            act.wait_ge(dve_s, SAMPLE_X)
            a(nc.scalar.activation(xss[:, 1], xss[:, 1], ACT.Exp))
            a(nc.scalar.activation(ems[:], runs[:], ACT.Exp, scale=-1.0))
            assert a.k == SCALES
            act.wait_ge(pe_s, SROW)
            a(nc.scalar.activation(srow_all[:], pw[:, 0:132], ACT.Copy))
            assert a.k == SROWS
            for i in range(4):
                act.wait_ge(pe_s, HANK + i)
                src = ps[:, i, :].rearrange("p (h k) -> p h k", k=2 * W)
                a(nc.scalar.activation(bias_prev[:, 2 * i:2 * i + 2], src[:, :, 0:W], ACT.Copy))
                a(nc.scalar.activation(bias[:, 2 * i:2 * i + 2, W:2 * W], src[:, :, W:2 * W], ACT.Copy))

        @block.vector
        def _(dve):
            v = Steps(dve, dve_s)
            dve.wait_ge(loaded, 16 * 9)
            v(nc.vector.tensor_scalar(small[:, 2:4], small[:, 0:2], 1 / CAP, None, ALU.mult))
            v(nc.vector.tensor_scalar(small_s[:, 2:4], small_s[:, 0:2], 1 / CAP, None, ALU.mult))
            assert v.k == CAPPED_BIAS
            dve.wait_ge(act_s, SIGMOIDS)
            v(nc.vector.tensor_scalar(gf[:], gf[:], 1.0, None, ALU.add))
            v(nc.vector.tensor_scalar(gfs[:], gfs[:], 1.0, None, ALU.add))
            assert v.k == ONE_MORE
            dve.wait_ge(act_s, LOGS)
            v(nc.vector.tensor_scalar(gf[:], gf[:], -1.0, None, ALU.mult))
            v(nc.vector.tensor_scalar(gfs[:], gfs[:], -1.0, None, ALU.mult))
            v(nc.vector.tensor_scalar(gi[:], gi[:], CAP, None, ALU.mult))
            v(nc.vector.tensor_scalar(gis[:], gis[:], CAP, None, ALU.mult))
            dve.wait_ge(pool_s, 3)
            v(nc.vector.tensor_tensor_scan(b[:], ones[:], gf[:], 0.0, ALU.mult, ALU.add))
            v(nc.vector.tensor_tensor_scan(own[:], gf[:], gi[:], NEG, ALU.add, ALU.max))
            assert v.k == OWN
            dve.wait_ge(pe_s, ENDS)
            v(nc.vector.tensor_copy(ends[:].rearrange("a w h c -> a (w h c)"), pe_row[0:1, 0:2 * R]))
            v(nc.vector.tensor_tensor(ends[:, 1, :, 0], ends[:, 1, :, 0], ends[:, 0, :, 0], ALU.max))
            v(nc.vector.memset(ends[:, 0, :, 0], NEG))
            v(nc.vector.tensor_tensor_scan(after[:].rearrange("a h c -> a (h c)"), ends[:, 0].rearrange("a h c -> a (h c)"),
                                           ends[:, 1].rearrange("a h c -> a (h c)"), 0.0, ALU.add, ALU.max))
            v(nc.vector.tensor_copy(before[:, :, 1:NC], after[:, :, 0:NC - 1]))
            assert v.k == BEFORE
            dve.wait_ge(pe_s, INHERITED)
            v(nc.vector.tensor_copy(inherited[:], pe_row[0:R, 256:257]))
            v(nc.vector.scalar_tensor_tensor(run[:], b[:], inherited[:, 0:1], own[:], ALU.add, ALU.max))
            assert v.k == MAXIMA
            v(nc.vector.tensor_tensor(xs[:, 0], b[:], run[:], ALU.subtract))
            v(nc.vector.tensor_scalar(xs[:, 1], xs[:, 0], inherited[:, 0:1], None, ALU.add))
            assert v.k == EXPONENTS
            v(nc.vector.tensor_tensor(u[:], gi[:], b[:], ALU.subtract))
            assert v.k == U
            v(nc.vector.tensor_copy(m_end[:], after[:, :, NC - 1]))
            at = lambda r, t: r[:, t:NS:DT]
            v(nc.vector.tensor_copy(at(b_s, 0), at(gfs, 0)))
            for t in range(1, DT):
                v(nc.vector.tensor_tensor(at(b_s, t), at(b_s, t - 1), at(gfs, t), ALU.add))
            for t in range(DT):
                v(nc.vector.tensor_tensor(at(runs, t), m0[:] if t == 0 else at(runs, t - 1), at(gfs, t), ALU.add))
                v(nc.vector.tensor_tensor(at(runs, t), at(runs, t), at(gis, t), ALU.max))
            v(nc.vector.tensor_tensor(xss[:, 0], b_s[:], runs[:], ALU.subtract))
            v(nc.vector.tensor_copy(m_last[:], at(runs, DT - 1)))
            v(nc.vector.tensor_tensor(xss[:, 1].rearrange("h (c t) -> h c t", t=DT),
                                      xss[:, 0].rearrange("h (c t) -> h c t", t=DT),
                                      m0[:].unsqueeze(2).broadcast_to([H, DB, DT]), ALU.add))
            v(nc.vector.tensor_tensor(us[:], gis[:], b_s[:], ALU.subtract))
            assert v.k == SAMPLE_X
            dve.wait_ge(pe_s, COLUMNS)
            for i in range(2):
                v(nc.vector.tensor_copy(cols[:, 0:NC, 32 * i:32 * i + H], pt[:, i * R:i * R + R].rearrange("p (h c) -> p c h", c=NC)))
                v(nc.vector.tensor_copy(cols[0:NS, NC, 32 * i:32 * i + H], pt[0:NS, 2 * R + i * H:2 * R + i * H + H]))

        @block.tensor
        def _(pe):
            q = lambda ins: ins.then_inc(pe_s, 1)
            pe.wait_ge(keep["ident_in"], 16)
            pe.wait_ge(dve_s, OWN)
            for i, t in enumerate((b, own)):
                last = pe.transpose(pe_row[0:1, i * R:i * R + R], t[:, C - 1:C], ident[0:R, 0:R])
            q(last)
            pe.wait_ge(dve_s, BEFORE)
            q(pe.transpose(pe_row[0:R, 256:257], before[:].rearrange("a h c -> a (h c)"), ident[0:1, 0:1]))
            pe.wait_ge(table_in, 16 * 3)
            pe.wait_ge(ext_in, 16 * 9)
            q(pe.matmul(pw[:, 0:132], repl[:], srow[:], start=True, stop=True))
            for i in range(4):
                q(pe.matmul(ps[:, i, :], anti[:], hank[:, 2 * i:2 * i + 2, :], start=True, stop=True))
            pe.wait_ge(act_s, SCALES)
            pe.wait_ge(dve_s, SAMPLE_X)
            for i, (t, ts) in enumerate(((u, us), (em, ems))):
                pe.transpose(pt[:, i * R:i * R + R], t[:], ident[0:R, 0:R])
                last = pe.transpose(pt[0:NS, 2 * R + i * H:2 * R + i * H + H], ts[:], ident[0:H, 0:H])
            q(last)


def prompt_outputs(m):
    return {
        "state": m.sb("state", [P, H, P + 1]),
        "nlast": m.sb("nlast", [P, H]),
        "mix": m.sb("mixed", [P, 2, 8, C]),
        "mix_out": [m.sem(f"c_mix_out{s}") for s in range(2)],
        "kv_out": m.sem("c_kv_out"), "st_out": m.sem("c_st_out"),
    }


def prompt(nc, io, keep, first, taken, outs):
    cols, bias, bias_prev, ident = keep["cols"], keep["bias"], keep["bias_prev"], keep["ident"]
    with ExitStack() as ctx:
        m = Store(nc, ctx)
        state, nlast, mix, mix_out, kv_out, st_out = (outs[n] for n in ("state", "nlast", "mix", "mix_out", "kv_out", "st_out"))
        inp, kwin, svT, xs, loaded = (first[n] for n in ("inp", "kwin", "svT", "xs", "loaded"))
        causal = m.sb("causal", [P, C])
        ones = m.sb("ones", [P, 1])
        sinks = m.sb("sinks", [P, 8])
        gml = m.sb("gml", [P, H])
        expo = m.sb("expo", [P, H, C])
        decay = m.sb("decay", [P, H, C])
        qs = m.sb("qs", [P, H, C])
        prob = m.sb("prob", [P, H, C])
        kw = m.sb("kw", [P, H, P])
        vaug = m.sb("vaug", [P, H, P + 1])
        den = m.sb("den", [P, H])
        ucol = m.sb("ucol", [P, 2, H])
        rec = m.sb("rec", [P, H])
        ssq = m.sb("ssq", [P, H])
        root = m.sb("root", [P, H])
        hn = m.sb("hn", [P, H, P])
        gate = m.sb("gate", [P, H, C])
        sq8 = m.sb("sq8", [P, J, C])
        vs = m.sb("vs", [P, 2, P])
        sw = m.sb("sw", [P, 2, 2, 2 * W])
        pw = m.sb("pw", [P, 2, 2, 2 * W])
        nmx = m.sb("nmx", [P, 8])
        mx = m.sb("mx", [P, 8])
        psums = m.sb("psums", [P, 2, 8])
        snk = m.sb("snk", [P, 8])
        ptw = m.sb("ptw", [P, 2, 4, W])
        ow = m.sb("ow", [P, 4, P])
        m0, m3 = m.ps("m0b", [P, 512]), m.ps("m3b", [P, 512])
        m12 = m.ps("m12", [P, 2, 512])
        w01 = m.ps("w01", [P, 2, 512])
        w2, w3 = m.ps("w2b", [P, 512]), m.ps("w3b", [P, 512])
        heads_out = m12[:, :, 0:258].rearrange("p b (h e) -> p b h e", e=P + 1)

        const_in, zeroed, fence = m.sem("c_const"), m.sem("c_zeroed"), m.sem("c_fence")
        names = ("k_turned v_turned scores sv_turned win out_ml state_up p_turned swa_out h_turned o_turned "
                 "e_ready qs_ready sv_ready nmx_ready p_ready kw_ready st_ready den_ready hn_ready ml_mixed "
                 "ow_ready msq_ready snk_arg sq_ready v_copied d_exp tanh_ready p_exp pt_copied ssq_ready root_ready snk_exp "
                 "u_ready gate_sum gate_ready bias_whole swa_mixed").split()
        S = {n: m.sem("c_" + n) for n in names}
        each = dict.fromkeys(names, 1) | dict.fromkeys(("win", "p_turned", "nmx_ready", "p_exp", "pt_copied"), 4)
        dve_s = m.sem("c_dve")
        DVE_STEPS = 13
        AHEAD = 2

        def wait(eng, name, c, k=1):
            eng.wait_ge(S[name], c * each[name] + k + 1)

        block = ctx.enter_context(nc.Block())

        @block.sync
        def _(sp):
            def load(c, s):
                load_tokens(sp, io, first, c, s)
                load_rows(sp, io, first, c, s)

            def store(c, s):
                sp.dma_start(io["mixT"][:, :, bass.ds(c * C, C)].rearrange("t p n -> p t n"), mix[:, s]).then_inc(mix_out[s], 16)

            for dst, src in ((causal[:], io["c_causal"]), (sinks[:], bass.AP(tensor=io["sinks"].tensor, offset=0, ap=[[0, P], [1, 8]])), (gml[:], io["g_ml"])):
                sp.dma_start(dst, src).then_inc(const_in, 16)
            load_sample(sp, io, taken)
            sp.dma_start(io["p_k"], io["projT"][SK, :, SEQ - W:SEQ]).then_inc(kv_out, 16)
            sp.dma_start(io["p_v"], io["projT"][SV, :, SEQ - W:SEQ]).then_inc(kv_out, 16)
            with sp.Fori(0, NC // 2 - 1) as i:
                for s in range(2):
                    wait(sp, "st_ready", 2 * i + s)
                    wait(sp, "tanh_ready", 2 * i + s)
                    sp.wait_ge(const_in, 48)
                    load(2 * i + 2 + s, s)
                    wait(sp, "ml_mixed", 2 * i + s)
                    wait(sp, "swa_mixed", 2 * i + s)
                    sp.wait_ge(const_in, 48)
                    store(2 * i + s, s)
            for s in range(2):
                wait(sp, "ml_mixed", NC - 2 + s)
                wait(sp, "swa_mixed", NC - 2 + s)
                store(NC - 2 + s, s)
            sp.wait_ge(dve_s, NC * DVE_STEPS + AHEAD + 1)
            sp.dma_start(io["p_C"], state[:, :, 0:P]).then_inc(st_out, 16)
            sp.dma_start(io["p_n"], nlast[:]).then_inc(st_out, 16)

        @block.gpsimd
        def _(pool):
            nc.gpsimd.memset(state[:], 0.0).then_inc(zeroed, 1)
            nc.gpsimd.memset(vs[:], 0.0).then_inc(zeroed, 1)
            nc.gpsimd.memset(vaug[:], 1.0).then_inc(zeroed, 1)
            nc.gpsimd.memset(ones[:], 1.0).then_inc(zeroed, 1)
            for n in names:
                pool.sem_inc(S[n], 1)
            for s in range(2):
                pool.sem_inc(mix_out[s], 16)
            pool.wait_ge(const_in, 48)
            pool.wait_ge(zeroed, 4)

            def chunk(i, s):
                c = 2 * i + s
                pool.wait_ge(loaded[s], i * 64 + 64)
                wait(pool, "d_exp", c, 0)
                nc.gpsimd.tensor_tensor(expo[:], xs[:, s, :, 0], causal[:].unsqueeze(1).broadcast_to([P, H, C]),
                                        ALU.add).then_inc(S["e_ready"], 1)
                wait(pool, "out_ml", c, 0)
                nc.gpsimd.tensor_tensor(qs[:], inp[:, s, MQ:MQ + 4], xs[:, s, :, 1], ALU.mult).then_inc(S["qs_ready"], 1)
                wait(pool, "tanh_ready", c)
                nc.gpsimd.tensor_tensor(gate[:], gate[:], ones[:].unsqueeze(2).broadcast_to([P, H, C]), ALU.add).then_inc(S["gate_sum"], 1)
                wait(pool, "gate_sum", c)
                nc.gpsimd.tensor_tensor(gate[:], gate[:], gml[:].unsqueeze(2).broadcast_to([P, H, C]),
                                        ALU.mult).then_inc(S["gate_ready"], 1)

            for s in range(2):
                chunk(0, s)
                if s == 0:
                    wait(pool, "nmx_ready", 0, 4)
                    nc.gpsimd.tensor_copy(bias[:, :, 0:W], bias_prev[:]).then_inc(S["bias_whole"], 1)
            with pool.Fori(1, NC // 2) as i:
                for s in range(2):
                    chunk(i, s)

        @block.tensor
        def _(pe):
            def window_scores(c, s, r):
                wait(pe, "nmx_ready", c, r)
                for g in range(2):
                    gp = slice(64 * g, 64 * g + 64)
                    for a in range(2):
                        last = pe.matmul(w01[:, g, a * 256:a * 256 + 256], sq8[gp, r + a], kwin[gp, s],
                                         start=True, stop=True)
                    last.then_inc(S["win"], 1)

            def turn_window(c, r, bank):
                wait(pe, "p_exp", c, r + 1)
                for g in range(2):
                    for half in range(2):
                        last = pe.transpose(bank[:, (2 * g + half) * W:(2 * g + half + 1) * W],
                                            pw[:, r % 2, g, half * W:half * W + W], ident[:])
                last.then_inc(S["p_turned"], 1)

            def window_values(c, s, r):
                wait(pe, "pt_copied", c, r + 1)
                for g in range(2):
                    for half in range(2):
                        last = pe.matmul(w3[:, r * P + g * 64:r * P + g * 64 + 64], ptw[:, r % 2, 2 * g + half],
                                         vs[:, s if half else 1 - s, g * 64:g * 64 + 64],
                                         start=(half == 0), stop=(half == 1))
                return last

            def turn_keys(c, s):
                for h in range(H):
                    last = pe.transpose(m0[:, h * C:h * C + C], inp[:, s, MK + h], ident[:])
                last.then_inc(S["k_turned"], 1)

            def chunk(i, s, more):
                c = 2 * i + s
                q, k, v = inp[:, s, MQ:MQ + 4], inp[:, s, MK:MK + 4], inp[:, s, MV:MV + 4]
                wait(pe, "hn_ready", c, 0)
                for h in range(H):
                    last = pe.transpose(m12[:, 0, h * C:h * C + C], v[:, h], ident[:])
                last.then_inc(S["v_turned"], 1)
                for h in range(H):
                    last = pe.matmul(m12[:, 1, h * C:h * C + C], k[:, h], q[:, h], start=True, stop=True)
                last.then_inc(S["scores"], 1)
                wait(pe, "ow_ready", c, 0)
                pe.transpose(w3[:, 0:P], svT[:, s], ident[:]).then_inc(S["sv_turned"], 1)
                wait(pe, "swa_mixed", c, 0)
                turn_window(c, 0, w2)
                wait(pe, "ml_mixed", c, 0)
                turn_window(c, 1, m3)
                window_scores(c, s, 2)
                wait(pe, "p_ready", c)
                wait(pe, "v_copied", c)
                wait(pe, "qs_ready", c)
                for h in range(H):
                    pe.matmul(heads_out[:, h // 2, h % 2], prob[:, h], vaug[:, h], start=True, stop=False)
                    last = pe.matmul(heads_out[:, h // 2, h % 2], qs[:, h], state[:, h], start=False, stop=True)
                last.then_inc(S["out_ml"], 1)
                wait(pe, "kw_ready", c)
                wait(pe, "pt_copied", c, 2)
                for h in range(H):
                    last = pe.matmul((m3, m0)[h // 2][:, (h % 2) * 129:(h % 2) * 129 + 129], kw[:, h], vaug[:, h],
                                     start=True, stop=True)
                last.then_inc(S["state_up"], 1)
                wait(pe, "sv_ready", c)
                window_values(c, s, 0)
                turn_window(c, 2, w2)
                window_values(c, s, 1)
                wait(pe, "pt_copied", c, 3)
                turn_window(c, 3, w2)
                if more:
                    pe.wait_ge(loaded[1 - s], (i + s) * 64 + 64)
                    wait(pe, "sq_ready", c + 1)
                    window_scores(c + 1, 1 - s, 0)
                window_values(c, s, 2)
                window_values(c, s, 3).then_inc(S["swa_out"], 1)
                wait(pe, "st_ready", c)
                if more:
                    turn_keys(c + 1, 1 - s)
                wait(pe, "hn_ready", c)
                for h in range(H):
                    last = pe.transpose(m3[:, h * C:h * C + C], hn[:, h], ident[:])
                last.then_inc(S["h_turned"], 1)
                wait(pe, "ow_ready", c)
                for r in range(J):
                    last = pe.transpose(w2[:, r * C:r * C + C], ow[:, r], ident[:])
                last.then_inc(S["o_turned"], 1)

            pe.wait_ge(zeroed, 4)
            pe.wait_ge(loaded[0], 64)
            turn_keys(0, 0)
            wait(pe, "sq_ready", 0)
            window_scores(0, 0, 0)
            with pe.Fori(0, NC // 2 - 1) as i:
                for s in range(2):
                    chunk(i, s, True)
            for s in range(2):
                chunk(NC // 2 - 1, s, s == 0)

        @block.scalar
        def _(act):
            def window_exp(c, s, r):
                wait(act, "nmx_ready", c, r + 1)
                for g in range(2):
                    a = 2 * r + g
                    last = nc.scalar.activation(pw[:, r % 2, g], sw[:, r % 2, g], ACT.Exp, bias=nmx[:, a:a + 1],
                                                accum_out=psums[:, s, a:a + 1])
                last.then_inc(S["p_exp"], 1)

            def copy_turned(c, r):
                wait(act, "p_turned", c, r + 1)
                nc.scalar.activation(ptw[:, r % 2].rearrange("p a q -> p (a q)"), (m3 if r == 1 else w2)[:], ACT.Copy).then_inc(S["pt_copied"], 1)

            def scale_queries(s):
                nc.scalar.activation(sq8[:], inp[:, s, SQ:SQ + 4], ACT.Copy, scale=SWA_SCALE).then_inc(S["sq_ready"], 1)

            def chunk(i, s, more):
                c = 2 * i + s
                wait(act, "e_ready", c)
                wait(act, "u_ready", c)
                wait(act, "kw_ready", c, 0)
                for h in range(H):
                    last = nc.scalar.activation(decay[:, h], expo[:, h], ACT.Exp, bias=ucol[:, s, h:h + 1])
                last.then_inc(S["d_exp"], 1)
                wait(act, "v_turned", c)
                nc.scalar.activation(vaug[:, :, 0:P], m12[:, 0].rearrange("p (h e) -> p h e", e=P), ACT.Copy).then_inc(S["v_copied"], 1)
                copy_turned(c, 0)
                copy_turned(c, 1)
                wait(act, "ml_mixed", c, 0)
                nc.scalar.activation(gate[:], inp[:, s, MO:MO + 4], ACT.Tanh, scale=0.5).then_inc(S["tanh_ready"], 1)
                window_exp(c, s, 2)
                window_exp(c, s, 3)
                if more:
                    act.wait_ge(loaded[1 - s], (i + s) * 64 + 64)
                    wait(act, "win", c, 4)
                    scale_queries(1 - s)
                copy_turned(c, 2)
                wait(act, "h_turned", c, 0)
                wait(act, "den_ready", c)
                for h in range(H):
                    last = nc.scalar.activation(hn[:, h], heads_out[:, h // 2, h % 2, 0:P], ACT.Square,
                                                accum_out=ssq[:, h:h + 1])
                last.then_inc(S["ssq_ready"], 1)
                copy_turned(c, 3)
                wait(act, "msq_ready", c)
                nc.scalar.activation(root[:], root[:], ACT.Sqrt).then_inc(S["root_ready"], 1)
                wait(act, "snk_arg", c)
                nc.scalar.activation(snk[:], snk[:], ACT.Exp).then_inc(S["snk_exp"], 1)
                act.wait_ge(mix_out[s], i * 16 + 16)
                wait(act, "o_turned", c)
                nc.scalar.activation(mix[:, s, 4:8].rearrange("p h t -> p (h t)"), w2[:], ACT.Copy).then_inc(S["swa_mixed"], 1)
                if more:
                    window_exp(c + 1, 1 - s, 0)
                    window_exp(c + 1, 1 - s, 1)

            act.wait_ge(loaded[0], 64)
            scale_queries(0)
            window_exp(0, 0, 0)
            window_exp(0, 0, 1)
            with act.Fori(0, NC // 2 - 1) as i:
                for s in range(2):
                    chunk(i, s, True)
            for s in range(2):
                chunk(NC // 2 - 1, s, s == 0)

        @block.vector
        def _(dve):
            def window_max(v, c, r, first=False):
                wait(dve, "win", c, 2 * (r // 2) + 2)
                if not first:
                    wait(dve, "p_exp", c, r - 1)
                dve.sem_inc(fence, 1)
                for g in range(2):
                    a, hd = 2 * r + g, g * J + r
                    last = nc.vector.tensor_tensor_reduce(
                        sw[:, r % 2, g], w01[:, g, (r % 2) * 256:(r % 2) * 256 + 256], bias[:, hd], 1.0,
                        sinks[:, a:a + 1], ALU.add, ALU.max, mx[:, a:a + 1])
                v(last)
                nc.vector.tensor_scalar(nmx[:, 2 * r:2 * r + 2], mx[:, 2 * r:2 * r + 2], -1.0, None,
                                        ALU.mult).then_inc(S["nmx_ready"], 1)

            def chunk(i, s, more):
                c = 2 * i + s
                v = Steps(dve, dve_s, c, DVE_STEPS)
                v.k = AHEAD
                emcol = cols[:, bass.ds(c, 1), 32:32 + H]
                sc_b = xs[:, s, :, 1]
                dve.wait_ge(loaded[s], i * 64 + 64)
                wait(dve, "d_exp", c, 0)
                nc.vector.tensor_copy(ucol[:, s].unsqueeze(1), cols[:, bass.ds(c, 1), 0:H]).then_inc(S["u_ready"], 1)
                wait(dve, "sv_turned", c)
                nc.vector.tensor_copy(vs[:, s], w3[:, 0:P]).then_inc(S["sv_ready"], 1)
                wait(dve, "d_exp", c)
                wait(dve, "scores", c)
                nc.vector.scalar_tensor_tensor(prob[:].rearrange("p h t -> p (h t)"), m12[:, 1], ML_SCALE,
                                               decay[:].rearrange("p h t -> p (h t)"), ALU.mult, ALU.mult).then_inc(S["p_ready"], 1)
                wait(dve, "k_turned", c)
                nc.vector.scalar_tensor_tensor(kw[:], m0[:].rearrange("p (h e) -> p h e", e=P), ML_SCALE,
                                               decay[:, :, C - 1:C].broadcast_to([P, H, P]), ALU.mult, ALU.mult).then_inc(S["kw_ready"], 1)
                window_max(v, c, 2)
                window_max(v, c, 3)
                wait(dve, "nmx_ready", c, 4)
                nc.vector.tensor_tensor(snk[:], sinks[:], nmx[:], ALU.add).then_inc(S["snk_arg"], 1)
                wait(dve, "out_ml", c)
                nc.vector.tensor_copy(den[:].rearrange("p (b h) -> p b h", h=2).unsqueeze(3),
                                      heads_out[:, :, :, P:P + 1]).then_inc(S["den_ready"], 1)
                wait(dve, "state_up", c)
                for h in range(H):
                    last = nc.vector.scalar_tensor_tensor(state[:, h], state[:, h], sc_b[:, h, C - 1:C],
                                                          (m3, m0)[h // 2][:, (h % 2) * 129:(h % 2) * 129 + 129],
                                                          ALU.mult, ALU.add)
                last.then_inc(S["st_ready"], 1)
                wait(dve, "den_ready", c)
                v(nc.vector.scalar_tensor_tensor(rec[:], den[:], -1.0, den[:], ALU.mult, ALU.max))
                v(nc.vector.tensor_tensor(rec[:].unsqueeze(1), rec[:].unsqueeze(1), emcol, ALU.max))
                v(nc.vector.reciprocal(rec[:], rec[:]))
                wait(dve, "ssq_ready", c)
                v(nc.vector.tensor_tensor(root[:], ssq[:], rec[:], ALU.mult))
                v(nc.vector.tensor_tensor(root[:], root[:], rec[:], ALU.mult))
                nc.vector.tensor_scalar(root[:], root[:], 1.0 / P, NORM_EPS, ALU.mult, ALU.add).then_inc(S["msq_ready"], 1)
                wait(dve, "root_ready", c)
                v(nc.vector.reciprocal(root[:], root[:]))
                v(nc.vector.tensor_tensor(rec[:], rec[:], root[:], ALU.mult))
                nc.vector.tensor_tensor(hn[:].rearrange("p (b h) e -> p b h e", h=2), heads_out[:, :, :, 0:P],
                                        rec[:].rearrange("p (b h) -> p b h", h=2).unsqueeze(3).broadcast_to([P, 2, 2, P]),
                                        ALU.mult).then_inc(S["hn_ready"], 1)
                wait(dve, "snk_exp", c)
                wait(dve, "p_exp", c, 4)
                v(nc.vector.tensor_tensor(snk[:], snk[:], psums[:, s], ALU.add))
                v(nc.vector.reciprocal(snk[:], snk[:]))
                wait(dve, "swa_out", c)
                nc.vector.tensor_tensor(ow[:].rearrange("p r (g d) -> p (r g) d", g=2), w3[:].rearrange("p (a d) -> p a d", d=64),
                                        snk[:].unsqueeze(2).broadcast_to([P, 8, 64]), ALU.mult).then_inc(S["ow_ready"], 1)
                if more:
                    wait(dve, "bias_whole", 0)
                    window_max(v, c + 1, 0)
                    window_max(v, c + 1, 1)
                dve.wait_ge(mix_out[s], i * 16 + 16)
                wait(dve, "h_turned", c)
                wait(dve, "gate_ready", c)
                nc.vector.scalar_tensor_tensor(mix[:, s, 0:4].rearrange("p h t -> p (h t)"), m3[:], 0.5,
                                               gate[:].rearrange("p h t -> p (h t)"), ALU.mult, ALU.mult).then_inc(S["ml_mixed"], 1)
                if more:
                    assert v.k == DVE_STEPS + AHEAD, v.k
                else:
                    dve.sem_inc(dve_s, AHEAD)

            dve.wait_ge(const_in, 48)
            dve.wait_ge(zeroed, 4)
            ahead = Steps(dve, dve_s)
            window_max(ahead, 0, 0, True)
            window_max(ahead, 0, 1, True)
            with dve.Fori(0, NC // 2 - 1) as i:
                for s in range(2):
                    chunk(i, s, True)
            for s in range(2):
                chunk(NC // 2 - 1, s, s == 0)
            dve.wait_ge(S["st_ready"], NC + 1)
            nc.vector.tensor_copy(nlast[:].unsqueeze(2), state[:, :, P:P + 1]).then_inc(dve_s, 1)


SAMPLE_LOADS = 12


def sample_inputs(m):
    return {
        "inp": m.sb("s_inp", [P, NPROJ, NS]), "xs": m.sb("s_xs", [P, H, 2, NS]), "state": m.sb("s_state", [P, DB * H, P + 1]),
        "n0": m.sb("s_n0", [P, DB * H]), "kc": m.sb("s_kc", [P, DB, W]), "vc": m.sb("s_vc", [P, DB, P]),
        "causal": m.sb("s_causal", [NS, NS]), "sinkcol": m.sb("s_sinkcol", [P, 1]), "gml": m.sb("s_gml", [P, H]),
        "loaded": m.sem("s_loaded"),
    }


def load_sample(sp, io, t):
    tok = slice(SEQ, NT)
    for dst, src in (
            (t["inp"][:], io["projT"][:, :, tok].rearrange("t p n -> p t n")),
            (t["xs"][:].rearrange("p h w n -> p (h w) n"),
             bass.AP(tensor=io["xsT"].tensor, offset=SEQ, ap=[[0, P], [NT, 2 * H], [1, NS]])),
            (t["causal"][:], io["c_causal_s"]), (t["sinkcol"][:], io["sink_col"]), (t["gml"][:], io["g_ml"]), (t["n0"][:], io["n0"]),
            (t["kc"][:], io["cache_kT"]), (t["vc"][:], io["cache_v"].rearrange("b k n -> k b n")),
            *((t["state"][:, q * 8:q * 8 + 8, 0:P], io["state_C"][:, q * 8:q * 8 + 8]) for q in range(4))):
        sp.dma_start(dst, src).then_inc(t["loaded"], 16)


def layer_inputs(m):
    return {
        "raw": m.sb("l_raw", [P, 2, HALF, P]), "whi": m.sb("l_whi", [P, 2, HALF, P], F32R), "wlo": m.sb("l_wlo", [P, 2, HALF, P], F32R),
        "ah": m.sb("ah", [P, KD, TG], F32R),
        "al": m.sb("al", [P, KD, TG], F32R),
        "mixr": m.sb("mixr", [P, KD, TG]),
        "nxt": m.sb("nxt", [P, KD, TG]),
        "sample_stored": m.sem("s_stored"),
        "raw_in": [m.sem(f"l_raw_in{s}") for s in range(2)],
        "S": {n: m.sem("l_" + n) for n in
              "const_in mix_in x_in hi_done lo_done slab_done evac mix_split ta_full tb_full normed root_arg root_done "
              "y_scaled x1_ready x1_hi x1_split silu_done h_hi h_split mix_hi y_ready moved".split()},
    }


def first_loads(sp, io, t):
    for s in range(2):
        sp.dma_start(t["raw"][:, s, 0:KD], io["wB"][s]).then_inc(t["raw_in"][s], 16)
    sp.dma_start(t["mixr"][:], io["mixT"][:, :, 0:TG].rearrange("t p n -> p t n")).then_inc(t["S"]["mix_in"], 16)
    sp.dma_start(t["nxt"][:], io["xT"][0]).then_inc(t["S"]["x_in"], 16)


def sample(nc, io, keep, taken, outs, ahead):
    cols, ident, sbias = keep["cols"], keep["ident"], keep["sbias"]
    with ExitStack() as ctx:
        m = Store(nc, ctx)
        inp, xs, state, n0, kc, vc, causal, sinkcol, gml = (
            taken[n] for n in ("inp", "xs", "state", "n0", "kc", "vc", "causal", "sinkcol", "gml"))
        expo = m.sb("s_expo", [NS, H, NS])
        decay = m.sb("s_decay", [NS, H, NS])
        prob = m.sb("s_prob", [NS, H, NS])
        vaug = m.sb("s_vaug", [NS, H, P + 1])
        ktok = m.sb("s_ktok", [NS, H, P])
        kw = m.sb("s_kw", [NS, DB, H, P])
        qs = m.sb("s_qs", [P, H, DB * (NS + DT)])
        qb = m.sb("s_qb", [P, DB, 2, DT, J])
        swin = m.sb("s_swin", [P, 2, W + NS])
        mx, nmx, psums, snk = (m.sb(n, [P, 2]) for n in ("s_mx", "s_nmx", "s_psums", "s_snk"))
        kvtok = m.sb("s_kvtok", [NS, 2, P])
        pt1 = m.sb("s_pt1", [P, 2, P])
        pt2 = m.sb("s_pt2", [NS, 2, P])
        den, rec, ssq, root = (m.sb(n, [NS, H]) for n in ("s_den", "s_rec", "s_ssq", "s_root"))
        sqjunk = m.sb("s_sqjunk", [NS, H, P])
        hn = m.sb("s_hn", [NS, H, P])
        gate = m.sb("s_gate", [P, H, NS])
        mix = m.sb("s_mixed", [P, 8, NS])
        kv = m.ps("s_kv", [P, 2, 512])
        upd = m.ps("s_upd", [P, 2, 512])
        ho = m.ps("s_ho", [P, 2, 512])
        sc = m.ps("s_sc", [P, 512])
        wi = m.ps("s_wi", [P, 512])
        heads_out = ho[0:NS, :, 0:258].rearrange("p b (h e) -> p b h e", e=P + 1)
        names = "zeroed v_done a_done kv_turned scores win p_turned win_out heads up h_turned".split()
        S = {n: m.sem("s_" + n) for n in names}
        block = ctx.enter_context(nc.Block())
        sig = {n: m.sem("s_v_" + n) for n in ("expo", "prob", "kw", "nmx", "snk", "wprob", "pt", "den", "msq", "hn", "state", "mixed", "tok", "qb", "qs")}

        @block.sync
        def _(sp):
            tok = slice(SEQ, NT)
            for s in range(2):
                sp.wait_ge(outs["mix_out"][s], 8 * NC + 16)
            first_loads(sp, io, ahead)
            sp.wait_ge(outs["st_out"], 32)
            sp.wait_ge(outs["kv_out"], 32)
            for a in "kv":
                sp.dma_start(io[f"s_{a}"][:, 0:W - DT], io[f"cache_{a}"][:, DT:W]).then_inc(ahead["sample_stored"], 16)
            sp.wait_ge(sig["tok"], 1)
            for i, a in enumerate("kv"):
                sp.dma_start(io[f"s_{a}"][:, W - DT:W], kvtok[:, i]).then_inc(ahead["sample_stored"], 16)
            for s in range(2):
                sp.wait_ge(ahead["S"]["lo_done"], s + 1)
                sp.dma_start(ahead["raw"][:, s, 0:KD], io["wB"][2 + s]).then_inc(ahead["raw_in"][s], 16)
            sp.wait_ge(sig["mixed"], 3)
            sp.dma_start(io["mixT"][:, :, tok].rearrange("t p n -> p t n"), mix[:]).then_inc(ahead["sample_stored"], 16)
            sp.wait_ge(sig["state"], DB + 1)
            sp.dma_start(io["s_C"], state[:, :, 0:P]).then_inc(ahead["sample_stored"], 16)
            sp.dma_start(io["s_n"], n0[:]).then_inc(ahead["sample_stored"], 16)

        @block.gpsimd
        def _(pool):
            nc.gpsimd.memset(qs[:], 0.0).then_inc(S["zeroed"], 1)
            nc.gpsimd.memset(qb[:], 0.0).then_inc(S["zeroed"], 1)
            nc.gpsimd.memset(vaug[:], 1.0).then_inc(S["zeroed"], 1)
            pool.wait_ge(S["a_done"], 2)
            pool.wait_ge(S["v_done"], 1)
            for b in range(DB):
                e = DT * b + DT - 1
                nc.gpsimd.tensor_tensor(kw[:, b], ktok[:], decay[:, :, e:e + 1].broadcast_to([NS, H, P]), ALU.mult).then_inc(sig["kw"], 1)
            L = ahead["S"]
            for s in range(2):
                pool.wait_ge(L["hi_done"], s + 1)
                nc.gpsimd.tensor_tensor(ahead["wlo"][:, s, 0:KD], ahead["raw"][:, s, 0:KD],
                                        ahead["whi"][:, s, 0:KD].bitcast(F32), ALU.subtract).then_inc(L["lo_done"], 1)
            pool.wait_ge(L["mix_hi"], 1)
            nc.gpsimd.tensor_tensor(ahead["al"][:], ahead["mixr"][:], ahead["ah"][:].bitcast(F32), ALU.subtract).then_inc(L["mix_split"], 1)

        @block.tensor
        def _(pe):
            pe.wait_ge(taken["loaded"], 16 * SAMPLE_LOADS)
            for i, a in enumerate((SK, SV)):
                last = pe.transpose(sc[0:NS, P + i * P:2 * P + i * P], inp[:, a], ident[:])
            for h in range(H):
                pe.transpose(kv[0:NS, 0, h * P:h * P + P], inp[:, MK + h], ident[:])
                last = pe.transpose(kv[0:NS, 1, h * P:h * P + P], inp[:, MV + h], ident[:])
            last.then_inc(S["kv_turned"], 1)
            for h in range(H):
                last = pe.matmul(sc[0:NS, h * NS:h * NS + NS], inp[:, MK + h], inp[:, MQ + h], start=True, stop=True)
            last.then_inc(S["scores"], 1)
            pe.wait_ge(sig["qb"], 2)
            for b in range(DB):
                half, rows = b // 4, slice(32 * (b % 4), 32 * (b % 4) + 32)
                q = qb[:, b].rearrange("p g t j -> p (g t j)")
                pe.matmul(wi[rows, half * 160:half * 160 + W], q, kc[:, b], start=True, stop=True)
                last = pe.matmul(wi[rows, half * 160 + W:half * 160 + 160], q, inp[:, SK], start=True, stop=True)
            last.then_inc(S["win"], 1)
            pe.wait_ge(sig["prob"], 2)
            pe.wait_ge(sig["qs"], 1)
            for h in range(H):
                pe.matmul(heads_out[:, h // 2, h % 2], prob[:, h], vaug[:, h], start=True, stop=False)
                for b in range(DB):
                    last = pe.matmul(heads_out[:, h // 2, h % 2], qs[:, h, b * NS:b * NS + NS], state[:, b * H + h],
                                     start=False, stop=(b == DB - 1))
            last.then_inc(S["heads"], 1)
            def update(b):
                pe.wait_ge(sig["kw"], b + 1)
                if b >= 2:
                    pe.wait_ge(sig["state"], b)
                for h in range(H):
                    last = pe.matmul((upd, kv)[b % 2][:, h // 2, (h % 2) * 129:(h % 2) * 129 + 129], kw[:, b, h], vaug[:, h],
                                     start=True, stop=True)
                last.then_inc(S["up"], 1)

            update(0)
            update(1)
            pe.wait_ge(sig["wprob"], 1)
            for half in range(2):
                pe.transpose(wi[:, half * P:half * P + P], swin[:, half, 0:W], ident[:])
                last = pe.transpose(wi[0:NS, 256 + half * P:256 + half * P + P], swin[:, half, W:W + NS], ident[:])
            last.then_inc(S["p_turned"], 1)
            pe.wait_ge(sig["pt"], 1)
            for b in range(DB):
                half, c = b // 4, slice(32 * (b % 4), 32 * (b % 4) + 32)
                pe.matmul(sc[:, b * 32:b * 32 + 32], vc[:, b], pt1[:, half, c], start=True, stop=False)
                last = pe.matmul(sc[:, b * 32:b * 32 + 32], kvtok[:, 1], pt2[:, half, c], start=False, stop=True)
            last.then_inc(S["win_out"], 1)
            pe.wait_ge(sig["hn"], 1)
            for h in range(H):
                last = pe.transpose(wi[:, h * NS:h * NS + NS], hn[:, h], ident[0:NS, 0:NS])
            last.then_inc(S["h_turned"], 1)
            for b in range(2, DB):
                update(b)

        @block.scalar
        def _(act):
            a = Steps(act, S["a_done"])
            act.wait_ge(taken["loaded"], 16 * SAMPLE_LOADS)
            a(nc.scalar.activation(gate[:], inp[:, MO:MO + 4], ACT.Tanh, scale=0.5))
            act.wait_ge(sig["expo"], 1)
            a(nc.scalar.activation(decay[:], expo[:], ACT.Exp))
            act.wait_ge(sig["nmx"], 1)
            for half in range(2):
                a(nc.scalar.activation(swin[:, half], swin[:, half], ACT.Exp, bias=nmx[:, half:half + 1],
                                       accum_out=psums[:, half:half + 1]))
            act.wait_ge(sig["snk"], 1)
            a(nc.scalar.activation(snk[:], snk[:], ACT.Exp))
            act.wait_ge(sig["den"], 1)
            for h in range(H):
                a(nc.scalar.activation(sqjunk[:, h], heads_out[:, h // 2, h % 2, 0:P], ACT.Square, accum_out=ssq[:, h:h + 1]))
            act.wait_ge(sig["msq"], 1)
            a(nc.scalar.activation(root[:], root[:], ACT.Sqrt))
            L = ahead["S"]
            for s in range(2):
                act.wait_ge(ahead["raw_in"][s], 16)
                nc.scalar.activation(ahead["whi"][:, s, 0:KD], ahead["raw"][:, s, 0:KD], ACT.Copy).then_inc(L["hi_done"], 1)
            act.wait_ge(L["mix_in"], 16)
            nc.scalar.activation(ahead["ah"][:], ahead["mixr"][:], ACT.Copy).then_inc(L["mix_hi"], 1)

        @block.vector
        def _(dve):
            v = Steps(dve, S["v_done"])
            dve.wait_ge(taken["loaded"], 16 * SAMPLE_LOADS)
            dve.wait_ge(S["zeroed"], 3)
            nc.vector.tensor_copy(state[:, :, P:P + 1], n0[:].unsqueeze(2)).then_inc(sig["state"], 1)
            for g in range(2):
                gp = slice(64 * g, 64 * g + 64)
                nc.vector.tensor_scalar(qb[gp, :, g], inp[gp, SQ:SQ + 4].rearrange("p j (b t) -> p b t j", t=DT),
                                        SWA_SCALE, None, ALU.mult).then_inc(sig["qb"], 1)
            for h in range(H):
                last = nc.vector.scalar_tensor_tensor(expo[:, h], xs[0:NS, h, 0], cols[0:NS, NC, h:h + 1], causal[:],
                                                      ALU.add, ALU.add)
            last.then_inc(sig["expo"], 1)
            for h in range(H):
                last = nc.vector.tensor_tensor(
                    qs[:, h].rearrange("p (b r) -> p b r", r=NS + DT)[:, :, 0:DT],
                    inp[:, MQ + h].rearrange("p (b t) -> p b t", t=DT), xs[:, h, 1].rearrange("p (b t) -> p b t", t=DT), ALU.mult)
            last.then_inc(sig["qs"], 1)
            dve.wait_ge(S["scores"], 1)
            nc.vector.tensor_copy(kvtok[:].rearrange("p a n -> p (a n)"), sc[0:NS, P:3 * P]).then_inc(sig["tok"], 1)
            v(nc.vector.tensor_scalar(ktok[:].rearrange("p h e -> p (h e)"), kv[0:NS, 0], ML_SCALE, None, ALU.mult))
            nc.vector.tensor_copy(vaug[:, :, 0:P], kv[0:NS, 1].rearrange("p (h e) -> p h e", e=P)).then_inc(sig["prob"], 1)
            dve.wait_ge(S["a_done"], 2)
            dve.wait_ge(S["scores"], 1)
            nc.vector.scalar_tensor_tensor(prob[:].rearrange("p h t -> p (h t)"), sc[0:NS, 0:P], ML_SCALE,
                                           decay[:].rearrange("p h t -> p (h t)"), ALU.mult, ALU.mult).then_inc(sig["prob"], 1)
            dve.wait_ge(S["win"], 1)
            v(nc.vector.tensor_tensor(swin[:].rearrange("p a k -> p (a k)"), wi[:, 0:320], sbias[:].rearrange("p a k -> p (a k)"), ALU.add))
            v(nc.vector.tensor_reduce(mx[:], swin[:], AX.X, ALU.max))
            v(nc.vector.tensor_scalar(mx[:], mx[:], sinkcol[:, 0:1], None, ALU.max))
            nc.vector.tensor_scalar(nmx[:], mx[:], -1.0, None, ALU.mult).then_inc(sig["nmx"], 1)
            dve.wait_ge(sig["nmx"], 1)
            nc.vector.tensor_scalar(snk[:], nmx[:], sinkcol[:, 0:1], None, ALU.add).then_inc(sig["snk"], 1)
            dve.wait_ge(S["heads"], 1)
            nc.vector.tensor_copy(den[:].rearrange("p (b h) -> p b h", h=2).unsqueeze(3), heads_out[:, :, :, P:P + 1]).then_inc(sig["den"], 1)
            dve.wait_ge(S["a_done"], 5)
            v(nc.vector.tensor_tensor(snk[:], snk[:], psums[:], ALU.add))
            v(nc.vector.reciprocal(snk[:], snk[:]))
            for half in range(2):
                last = nc.vector.tensor_scalar(swin[:, half], swin[:, half], snk[:, half:half + 1], None, ALU.mult)
            last.then_inc(sig["wprob"], 1)
            dve.wait_ge(sig["den"], 1)
            v(nc.vector.scalar_tensor_tensor(rec[:], den[:], -1.0, den[:], ALU.mult, ALU.max))
            v(nc.vector.tensor_tensor(rec[:], rec[:], cols[0:NS, NC, 32:32 + H], ALU.max))
            v(nc.vector.reciprocal(rec[:], rec[:]))
            dve.wait_ge(S["a_done"], 9)
            v(nc.vector.tensor_tensor(root[:], ssq[:], rec[:], ALU.mult))
            v(nc.vector.tensor_tensor(root[:], root[:], rec[:], ALU.mult))
            nc.vector.tensor_scalar(root[:], root[:], 1.0 / P, NORM_EPS, ALU.mult, ALU.add).then_inc(sig["msq"], 1)
            dve.wait_ge(S["p_turned"], 1)
            v(nc.vector.tensor_copy(pt1[:].rearrange("p a n -> p (a n)"), wi[:, 0:256]))
            nc.vector.tensor_copy(pt2[:].rearrange("p a n -> p (a n)"), wi[0:NS, 256:512]).then_inc(sig["pt"], 1)
            dve.wait_ge(S["a_done"], 10)
            v(nc.vector.reciprocal(root[:], root[:]))
            v(nc.vector.tensor_tensor(rec[:], rec[:], root[:], ALU.mult))
            nc.vector.tensor_tensor(hn[:].rearrange("p (b h) e -> p b h e", h=2), heads_out[:, :, :, 0:P],
                                    rec[:].rearrange("p (b h) -> p b h", h=2).unsqueeze(3).broadcast_to([NS, 2, 2, P]),
                                    ALU.mult).then_inc(sig["hn"], 1)
            v(nc.vector.tensor_scalar(gate[:], gate[:], 1.0, 0.5, ALU.add, ALU.mult))
            v(nc.vector.tensor_tensor(gate[:], gate[:], gml[:].unsqueeze(2).broadcast_to([P, H, NS]), ALU.mult))
            for b in range(DB):
                dve.wait_ge(S["up"], b + 1)
                for h in range(H):
                    last = nc.vector.scalar_tensor_tensor(
                        state[:, b * H + h], state[:, b * H + h], xs[:, h, 1, DT * b + DT - 1:DT * b + DT],
                        (upd, kv)[b % 2][:, h // 2, (h % 2) * 129:(h % 2) * 129 + 129], ALU.mult, ALU.add)
                if b < DB - 1:
                    last.then_inc(sig["state"], 1)
            v(last)
            nc.vector.tensor_copy(n0[:].unsqueeze(2), state[:, :, P:P + 1]).then_inc(sig["state"], 1)
            dve.wait_ge(S["win_out"], 1)
            for g in range(2):
                gp = slice(64 * g, 64 * g + 64)
                nc.vector.tensor_copy(mix[gp, 4:8].rearrange("p j (b t) -> p b t j", t=DT),
                                      sc[gp, 0:DB * 32].rearrange("p (b g t j) -> p b g t j", g=2, t=DT, j=J)[:, :, g]).then_inc(sig["mixed"], 1)
            dve.wait_ge(S["h_turned"], 1)
            nc.vector.tensor_tensor(mix[:, 0:4].rearrange("p h t -> p (h t)"), wi[:, 0:P],
                                    gate[:].rearrange("p h t -> p (h t)"), ALU.mult).then_inc(sig["mixed"], 1)


def layer(nc, io, ahead):
    OUT1, IN, OUT2 = 8, 2 * KF, 16
    FIRST = OUT1 + IN
    SLABS = OUT1 + IN + OUT2
    TILES = OUT1 + IN + 8
    HEAD = 2
    BANKS = 4
    NORMS = 2 * NTT
    with ExitStack() as ctx:
        m = Store(nc, ctx)
        raw, whi, wlo, ah, al, mixr, nxt, raw_in, S = (
            ahead[n] for n in ("raw", "whi", "wlo", "ah", "al", "mixr", "nxt", "raw_in", "S"))
        res = m.sb("res", [P, KD, TG])
        hh = m.sb("hh", [P, KF, TG], F32R)
        hl = m.sb("hl", [P, KF, TG], F32R)
        hbuf = m.sb("hbuf", [P, TG])
        silu = m.sb("silu", [P, 2, TG])
        nrm = m.sb("nrm", [TOK, 2, D])
        g2b = m.sb("g2b", [TOK, D])
        b2b = m.sb("b2b", [TOK, D])
        gb1 = m.sb("gb1", [P, 2, KD])
        ident = m.sb("l_ident", [P, P])
        stats = m.sb("stats", [TOK, 2, 6])
        mv = m.sb("mv", [TOK, 2])
        rstd = m.sb("rstd", [TOK, 2])
        acc = m.ps("l_acc", [P, BANKS, 512])
        turned = m.ps("turned", [P, 2, 512])
        back = m.ps("back", [P, 2, 512])
        y_out = [m.sem(f"l_y_out{s}") for s in range(2)]
        dve_s = m.sem("l_dve")
        fences = m.sem("l_fences")
        CONSTS = 16 * 5

        def apart(eng):
            eng.sem_inc(fences, 1)

        block = ctx.enter_context(nc.Block())

        @block.sync
        def _(sp):
            def slab8(i, s):
                sp.dma_start(raw[:, s, 0:KD], io["wB"][bass.ds(i, 1)].rearrange("a p k n -> (a p) k n")).then_inc(raw_in[s], 16)

            def slab11(i, s):
                sp.dma_start(raw[:, s], io["w2"][bass.ds(i, 1)].rearrange("a p k n -> (a p) k n")).then_inc(raw_in[s], 16)

            def stream(base, lo, hi, load, off):
                with sp.Fori(lo, hi) as u:
                    for s in range(2):
                        sp.wait_ge(S["lo_done"], base + 2 * u + s - 1)
                        apart(sp)
                        load(2 * u + s + off, s)

            def mixed(g):
                sp.dma_start(mixr[:], io["mixT"][:, :, bass.ds(g * TG, TG)].rearrange("t p n -> p t n")).then_inc(S["mix_in"], 16)

            def tokens(g):
                sp.dma_start(nxt[:], io["xT"][bass.ds(g, 1)].rearrange("a p k n -> (a p) k n")).then_inc(S["x_in"], 16)

            stream(0, 2, 3, slab8, 0)
            sp.wait_ge(ahead["sample_stored"], 7 * 16)
            row = lambda a: bass.AP(tensor=io[a].tensor, offset=0, ap=[[0, TOK], [1, D]])
            for dst, src in ((ident[:], io["c_ident"]), (gb1[:, 0], io["g1"]), (gb1[:, 1], io["b1"]), (g2b[:], row("g2")), (b2b[:], row("b2"))):
                sp.dma_start(dst, src).then_inc(S["const_in"], 16)

            def with_next(g, base, lo, hi, off):
                stream(base, lo, hi - 12, slab8, off)
                sp.wait_ge(S["mix_split"], g + 1)
                apart(sp)
                mixed(g + 1)
                stream(base, hi - 12, hi - 7, slab8, off)
                sp.wait_ge(S["moved"], g + 1)
                apart(sp)
                tokens(g + 1)
                stream(base, hi - 7, hi, slab8, off)

            def heads(g):
                at = g * SLABS + FIRST
                stream(at, 0, HEAD, slab11, 0)
                stream(at + 2 * HEAD, 0, OUT1 // 2, slab8, 0)
                stream(at + OUT1, HEAD, 8, slab11, 0)
                return at + OUT1 + OUT2

            with_next(0, 0, 3, (OUT1 + IN) // 2, 0)
            with sp.Fori(0, NG - 2) as g:
                with_next(g + 1, heads(g), 0, KF, OUT1)
            stream(heads(NG - 2), 0, KF, slab8, OUT1)
            stream((NG - 1) * SLABS + FIRST, 0, 8, slab11, 0)

        @block.gpsimd
        def _(pool):
            def rest(base, lo, hi, k):
                with pool.Fori(lo, hi) as u:
                    for s in range(2):
                        pool.wait_ge(S["hi_done"], base + 2 * u + s + 1)
                        nc.gpsimd.tensor_tensor(wlo[:, s, 0:k], raw[:, s, 0:k], whi[:, s, 0:k].bitcast(F32), ALU.subtract).then_inc(S["lo_done"], 1)

            rest(0, 1, OUT1 // 2, KD)
            rest(0, OUT1 // 2, OUT1 // 2 + 1, KD)
            for i in range(NTT):
                t = slice(i * TOK, i * TOK + TOK)
                pool.wait_ge(S["x1_hi"], i + 1)
                nc.gpsimd.tensor_tensor(al[:, :, t], nxt[:, :, t], ah[:, :, t].bitcast(F32), ALU.subtract).then_inc(S["x1_split"], 1)
            rest(0, OUT1 // 2 + 1, FIRST // 2, KD)
            with pool.Fori(0, NG - 1) as g:
                at = g * SLABS + FIRST
                rest(at, 0, HEAD, HALF)
                rest(at + 2 * HEAD, 0, OUT1 // 2, KD)
                rest(at + OUT1, HEAD, 8, HALF)
                rest(at + OUT1 + OUT2, 0, KF, KD)
            rest((NG - 1) * SLABS + FIRST, 0, 8, HALF)
            pool.wait_ge(S["const_in"], CONSTS)
            for i in range(NTT - 1):
                pool.wait_ge(S["normed"], (NG - 1) * NORMS + NTT + i + 1)
                nc.gpsimd.tensor_tensor(nrm[:, i % 2], nrm[:, i % 2], g2b[:], ALU.mult).then_inc(S["y_scaled"], 1)

        @block.scalar
        def _(act):
            def rounded_slab(n, k, s):
                act.wait_ge(raw_in[s], n * 8 + 16)
                act.wait_ge(S["slab_done"], n + s + 1)
                act.wait_ge(S["mix_hi"], 1)
                nc.scalar.activation(whi[:, s, 0:k], raw[:, s, 0:k], ACT.Copy).then_inc(S["hi_done"], 1)

            def rounded(n, k):
                for s in range(2):
                    rounded_slab(n, k, s)

            def root(n):
                act.wait_ge(S["root_arg"], n + 1)
                act.wait_ge(S["mix_hi"], 1)
                nc.scalar.activation(rstd[:, 0:1], rstd[:, 0:1], ACT.Sqrt).then_inc(S["root_done"], 1)

            def store(g, i):
                act.wait_ge(S["y_ready"], g * NTT + i + 1)
                act.dma_start(io["y"][bass.ds(g * TG + i * TOK, TOK), :], nrm[:, i % 2]).then_inc(y_out[i % 2], 16)

            def gated(g, base, j, s):
                act.wait_ge(S["slab_done"], base + 2 * j + 3)
                act.wait_ge(S["h_split"], g * KF + j + 1)
                act.wait_ge(S["mix_hi"], 1)
                nc.scalar.activation(silu[:, s], acc[:, 2 * s, 0:TG], ACT.Silu).then_inc(S["silu_done"], 1)

            def pair(g, base, j, s, k=KD, between=None):
                rounded_slab(base + 2 * j + 2, k, 0)
                if between is not None:
                    between()
                gated(g, base, j, s)
                rounded_slab(base + 2 * j + 2, k, 1)

            def pairs(g, base, lo, hi, last):
                with act.Fori(lo // 2, hi // 2 - last) as q:
                    for s in range(2):
                        pair(g, base, 2 * q + s, s)
                if last:
                    pair(g, base, hi - 2, 0)
                    pair(g, base, hi - 1, 1, HALF)

            for s in range(2):
                act.sem_inc(y_out[s], 16)
            with act.Fori(1, 5) as u:
                rounded(u * 2, KD)
            def x1_hi(i):
                t = slice(i * TOK, i * TOK + TOK)
                act.wait_ge(S["x1_ready"], i + 1)
                nc.scalar.activation(ah[:, :, t], nxt[:, :, t], ACT.Copy).then_inc(S["x1_hi"], 1)

            for i in range(NTT):
                root(i)
                if i:
                    x1_hi(i - 1)
            x1_hi(NTT - 1)
            pairs(0, OUT1, 0, KF, 1)
            with act.Fori(0, NG - 1) as g:
                at = g * SLABS + FIRST
                norm = g * NORMS + NTT
                rounded(at + 2, HALF)
                rounded(at + 4, KD)
                with act.Fori(1, OUT1 // 2) as u:
                    rounded(at + 4 + 2 * u, KD)
                rounded(at + OUT1 + 2 * HEAD, HALF)
                for t in range(HEAD, 8):
                    rounded(at + OUT1 + 2 * t + 2, HALF if t < 7 else KD)
                    if t < HEAD + NTT:
                        root(norm + t - HEAD)
                for j in range(NTT + 2):
                    def between():
                        if 1 <= j <= NTT:
                            root(norm + NTT + j - 1)
                        if j >= 2:
                            store(g, j - 2)
                    pair(g + 1, at + OUT1 + OUT2, j, j % 2, between=between)
                pairs(g + 1, at + OUT1 + OUT2, NTT + 2, KF, 1)
            at = (NG - 1) * SLABS + FIRST
            with act.Fori(1, 8) as u:
                rounded(at + 2 * u, HALF)
            for i in range(NTT):
                root((NG - 1) * NORMS + NTT + i)
                if i:
                    store(NG - 1, i - 1)
            store(NG - 1, NTT - 1)
            for s in range(2):
                act.wait_ge(y_out[s], 16 + 16 * NG * NTT // 2)

        @block.tensor
        def _(pe):
            def slab(n, s, bank, hx, lx, k0, k, total):
                pe.wait_ge(S["lo_done"], n + 1)
                for c in range(k):
                    a = k0 + c
                    pe.matmul(acc[:, bank, 0:TG], whi[:, s, c], hx[:, a], start=(a == 0), stop=False)
                    pe.matmul(acc[:, bank, 0:TG], whi[:, s, c], lx[:, a], start=False, stop=False)
                    last = pe.matmul(acc[:, bank, 0:TG], wlo[:, s, c], hx[:, a], start=False, stop=(a == total - 1))
                last.then_inc(S["slab_done"], 1)

            def tile(n, m, b):
                pe.wait_ge(S["evac"], m + 1)
                slab(n, b % 2, b, ah, al, 0, KD, KD)

            def tile2(n, m, b, h_done=None):
                pe.wait_ge(S["evac"], m + 1)
                for s in range(2):
                    if h_done is not None:
                        pe.wait_ge(S["h_split"], h_done - (0 if s else KF - HALF))
                    slab(n + s, s, b, hh, hl, s * HALF, HALF, KF)

            def turn(src, i, turned=turned):
                for k in range(KD):
                    last = pe.transpose(turned[0:TOK, k // 4, (k % 4) * P:(k % 4) * P + P],
                                        src[:, k, i * TOK:i * TOK + TOK], ident[:])
                last.then_inc(S["ta_full"], 1)

            def turn_back(g, i, alone=False):
                if not alone:
                    pe.wait_ge(S["x1_split"], g * NTT + i + 1)
                elif i:
                    pe.wait_ge(S["x1_ready"], i)
                for k in range(KD):
                    last = pe.transpose(back[:, k // 4, (k % 4) * TOK:(k % 4) * TOK + TOK],
                                        nrm[:, i % 2, k * P:k * P + P], ident[0:TOK, 0:TOK])
                last.then_inc(S["tb_full"], 1)

            pe.sem_inc(S["slab_done"], 2)
            pe.wait_ge(S["mix_split"], 1)
            with pe.Fori(0, OUT1 // BANKS) as q:
                for b in range(BANKS):
                    tile(q * BANKS + b, q * BANKS + b, b)
            pe.wait_ge(S["evac"], OUT1 + BANKS)
            pe.wait_ge(S["const_in"], CONSTS)
            turn(nxt, 0)
            for i in range(NTT):
                pe.wait_ge(S["normed"], i + 1)
                if i < NTT - 1:
                    turn(nxt, i + 1)
                turn_back(0, i, alone=True)
            pe.wait_ge(S["x1_split"], NTT + 1)
            with pe.Fori(0, IN // BANKS) as q:
                for b in range(BANKS):
                    tile(q * BANKS + b + OUT1, q * BANKS + b + OUT1, b)
            with pe.Fori(0, NG - 1) as g:
                at = g * SLABS + FIRST
                ta = g * TILES + FIRST
                norm = g * NORMS + NTT
                for t in range(HEAD):
                    tile2(at + 2 * t, ta + t, t, None if t else g * KF + KF + 2)
                pe.wait_ge(S["mix_split"], g + 2)
                for t in range(OUT1):
                    tile(at + 2 * HEAD + t, ta + HEAD + t, (HEAD + t) % BANKS)
                for t in range(HEAD, 8):
                    tile2(at + OUT1 + 2 * t, ta + OUT1 + t, t % BANKS)
                    i = t - HEAD
                    if i == 0:
                        pe.wait_ge(S["evac"], ta + HEAD + OUT1 + BANKS)
                    if 1 <= i <= NTT:
                        pe.wait_ge(S["normed"], norm + i)
                    if i < NTT:
                        turn(nxt, i)
                    if 1 <= i <= NTT:
                        turn_back(g + 1, i - 1)
                pe.wait_ge(S["x1_split"], (g + 2) * NTT + 1)
                ai, ti = at + OUT1 + OUT2, ta + OUT1 + 8
                for j in range(NTT):
                    for b in range(2):
                        tile(ai + 2 * j + b, ti + 2 * j + b, (2 * j + b) % BANKS)
                    if j == 0:
                        pe.wait_ge(S["evac"], ti + BANKS)
                    pe.wait_ge(S["normed"], norm + NTT + j)
                    turn(res, j)
                apart(pe)
                with pe.Fori(NTT // 2, KF // 2) as q:
                    for b in range(BANKS):
                        tile(ai + q * BANKS + b, ti + q * BANKS + b, b)
            at, ta = (NG - 1) * SLABS + FIRST, (NG - 1) * TILES + FIRST
            pe.wait_ge(S["h_split"], NG * KF + 2)
            with pe.Fori(0, 2) as q:
                for b in range(BANKS):
                    tile2(at + 8 * q + 2 * b, ta + BANKS * q + b, b)
            pe.wait_ge(S["evac"], ta + 8 + BANKS)
            for i in range(NTT):
                if i >= 2:
                    pe.wait_ge(S["normed"], (NG - 1) * NORMS + NTT + i - 1)
                turn(res, i, (turned, acc[:, 0:2])[i % 2])

        @block.vector
        def _(dve):
            dve.sem_inc(S["evac"], BANKS)
            dve.sem_inc(S["x1_split"], 1)
            dve.sem_inc(S["h_split"], 2)

            def split_mix(turn):
                nc.vector.tensor_copy(ah[:], mixr[:]).then_inc(S["mix_hi"], 1)
                dve.wait_ge(S["mix_hi"], turn + 1)
                nc.vector.tensor_tensor(al[:], mixr[:], ah[:].bitcast(F32), ALU.subtract).then_inc(S["mix_split"], 1)

            def add(dst, t, bank, slab):
                dve.wait_ge(S["slab_done"], slab + 3)
                nc.vector.scalar_tensor_tensor(dst[:, t], dst[:, t], ALPHA, acc[:, bank, 0:TG], ALU.mult, ALU.add).then_inc(S["evac"], 1)

            def normed(v, n, g, i, second, turned=turned):
                dve.wait_ge(S["ta_full"], n + 1)
                for b in range(2):
                    last = nc.vector.bn_stats(stats[:, b], turned[0:TOK, b])
                v(last)
                apart(dve)
                v(nc.vector.bn_aggr(mv[:], stats[:].rearrange("p a b -> p (a b)")))
                nc.vector.tensor_scalar(rstd[:, 0:1], mv[:, 1:2], LN_EPS, None, ALU.add).then_inc(S["root_arg"], 1)
                dve.wait_ge(S["root_done"], n + 1)
                v(nc.vector.reciprocal(rstd[:, 1:2], rstd[:, 0:1]))
                dve.wait_ge(y_out[i % 2], 16 * (2 * g + (i // 2 if second else 0) + 1))
                nc.vector.tensor_scalar(nrm[:, i % 2], turned[0:TOK].rearrange("p b n -> p (b n)"), mv[:, 0:1], rstd[:, 1:2],
                                        ALU.subtract, ALU.mult).then_inc(S["normed"], 1)

            def split(v, g, i, alone=False):
                t = slice(i * TOK, i * TOK + TOK)
                dve.wait_ge(S["tb_full"], g * NTT + i + 1)
                for b in range(2):
                    last = nc.vector.tensor_tensor(
                        nxt[:, 4 * b:4 * b + 4, t], back[:, b, 0:4 * TOK].rearrange("p (k t) -> p k t", t=TOK),
                        gb1[:, 0, 4 * b:4 * b + 4].unsqueeze(2).broadcast_to([P, 4, TOK]), ALU.mult)
                v(last)
                add_bias = nc.vector.tensor_tensor(nxt[:, :, t], nxt[:, :, t], gb1[:, 1].unsqueeze(2).broadcast_to([P, KD, TOK]), ALU.add)
                if alone:
                    add_bias.then_inc(S["x1_ready"], 1)
                    return
                v(add_bias)
                v(nc.vector.tensor_copy(ah[:, :, t], nxt[:, :, t]))
                nc.vector.tensor_tensor(al[:, :, t], nxt[:, :, t], ah[:, :, t].bitcast(F32), ALU.subtract).then_inc(S["x1_split"], 1)

            def output(v, n, i):
                dve.wait_ge(S["normed"], n + 1)
                v(nc.vector.tensor_tensor(nrm[:, i % 2], nrm[:, i % 2], g2b[:], ALU.mult))
                nc.vector.tensor_tensor(nrm[:, i % 2], nrm[:, i % 2], b2b[:], ALU.add).then_inc(S["y_ready"], 1)

            def gated(g, base, tiles, j, s):
                dve.wait_ge(S["silu_done"], g * KF + j + 1)
                dve.wait_ge(S["slab_done"], base + 2 * j + 4)
                dve.wait_ge(S["h_split"], g * KF + j + 2)
                nc.vector.tensor_tensor(hbuf[:], silu[:, s], acc[:, 2 * s + 1, 0:TG], ALU.mult).then_inc(S["evac"], 2)
                dve.wait_ge(S["evac"], tiles + 2 * j + 2 + BANKS)
                at = bass.ds(j, 1)
                nc.vector.tensor_copy(hh[:, at], hbuf[:].unsqueeze(1)).then_inc(S["h_hi"], 1)
                dve.wait_ge(S["h_hi"], g * KF + j + 1)
                nc.vector.tensor_tensor(hl[:, at], hbuf[:].unsqueeze(1), hh[:, at].bitcast(F32), ALU.subtract).then_inc(S["h_split"], 1)

            dve.wait_ge(S["x_in"], 16)
            for t in range(OUT1):
                add(nxt, t, t % BANKS, t)
            dve.wait_ge(S["const_in"], CONSTS)
            v = Steps(dve, dve_s)
            for i in range(NTT):
                normed(v, i, 0, i, False)
                if i:
                    split(v, 0, i - 1, alone=True)
            split(v, 0, NTT - 1, alone=True)
            dve.wait_ge(S["x1_split"], NTT + 1)
            nc.vector.tensor_copy(res[:], nxt[:]).then_inc(S["moved"], 1)
            with dve.Fori(0, KF // 2) as q:
                for s in range(2):
                    gated(0, OUT1, OUT1, 2 * q + s, s)
            before = v.k
            with dve.Fori(0, NG - 1) as g:
                at = g * SLABS + FIRST
                ta = g * TILES + FIRST
                norm = g * NORMS + NTT
                v = Steps(dve, dve_s, g, 3 * NORMS + 4 * NTT)
                v.k = before
                dve.wait_ge(S["mix_in"], g * 16 + 32)
                dve.wait_ge(S["slab_done"], at + 2)
                split_mix(g + 1)
                for t in range(HEAD):
                    add(res, t, t, at + 2 * t + 1)
                dve.wait_ge(S["x_in"], g * 16 + 32)
                for t in range(OUT1):
                    add(nxt, t, (HEAD + t) % BANKS, at + 2 * HEAD + t)
                for t in range(HEAD, 8):
                    add(res, t, t % BANKS, at + OUT1 + 2 * t + 1)
                    i = t - HEAD
                    if 1 <= i <= NTT:
                        split(v, g + 1, i - 1)
                    if i < NTT:
                        normed(v, norm + i, g, i, False)
                ai, ti = at + OUT1 + OUT2, ta + OUT1 + 8
                for j in range(NTT):
                    gated(g + 1, ai, ti, j, j % 2)
                    normed(v, norm + NTT + j, g, j, True)
                    output(v, norm + NTT + j, j)
                dve.wait_ge(S["x1_split"], (g + 2) * NTT + 1)
                nc.vector.tensor_copy(res[:], nxt[:]).then_inc(S["moved"], 1)
                with dve.Fori(NTT // 2, KF // 2) as q:
                    for s in range(2):
                        gated(g + 1, ai, ti, 2 * q + s, s)
                assert v.k == before + v.each
            at = (NG - 1) * SLABS + FIRST
            for t in range(8):
                add(res, t, t % BANKS, at + 2 * t + 1)
            v = Steps(dve, dve_s, NG - 1, v.each)
            v.k = before
            for i in range(NTT):
                normed(v, (NG - 1) * NORMS + NTT + i, NG - 1, i, True, (turned, acc[:, 0:2])[i % 2])
                if i:
                    dve.wait_ge(S["y_scaled"], i)
                    nc.vector.tensor_tensor(nrm[:, (i - 1) % 2], nrm[:, (i - 1) % 2], b2b[:], ALU.add).then_inc(S["y_ready"], 1)
            output(v, NG * NORMS - 1, NTT - 1)


def bass_hymba_step(nc, io):
    io["projT"] = nc.dram_tensor("projT", [NPROJ, P, NT], F32, kind="Internal").ap()
    io["gateT"] = nc.dram_tensor("gateT", [8, NT], F32, kind="Internal").ap()
    io["xsT"] = nc.dram_tensor("xsT", [H, 2, NT], F32, kind="Internal").ap()
    io["ext"] = nc.dram_tensor("ext", [8, HJ], F32, kind="Internal").ap()
    io["mixT"] = nc.dram_tensor("mixT", [8, P, NT], F32, kind="Internal").ap()
    kept = ExitStack()
    gate_in = gate_inputs(Store(nc, kept))
    proj_out = project(nc, io, gate_in)
    ahead = layer_inputs(Store(nc, kept))
    with ExitStack() as ctx:
        m = Store(nc, ctx)
        keep = {
            "ident": m.sb("ident", [P, P]),
            "cols": m.sb("cols", [P, NC + 1, 64]),
            "bias": m.sb("bias", [P, 8, 2 * W]),
            "bias_prev": m.sb("bias_prev", [P, 8, W]),
            "sbias": m.sb("sbias", [P, 2, P + NS]),
            "ident_in": m.sem("ident_in"),
        }
        taken = sample_inputs(m)
        outs = prompt_outputs(m)
        with ExitStack() as inputs:
            first = prompt_inputs(Store(nc, inputs))
            gates(nc, io, keep, gate_in, first, proj_out)
            prompt(nc, io, keep, first, taken, outs)
        sample(nc, io, keep, taken, outs, ahead)
    layer(nc, io, ahead)
    kept.close()


def constants():
    eye = np.eye(P, dtype=np.float32)
    dist = 255 - np.arange(HJ)
    n = np.maximum(dist, 1).astype(np.float32)
    large = 16 + (np.log(n / np.float32(16)) / np.float32(np.log(8.0)) * np.float32(16)).astype(np.int32)
    bucket = np.where(dist < 16, np.maximum(dist, 0), np.minimum(large, 31))
    seen = (dist >= 0) & (dist < W)
    onehot = ((np.arange(32)[:, None] == bucket) & seen).astype(np.float32)
    row = np.arange(P)
    seq = np.arange(NS) // DT
    smask = np.stack([np.where(half * 4 + row[:, None] // 32 == seq, 0.0, NEG) for half in range(2)], 1)
    s, t = np.arange(C)[:, None], np.arange(C)
    ds, dt = np.arange(NS)[:, None], np.arange(NS)
    return {
        "c_ident": eye, "c_anti": eye[::-1], "c_onehot": onehot,
        "c_outside": np.tile(np.where(seen, 0.0, NEG), (8, 1)),
        "c_repl": (np.arange(32)[:, None] == row % 32).astype(np.float32),
        "c_smask": smask,
        "c_causal": np.where(s <= t, 0.0, NEG),
        "c_causal_s": np.where((ds <= dt) & (ds // DT == dt // DT), 0.0, NEG),
    }


def w_in_order():
    base = 2056
    sq = [base + (g * J + j) * 64 + d for j in range(J) for g in range(2) for d in range(64)]
    return np.array([*range(2048), *sq, *range(base + 512, base + 768)]), np.arange(2048, 2056)


def layout(a):
    f = lambda k: np.asarray(a[k], np.float32)
    cols, gates = w_in_order()
    slabs = lambda w, k: np.ascontiguousarray(w.reshape(k, P, w.shape[1] // P, P).transpose(2, 1, 0, 3))
    x = np.concatenate([f("x_prompt").reshape(SEQ, D), f("x_sample").reshape(NS, D)])
    w = f("w_in")[0]
    out = {
        "xT": np.ascontiguousarray(x.reshape(NG, TG, KD, P).transpose(0, 3, 2, 1)),
        "wA": slabs(w[:, cols], KD),
        "wG": np.ascontiguousarray(w[:, gates].reshape(KD, P, 8).transpose(1, 0, 2)),
    }
    swa = [512 + (g * J + j) * 64 + d for j in range(J) for g in range(2) for d in range(64)]
    w1 = slabs(f("w_ffn_in")[0], KD)
    out.update({
        "wB": np.concatenate([slabs(f("w_out")[0][[*range(512), *swa]], KD), w1.reshape(2, KF, P, KD, P).swapaxes(0, 1).reshape(2 * KF, P, KD, P)]),
        "w2": f("w_ffn_out")[0].reshape(2, HALF, P, KD, P).transpose(3, 0, 2, 1, 4).reshape(2 * KD, P, HALF, P),
        "g1": f("ln1_g").reshape(KD, P).T, "b1": f("ln1_b").reshape(KD, P).T, "g2": f("ln2_g"), "b2": f("ln2_b"),
    })
    out.update({
        "b_ig": f("b_igate").reshape(H, 1), "b_fg": f("b_fgate").reshape(H, 1),
        "m0": f("state_mlstm_m")[0].T, "rel_bias": f("rel_bias"),
    })
    heads = [g * J + j for j in range(J) for g in range(2)]
    sinks = f("swa_sinks")[0]
    out.update({
        "sinks": sinks[heads].reshape(1, 8),
        "sink_col": np.broadcast_to(sinks.reshape(1, 2, 1, J), (4, 2, DT, J)).reshape(P, 1),
        "g_ml": f("ml_norm_g").reshape(H, P).T,
        "state_C": f("state_mlstm_C")[0].reshape(DB * H, P, P).transpose(1, 0, 2),
        "n0": f("state_mlstm_n")[0].reshape(DB * H, P).T,
        "cache_kT": f("cache_swa_k")[0].reshape(DB, W, P).transpose(2, 0, 1),
        "cache_k": f("cache_swa_k")[0].reshape(DB, W, P),
        "cache_v": f("cache_swa_v")[0].reshape(DB, W, P),
    })
    out.update(constants())
    return {k: np.ascontiguousarray(v, dtype=np.float32) for k, v in out.items()}


OUTS = {
    "y": [NT, D],
    "p_C": [P, H, P], "p_n": [P, H], "p_m": [H, 1], "p_k": [P, W], "p_v": [P, W],
    "s_C": [P, DB * H, P], "s_n": [P, DB * H], "s_m": [H, DB], "s_k": [DB, W, P], "s_v": [DB, W, P],
}


def kernel(**inputs):
    import concourse.bacc as bacc
    from concourse.bass_utils import run_bass_kernel_spmd

    nc = bacc.Bacc("TRN2", target_bir_lowering=False, num_devices=1)
    arrays = layout(inputs)
    io = {n: nc.dram_tensor("in_" + n, a.shape, F32, kind="ExternalInput").ap() for n, a in arrays.items()}
    io.update({n: nc.dram_tensor("out_" + n, s, F32, kind="ExternalOutput").ap() for n, s in OUTS.items()})
    bass_hymba_step(nc, io)
    r = run_bass_kernel_spmd(nc, [{"in_" + n: a for n, a in arrays.items()}], core_ids=[0]).results[0]
    o = {n: r["out_" + n] for n in OUTS}
    one = lambda x: np.ascontiguousarray(x)[None]
    feature = lambda x: x.T.reshape(1, W, 2, 64)
    return (
        one(o["y"][0:SEQ]), np.ascontiguousarray(o["y"][SEQ:NT]).reshape(DB, DT, D),
        one(o["p_C"].transpose(1, 0, 2)[None]), one(o["p_n"].T[None]), one(o["p_m"].T), one(feature(o["p_k"])), one(feature(o["p_v"])),
        one(o["s_C"].transpose(1, 0, 2).reshape(DB, H, P, P)), one(o["s_n"].T.reshape(DB, H, P)), one(o["s_m"].T),
        one(o["s_k"].reshape(DB, W, 2, 64)), one(o["s_v"].reshape(DB, W, 2, 64)),
    )
```
